# Optimizing a Trainium2 kernel written in Bass

```python
import math
import jax, jax.numpy as jnp
from jax import lax
import numpy as np

D_MODEL = 1024
BATCH = 1
SEQ = 512
DEPTH = 2

GRID_W = 64
CTX_LEN = 256
EPS = 1e-6
ROPE_THETA = 10000.0
Q_BLOCK = 128

MIX_HALF = D_MODEL // 2
HEAD_DIM = 64
GQA_Q_HEADS = MIX_HALF // HEAD_DIM
GQA_KV_HEADS = GQA_Q_HEADS // 4
GQA_IN = (GQA_Q_HEADS + 2 * GQA_KV_HEADS) * HEAD_DIM

HG_DK = 128
HG_DV = 128
HG_HEADS = MIX_HALF // HG_DV
HG_W = HG_HEADS * HG_DK
HG_IN = 5 * HG_W
GLA_CHUNK = 64

MLA_HEADS = MIX_HALF // HEAD_DIM
MLA_NOPE = 64
MLA_ROPE = 32
MLA_V = 64
MLA_Q_RANK = 384
MLA_KV_RANK = 256
MLA_IN = MLA_Q_RANK + MLA_KV_RANK + MLA_ROPE

S5_WIDTH = MIX_HALF
S5_GROUP = 16
S5_GROUPS = S5_WIDTH // S5_GROUP
S5_STATE = 64

EVEN_IN = GQA_IN + HG_IN
ODD_IN = MLA_IN + S5_WIDTH
MIX_OUT = 2 * MIX_HALF

PEER_HEADS = 8
PEER_KEYS = 128
N_EXPERTS = PEER_KEYS * PEER_KEYS
PEER_TOPK = 16
PEER_QDIM = 256
PEER_HALF = PEER_QDIM // 2
PEER_BLOCK = 128

N_EVEN = (DEPTH + 1) // 2
N_ODD = DEPTH // 2

kernel_name = 'hybrid_gqa_hgrn2_mla_s5_peer_dit'

def _rms_norm(x, g):
    xf = x.astype(jnp.float32)
    y = xf * lax.rsqrt(jnp.mean(xf * xf, axis=-1, keepdims=True) + EPS)
    return (y * g.astype(jnp.float32)).astype(x.dtype)

def _modulate(h, shift, scale):
    return h * (1.0 + scale) + shift

def _axial_angles(rows, rot_dim):
    axis_dim = rot_dim // 2
    inv = ROPE_THETA ** (-jnp.arange(0, axis_dim, 2, dtype=jnp.float32) / axis_dim)
    t = jnp.arange(rows * GRID_W)
    r = (t // GRID_W).astype(jnp.float32)
    col = (t % GRID_W).astype(jnp.float32)
    return r[:, None] * inv, col[:, None] * inv

def _rope_1d(x, ang):
    cos = jnp.cos(ang)[:, None, :]
    sin = jnp.sin(ang)[:, None, :]
    x1, x2 = jnp.split(x.astype(jnp.float32), 2, axis=-1)
    return jnp.concatenate([x1 * cos - x2 * sin, x1 * sin + x2 * cos], axis=-1).astype(x.dtype)

def _rope_2d(x, angs):
    xr, xc = jnp.split(x, 2, axis=-1)
    return jnp.concatenate([_rope_1d(xr, angs[0]), _rope_1d(xc, angs[1])], axis=-1)

def _attend(q, k, v):
    b, hk, g, t, dq = q.shape
    nb = t // Q_BLOCK
    qb = jnp.moveaxis(q.reshape(b, hk, g, nb, Q_BLOCK, dq), 3, 0)
    scale = dq ** -0.5

    def block(qi):
        s = jnp.einsum('bhgqd,bhkd->bhgqk', qi, k).astype(jnp.float32) * scale
        p = jax.nn.softmax(s, axis=-1).astype(v.dtype)
        return jnp.einsum('bhgqk,bhkd->bhgqd', p, v)

    o = lax.map(block, qb)
    return jnp.moveaxis(o, 0, 3).reshape(b, hk, g, t, v.shape[-1])

def _merge_heads(o):
    return o.transpose(0, 3, 1, 2, 4).reshape(o.shape[0], o.shape[3], -1)

def _gqa(pa, pc, qn_g, kn_g, angs, need_ctx):
    nq = GQA_Q_HEADS * HEAD_DIM
    nk = GQA_KV_HEADS * HEAD_DIM
    grp = GQA_Q_HEADS // GQA_KV_HEADS

    def parts(p):
        b_, t_ = p.shape[0], p.shape[1]
        q = _rms_norm(p[..., :nq].reshape(b_, t_, GQA_Q_HEADS, HEAD_DIM), qn_g)
        k = _rms_norm(p[..., nq:nq + nk].reshape(b_, t_, GQA_KV_HEADS, HEAD_DIM), kn_g)
        v = p[..., nq + nk:].reshape(b_, t_, GQA_KV_HEADS, HEAD_DIM)
        return q, k, v

    def qh(a):
        return a.reshape(a.shape[0], a.shape[1], GQA_KV_HEADS, grp, HEAD_DIM).transpose(0, 2, 3, 1, 4)

    def kh(a):
        return a.transpose(0, 2, 1, 3)

    q, k, v = parts(pa)
    qc, kc, vc = parts(pc)
    q = _rope_2d(q, angs)
    k = _rope_2d(k, angs)
    k_all = jnp.concatenate([kh(kc), kh(k)], axis=2)
    v_all = jnp.concatenate([kh(vc), kh(v)], axis=2)
    y = _merge_heads(_attend(qh(q), k_all, v_all))
    yc = _merge_heads(_attend(qh(qc), kh(kc), kh(vc))) if need_ctx else None
    return y, yc

def _gla_scan(q, k, v, logf, s0):
    q, k, v, logf = (a.astype(jnp.float32) for a in (q, k, v, logf))
    b, h, t, dk = q.shape
    n = t // GLA_CHUNK

    def chunks(a):
        return jnp.moveaxis(a.reshape(b, h, n, GLA_CHUNK, a.shape[-1]), 2, 0)

    lower = jnp.tril(jnp.ones((GLA_CHUNK, GLA_CHUNK), dtype=bool))[:, :, None]

    def step(state, blk):
        qc, kc, vc, lc = blk
        cum = jnp.cumsum(lc, axis=2)
        rel = cum[:, :, :, None, :] - cum[:, :, None, :, :]
        dec = jnp.exp(jnp.where(lower, rel, -jnp.inf))
        att = jnp.einsum('bhtc,bhtsc,bhsc->bhts', qc, dec, kc)
        out = (jnp.einsum('bhts,bhsv->bhtv', att, vc)
               + jnp.einsum('bhtc,bhcv->bhtv', qc * jnp.exp(cum), state))
        last = cum[:, :, -1:, :]
        state = (jnp.exp(last[:, :, 0, :, None]) * state
                 + jnp.einsum('bhsc,bhsv->bhcv', kc * jnp.exp(last - cum), vc))
        return state, out

    s_final, o = lax.scan(step, s0, (chunks(q), chunks(k), chunks(v), chunks(logf)))
    return jnp.moveaxis(o, 0, 2).reshape(b, h, t, v.shape[-1]), s_final

def _hgrn2(pa, pc, lb, onorm_g, need_ctx):
    def heads(a):
        return a.reshape(a.shape[0], a.shape[1], HG_HEADS, -1).transpose(0, 2, 1, 3)

    def parts(p):
        q = heads(p[..., :HG_W])
        fs = (heads(p[..., HG_W:2 * HG_W]), heads(p[..., 2 * HG_W:3 * HG_W]))
        i = heads(p[..., 3 * HG_W:4 * HG_W])
        g = p[..., 4 * HG_W:]
        return q, fs, i, g

    def gate(fraw, lbd):
        lbd = lbd[None, :, None, :]
        f = lbd + (1.0 - lbd) * jax.nn.sigmoid(fraw.astype(jnp.float32))
        return 1.0 - f, jnp.log(f)

    q, fs, i, g = parts(pa)
    qc, fcs, ic, gc = parts(pc)
    s_zero = jnp.zeros((pa.shape[0], HG_HEADS, HG_DK, HG_DV), jnp.float32)
    o = 0.0
    oc = 0.0
    for d in range(2):
        fl = (lambda a: jnp.flip(a, axis=2)) if d == 1 else (lambda a: a)
        kc_, lc_ = gate(fcs[d], lb[d])
        k_, l_ = gate(fs[d], lb[d])
        o_ctx, s_ctx = _gla_scan(fl(qc), fl(kc_), fl(ic), fl(lc_), s_zero)
        o_lat, _ = _gla_scan(fl(q), fl(k_), fl(i), fl(l_), s_ctx)
        o = o + fl(o_lat)
        if need_ctx:
            oc = oc + fl(o_ctx)

    def readout(o_, g_):
        o_ = _rms_norm(o_, onorm_g).transpose(0, 2, 1, 3)
        return o_.reshape(o_.shape[0], o_.shape[1], -1) * jax.nn.silu(g_)

    return readout(o, g), (readout(oc, gc) if need_ctx else None)

def _mla(pa, pc, qa_g, w_qup, kva_g, w_kvup, angs, need_ctx):
    r0 = MLA_Q_RANK
    r1 = MLA_Q_RANK + MLA_KV_RANK

    def parts(p, rotate):
        b_, t_ = p.shape[0], p.shape[1]
        q = (_rms_norm(p[..., :r0], qa_g) @ w_qup).reshape(b_, t_, MLA_HEADS, MLA_NOPE + MLA_ROPE)
        kv = (_rms_norm(p[..., r0:r1], kva_g) @ w_kvup).reshape(b_, t_, MLA_HEADS, MLA_NOPE + MLA_V)
        q_nope, q_rope = q[..., :MLA_NOPE], q[..., MLA_NOPE:]
        k_rope = p[..., r1:][:, :, None, :]
        if rotate:
            q_rope = _rope_2d(q_rope, angs)
            k_rope = _rope_2d(k_rope, angs)
        q = jnp.concatenate([q_nope, q_rope], axis=-1)
        k = jnp.concatenate([kv[..., :MLA_NOPE],
                             jnp.broadcast_to(k_rope, (b_, t_, MLA_HEADS, MLA_ROPE))], axis=-1)
        v = kv[..., MLA_NOPE:]
        return q.transpose(0, 2, 1, 3)[:, :, None], k.transpose(0, 2, 1, 3), v.transpose(0, 2, 1, 3)

    q, k, v = parts(pa, True)
    qc, kc, vc = parts(pc, False)
    k_all = jnp.concatenate([kc, k], axis=2)
    v_all = jnp.concatenate([vc, v], axis=2)
    y = _merge_heads(_attend(q, k_all, v_all))
    yc = _merge_heads(_attend(qc, kc, vc)) if need_ctx else None
    return y, yc

def _diag_scan(abar, bu, h0):
    bu = jnp.moveaxis(bu, 1, 0)
    if h0 is not None:
        bu = bu.at[0].add(abar * h0)
    a = jnp.broadcast_to(abar, (bu.shape[0], 1) + abar.shape)

    def combine(l, r):
        return l[0] * r[0], r[0] * l[1] + r[1]

    _, h = lax.associative_scan(combine, (a, bu))
    return jnp.moveaxis(h, 0, 1)

def _s5(ua, uc, a_re, a_im, log_dt, b_re, b_im, c_re, c_im, d_skip, w_glu, b_glu, need_ctx):
    f32 = jnp.float32

    def grp(u):
        return u.astype(f32).reshape(u.shape[0], u.shape[1], S5_GROUPS, S5_GROUP)

    u = grp(ua)
    ucg = grp(uc)
    dsk = d_skip.astype(f32).reshape(S5_GROUPS, S5_GROUP)
    y = dsk * u
    yc = dsk * ucg if need_ctx else None
    for d in range(2):
        fl = (lambda a: jnp.flip(a, axis=1)) if d == 1 else (lambda a: a)
        lam = lax.complex(a_re[d].astype(f32), a_im[d].astype(f32))
        dt = jnp.exp(log_dt[d].astype(f32))[:, None]
        abar = jnp.exp(lam * dt)
        bbar = ((abar - 1.0) / lam)[..., None] * lax.complex(b_re[d].astype(f32), b_im[d].astype(f32))
        cmat = lax.complex(c_re[d].astype(f32), c_im[d].astype(f32))
        h_ctx = _diag_scan(abar, jnp.einsum('btgc,gpc->btgp', fl(ucg), bbar), None)
        h_lat = _diag_scan(abar, jnp.einsum('btgc,gpc->btgp', fl(u), bbar), h_ctx[:, -1])
        y = y + fl(jnp.einsum('gcp,btgp->btgc', cmat, h_lat).real)
        if need_ctx:
            yc = yc + fl(jnp.einsum('gcp,btgp->btgc', cmat, h_ctx).real)

    def glu(y_):
        z = jax.nn.gelu(y_.reshape(y_.shape[0], y_.shape[1], S5_WIDTH), approximate=False)
        return z * jax.nn.sigmoid(z @ w_glu + b_glu)

    return glu(y), (glu(yc) if need_ctx else None)

def _peer(h, wq, keys, u_tab, v_tab):
    shp = h.shape
    blocks = h.reshape(-1, PEER_BLOCK, shp[-1])

    def block(hb):
        n = hb.shape[0]
        q = (hb @ wq).reshape(n, PEER_HEADS, 2, PEER_HALF)
        s = jnp.einsum('thpk,hpnk->thpn', q, keys).astype(jnp.float32)
        s1, i1 = lax.top_k(s[:, :, 0], PEER_TOPK)
        s2, i2 = lax.top_k(s[:, :, 1], PEER_TOPK)
        cand = (s1[..., :, None] + s2[..., None, :]).reshape(n, PEER_HEADS, PEER_TOPK * PEER_TOPK)
        cidx = (i1[..., :, None] * PEER_KEYS + i2[..., None, :]).reshape(n, PEER_HEADS, PEER_TOPK * PEER_TOPK)
        sc, pos = lax.top_k(cand, PEER_TOPK)
        eidx = jnp.take_along_axis(cidx, pos, axis=-1)
        gw = jax.nn.softmax(sc, axis=-1)
        a = jnp.einsum('thkd,td->thk', u_tab[eidx], hb)
        w = (jax.nn.gelu(a.astype(jnp.float32), approximate=False) * gw).astype(hb.dtype)
        return jnp.einsum('thk,thkd->td', w, v_tab[eidx])

    return lax.map(block, blocks).reshape(shp)

def setup_inputs(seed: int = 0) -> dict:
    key = jax.random.key(seed)
    ks = iter(jax.random.split(key, 48))
    f32 = jnp.float32

    def nrm(shape, scale):
        return jax.random.normal(next(ks), shape, f32) * scale

    def gain(shape):
        return 1.0 + 0.02 * jax.random.normal(next(ks), shape, f32)

    d = D_MODEL
    a_im = (jnp.pi * jnp.arange(S5_STATE, dtype=f32)
            + 0.01 * jax.random.normal(next(ks), (N_ODD, 2, S5_GROUPS, S5_STATE), f32))
    return {
        'x': nrm((BATCH, SEQ, d), 1.0),
        'c': nrm((BATCH, d), 1.0),
        'ctx': nrm((BATCH, CTX_LEN, d), 1.0),
        'c_ctx': nrm((d,), 1.0),
        'ada_w': nrm((DEPTH, d, 6 * d), d ** -0.5),
        'ada_b': nrm((DEPTH, 6 * d), 0.02),
        'norm1_g': gain((DEPTH, d)),
        'norm2_g': gain((DEPTH, d)),
        'ev_w_in': nrm((N_EVEN, d, EVEN_IN), d ** -0.5),
        'ev_w_out': nrm((N_EVEN, MIX_OUT, d), MIX_OUT ** -0.5),
        'gqa_qn_g': gain((N_EVEN, HEAD_DIM)),
        'gqa_kn_g': gain((N_EVEN, HEAD_DIM)),
        'hg_lb_logits': nrm((2, N_EVEN + 1, HG_W), 0.5),
        'hg_onorm_g': gain((N_EVEN, HG_DV)),
        'od_w_in': nrm((N_ODD, d, ODD_IN), d ** -0.5),
        'od_w_out': nrm((N_ODD, MIX_OUT, d), MIX_OUT ** -0.5),
        'mla_qa_g': gain((N_ODD, MLA_Q_RANK)),
        'mla_w_qup': nrm((N_ODD, MLA_Q_RANK, MLA_HEADS * (MLA_NOPE + MLA_ROPE)), MLA_Q_RANK ** -0.5),
        'mla_kva_g': gain((N_ODD, MLA_KV_RANK)),
        'mla_w_kvup': nrm((N_ODD, MLA_KV_RANK, MLA_HEADS * (MLA_NOPE + MLA_V)), MLA_KV_RANK ** -0.5),
        's5_a_re': -0.5 + nrm((N_ODD, 2, S5_GROUPS, S5_STATE), 0.01),
        's5_a_im': a_im,
        's5_log_dt': jax.random.uniform(next(ks), (N_ODD, 2, S5_GROUPS), f32,
                                        minval=math.log(1e-3), maxval=math.log(1e-1)),
        's5_b_re': nrm((N_ODD, 2, S5_GROUPS, S5_STATE, S5_GROUP), (2 * S5_GROUP) ** -0.5),
        's5_b_im': nrm((N_ODD, 2, S5_GROUPS, S5_STATE, S5_GROUP), (2 * S5_GROUP) ** -0.5),
        's5_c_re': nrm((N_ODD, 2, S5_GROUPS, S5_GROUP, S5_STATE), S5_STATE ** -0.5),
        's5_c_im': nrm((N_ODD, 2, S5_GROUPS, S5_GROUP, S5_STATE), S5_STATE ** -0.5),
        's5_d': nrm((N_ODD, S5_WIDTH), 1.0),
        's5_w_glu': nrm((N_ODD, S5_WIDTH, S5_WIDTH), S5_WIDTH ** -0.5),
        's5_b_glu': nrm((N_ODD, S5_WIDTH), 0.02),
        'peer_wq': nrm((DEPTH, d, PEER_HEADS * PEER_QDIM), d ** -0.5),
        'peer_keys': nrm((DEPTH, PEER_HEADS, 2, PEER_KEYS, PEER_HALF), PEER_HALF ** -0.5),
        'peer_u': nrm((DEPTH, N_EXPERTS, d), d ** -0.5),
        'peer_v': nrm((DEPTH, N_EXPERTS, d), PEER_HEADS ** -0.5),
        'final_g': gain((d,)),
    }

def reference(x, c, ctx, c_ctx, ada_w, ada_b, norm1_g, norm2_g, ev_w_in, ev_w_out, gqa_qn_g, gqa_kn_g,
              hg_lb_logits, hg_onorm_g, od_w_in, od_w_out, mla_qa_g, mla_w_qup, mla_kva_g, mla_w_kvup,
              s5_a_re, s5_a_im, s5_log_dt, s5_b_re, s5_b_im, s5_c_re, s5_c_im, s5_d, s5_w_glu, s5_b_glu,
              peer_wq, peer_keys, peer_u, peer_v, final_g):
    rows = x.shape[1] // GRID_W
    angs_gqa = _axial_angles(rows, HEAD_DIM)
    angs_mla = _axial_angles(rows, MLA_ROPE)
    lb_all = jnp.cumsum(jax.nn.softmax(hg_lb_logits.astype(jnp.float32), axis=1), axis=1)
    s_c = jax.nn.silu(c)
    s_ctx = jax.nn.silu(c_ctx)
    xc = ctx
    for layer in range(DEPTH):
        need_ctx = layer < DEPTH - 1
        j = layer // 2
        mod = jnp.split((s_c @ ada_w[layer] + ada_b[layer])[:, None, :], 6, axis=-1)
        modc = jnp.split(s_ctx @ ada_w[layer] + ada_b[layer], 6, axis=-1)
        h = _modulate(_rms_norm(x, norm1_g[layer]), mod[0], mod[1])
        hc = _modulate(_rms_norm(xc, norm1_g[layer]), modc[0], modc[1])
        if layer % 2 == 0:
            pa = h @ ev_w_in[j]
            pc = hc @ ev_w_in[j]
            ya, yac = _gqa(pa[..., :GQA_IN], pc[..., :GQA_IN], gqa_qn_g[j], gqa_kn_g[j], angs_gqa, need_ctx)
            yb, ybc = _hgrn2(pa[..., GQA_IN:], pc[..., GQA_IN:],
                             lb_all[:, j].reshape(2, HG_HEADS, HG_DK), hg_onorm_g[j], need_ctx)
            w_out = ev_w_out[j]
        else:
            pa = h @ od_w_in[j]
            pc = hc @ od_w_in[j]
            ya, yac = _mla(pa[..., :MLA_IN], pc[..., :MLA_IN], mla_qa_g[j], mla_w_qup[j],
                           mla_kva_g[j], mla_w_kvup[j], angs_mla, need_ctx)
            yb, ybc = _s5(pa[..., MLA_IN:], pc[..., MLA_IN:], s5_a_re[j], s5_a_im[j], s5_log_dt[j],
                          s5_b_re[j], s5_b_im[j], s5_c_re[j], s5_c_im[j], s5_d[j], s5_w_glu[j],
                          s5_b_glu[j], need_ctx)
            w_out = od_w_out[j]
        x = x + mod[2] * (jnp.concatenate([ya, yb], axis=-1) @ w_out)
        if need_ctx:
            xc = xc + modc[2] * (jnp.concatenate([yac, ybc], axis=-1) @ w_out)
        h = _modulate(_rms_norm(x, norm2_g[layer]), mod[3], mod[4])
        x = x + mod[5] * _peer(h, peer_wq[layer], peer_keys[layer], peer_u[layer], peer_v[layer])
        if need_ctx:
            hc = _modulate(_rms_norm(xc, norm2_g[layer]), modc[3], modc[4])
            xc = xc + modc[5] * _peer(hc, peer_wq[layer], peer_keys[layer], peer_u[layer], peer_v[layer])
    return _rms_norm(x, final_g)


_drawn_inputs = setup_inputs


def setup_inputs(seed=0):
    import zlib

    import numpy as np

    out = dict(_drawn_inputs(seed))
    spreads = {}
    factors = {'gqa_qn_g': 7.35,
     'gqa_kn_g': 8.0,
     'hg_onorm_g': 2.966,
     'mla_qa_g': 8.0,
     'mla_kva_g': 6.332,
     's5_a_re': 200.0,
     's5_b_glu': 64.0,
     'final_g': 24.065,
     's5_a_im': 64.0,
     's5_log_dt': 64.0,
     's5_b_re': 64.0,
     's5_b_im': 64.0,
     's5_c_re': 64.0,
     's5_c_im': 64.0}
    for name, (base, spread) in spreads.items():
        noise = np.random.default_rng([zlib.crc32(name.encode()), seed]).standard_normal(out[name].shape)
        drawn = base * np.exp(spread * noise) if base else spread * noise
        out[name] = __import__('jax').numpy.asarray(drawn.astype(out[name].dtype))
    for name, factor in factors.items():
        out[name] = (out[name] * factor).astype(out[name].dtype)
    return out
```

```python
from contextlib import ExitStack

import numpy as np

import concourse.bass as bass
from concourse import mybir

F32 = mybir.dt.float32
F32R = mybir.dt.float32r
U32 = mybir.dt.uint32
ACT = mybir.ActivationFunctionType
ALU = mybir.AluOpType
AX = mybir.AxisListType

P = 128
D = 1024
DK = D // P
CTX, LAT = 256, 512
T = CTX + LAT
GRID_W = 64
EPS = 1e-6
BANK = 512

GQA_Q, GQA_KV, HEAD = 8, 2, 64
GQA_IN = (GQA_Q + 2 * GQA_KV) * HEAD
HG_HEADS = 4
EVEN_IN = GQA_IN + 5 * 512
MLA_H, MLA_NOPE, MLA_ROPE, MLA_V = 8, 64, 32, 64
MLA_QR, MLA_KVR = 384, 256
MLA_IN = MLA_QR + MLA_KVR + MLA_ROPE
ODD_IN = MLA_IN + 512
S5_G, S5_P, S5_C = 32, 64, 16

PEER_H, KEYS, TOPK, QDIM = 8, 128, 16, 256
SLOTS = PEER_H * TOPK
EXPERTS = KEYS * KEYS
LOWEST = -3.0e38
FIRST_SEM, SEM_BANK = 100, 77

VEC = {}
for _name, _n in (("c", 8), ("c_ctx", 8), ("norm1", 16), ("norm2", 16), ("final", 8), ("lb", 16), ("onorm", 1),
                  ("s5_d", 4), ("s5_bglu", 4), ("mla_qa", 3), ("mla_kva", 2)):
    VEC[_name] = (sum(n for _, n in VEC.values()), _n)
VEC_ROWS = sum(n for _, n in VEC.values())


class Steps:

    def __init__(self, engine, sem):
        self.engine, self.sem, self.n = engine, sem, 0

    def __call__(self, instruction):
        instruction.then_inc(self.sem, 1)
        self.n += 1

    def settle(self):
        self.engine.wait_ge(self.sem, self.n)


class Arena:

    uses = {}
    stages = 0

    def __init__(self, nc, stack):
        self.nc, self.stack, self.sems = nc, stack, []

    @staticmethod
    def fresh(name):
        Arena.uses[name] = n = Arena.uses.get(name, 0) + 1
        return name if n == 1 else f"{name}_{n}"

    def sb(self, name, shape, dt=F32):
        return self.stack.enter_context(self.nc.sbuf_tensor(Arena.fresh(name), shape, dt))

    def sem(self, *names):
        if not self.sems:
            Arena.stages += 1
            self.stack.callback(self.clear)
        base = FIRST_SEM + (Arena.stages % 2) * SEM_BANK
        for name in names:
            assert len(self.sems) < SEM_BANK
            self.sems.append(self.nc.alloc_semaphore(Arena.fresh(name), num=base + len(self.sems)))
        got = self.sems[-len(names):]
        return got[0] if len(got) == 1 else got

    def clear(self):
        base = FIRST_SEM + (Arena.stages % 2) * SEM_BANK
        self.nc.gpsimd.sem_clear(range(base, base + len(self.sems)))
        for sem in self.sems:
            self.nc.release_semaphore(sem)

    def block(self):
        return self.stack.enter_context(self.nc.Block())


def stage_load_tokens(nc, g):
    with ExitStack() as stack:
        a = Arena(nc, stack)
        tokens = a.sb("tokens", [P, T // P, D])
        rows = a.sb("rows", [VEC_ROWS, P])
        ada_rows = a.sb("ada_rows", [96, P])
        const_loaded, rows_loaded, tile_loaded = a.sem("const_loaded", "rows_loaded", "tile_loaded")
        transposed, evacuated_v, evacuated_s = a.sem("transposed", "evacuated_v", "evacuated_s")
        block = a.block()
        ps = g.ps

        @block.sync
        def _(sp):
            sp.dma_start(g.ident[:], g.d["k_ident"]).then_inc(const_loaded, 16)
            for j in range(T // P):
                src = g.d["ctx"][0, j * P:(j + 1) * P, :] if j < 2 else g.d["x"][0, (j - 2) * P:(j - 1) * P, :]
                if j:
                    sp.wait_ge(tile_loaded, 16 * j)
                sp.dma_start(tokens[:, j, :], src).then_inc(tile_loaded, 16)

        n_rows = 16 * (len(VEC) + 1)

        @block.tensor
        def _(pe):
            pe.wait_ge(const_loaded, 16)
            for j in range(T // P):
                pe.wait_ge(tile_loaded, 16 * (j + 1))
                slot = j % 3
                if j >= 3:
                    pe.wait_ge(evacuated_v, j - 2)
                    pe.wait_ge(evacuated_s, j - 2)
                for k in range(DK):
                    last = nc.tensor.transpose(ps[:, (slot * 8 + k) * P:(slot * 8 + k + 1) * P],
                                               tokens[:, j, k * P:(k + 1) * P], g.ident[:])
                last.then_inc(transposed, 1)
            pe.wait_ge(rows_loaded, n_rows)
            nc.tensor.transpose(ps[:, 6 * BANK:6 * BANK + VEC_ROWS], rows[:], g.ident[:VEC_ROWS, :VEC_ROWS])
            nc.tensor.transpose(ps[:, 7 * BANK:7 * BANK + 96], ada_rows[:], g.ident[:96, :96]).then_inc(transposed, 1)

        @block.vector
        def _(dve):
            nc.vector.memset(g.ones_d[:], 1.0 / D)
            for j in range(T // P):
                dve.wait_ge(transposed, j + 1)
                src = ps[:, (j % 3) * 1024:(j % 3) * 1024 + 512].rearrange("p (k t) -> p k t", t=P)
                nc.vector.tensor_copy(g.x_t[:, 0:4, j * P:(j + 1) * P], src).then_inc(evacuated_v, 1)
            dve.wait_ge(transposed, T // P + 1)
            nc.vector.tensor_copy(g.vec[:], ps[:, 6 * BANK:6 * BANK + VEC_ROWS])
            nc.vector.tensor_copy(g.ada_b[:], ps[:, 7 * BANK:7 * BANK + 96])

        @block.scalar
        def _(act):
            d = g.d
            loads = [("c", d["c"].rearrange("o (k p) -> (o k) p", p=P)),
                     ("c_ctx", d["c_ctx"].rearrange("(k p) -> k p", p=P)),
                     ("norm1", d["norm1_g"].rearrange("l (k p) -> (l k) p", p=P)),
                     ("norm2", d["norm2_g"].rearrange("l (k p) -> (l k) p", p=P)),
                     ("final", d["final_g"].rearrange("(k p) -> k p", p=P)),
                     ("lb", d["hg_lb_logits"].rearrange("d e (k p) -> (d e k) p", p=P)),
                     ("onorm", d["hg_onorm_g"]),
                     ("s5_d", d["s5_d"].rearrange("o (k p) -> (o k) p", p=P)),
                     ("s5_bglu", d["s5_b_glu"].rearrange("o (k p) -> (o k) p", p=P)),
                     ("mla_qa", d["mla_qa_g"].rearrange("o (k p) -> (o k) p", p=P)),
                     ("mla_kva", d["mla_kva_g"].rearrange("o (k p) -> (o k) p", p=P))]
            for name, src in loads:
                at, n = VEC[name]
                act.dma_start(rows[at:at + n, :], src).then_inc(rows_loaded, 16)
            act.dma_start(ada_rows[:], d["ada_b"].rearrange("l (k p) -> (l k) p", p=P)).then_inc(rows_loaded, 16)
            for j in range(T // P):
                act.wait_ge(transposed, j + 1)
                src = ps[:, (j % 3) * 1024 + 512:(j % 3) * 1024 + 1024].rearrange("p (k t) -> p k t", t=P)
                nc.scalar.copy(g.x_t[:, 4:8, j * P:(j + 1) * P], src).then_inc(evacuated_s, 1)


def stage_modulation(nc, g):
    COLS, RING = 512, 3
    with ExitStack() as stack:
        a = Arena(nc, stack)
        w = a.sb("ada_ring", [P, RING, DK, COLS])
        cond = a.sb("cond", [P, 2, DK])
        w_loaded = [a.sem(f"w_loaded{r}") for r in range(RING)]
        summed = [a.sem(f"summed{r}") for r in range(RING)]
        kept = [a.sem(f"kept{r}") for r in range(RING)]
        cond_ready, scaled = a.sem("cond_ready", "scaled")
        block = a.block()
        ps = g.ps
        tiles = COLS // P
        ada = [g.d["ada_w"][layer].rearrange("(k p) n -> p k n", p=P) for layer in range(2)]
        turns = 6 * D // COLS // RING

        def ring_turns(engine, emit):
            emit(0, 0, True)
            for layer in range(2):
                with engine.Fori(1 - layer, turns) as i:
                    emit(layer, i, False)

        @block.sync
        def _(sp):
            def turn(layer, i, first):
                for r in range(RING):
                    if not first:
                        sp.wait_ge(summed[r], i + layer * turns)
                    sp.dma_start(w[:, r], ada[layer][:, :, bass.ds((i * RING + r) * COLS, COLS)])\
                        .then_inc(w_loaded[r], 16)

            ring_turns(sp, turn)

        @block.scalar
        def _(act):
            nc.scalar.activation(cond[:], g.vec[:, 0:16].rearrange("p (s k) -> p s k", s=2), ACT.Silu)\
                .then_inc(cond_ready, 1)

        @block.tensor
        def _(pe):
            def turn(layer, i, first):
                for r in range(RING):
                    pe.wait_ge(w_loaded[r], i * 16 + (layer * turns + 1) * 16)
                    if not first:
                        pe.wait_ge(kept[r], i + layer * turns)
                    for m in range(tiles):
                        for k in range(DK):
                            last = nc.tensor.matmul(ps[:, r * BANK + 2 * m:r * BANK + 2 * m + 2],
                                                    w[:, r, k, m * P:(m + 1) * P], cond[:, :, k],
                                                    start=(k == 0), stop=(k == DK - 1))
                    last.then_inc(summed[r], 1)

            pe.wait_ge(cond_ready, 1)
            ring_turns(pe, turn)

        @block.vector
        def _(dve):
            def turn(layer, i, first):
                bias = g.ada_b[:, 48 * layer:48 * (layer + 1)]
                for r in range(RING):
                    dve.wait_ge(summed[r], i + layer * turns + 1)
                    sums = ps[:, r * BANK:r * BANK + 2 * tiles].rearrange("p (m s) -> p m s", s=2)
                    for s in range(2):
                        last = nc.vector.tensor_tensor(g.mod[:, layer, bass.ds((i * RING + r) * tiles, tiles), s],
                                                       sums[:, :, s],
                                                       bias[:, bass.ds((i * RING + r) * tiles, tiles)], ALU.add)
                    last.then_inc(kept[r], 1)

            ring_turns(dve, turn)
            for r in range(RING):
                dve.wait_ge(kept[r], 2 * turns)
            own = Steps(dve, scaled)
            for layer in range(2):
                for which, (norm, part) in enumerate((("norm1", 1), ("norm2", 4))):
                    at = VEC[norm][0] + 8 * layer
                    gs = g.gs[:, layer, which]
                    own(nc.vector.tensor_scalar(gs, g.mod[:, layer, 8 * part:8 * part + 8, :], 1.0, None, ALU.add))
                    own.settle()
                    own(nc.vector.tensor_tensor(gs, gs, g.vec[:, at:at + 8].unsqueeze(2).to_broadcast([P, 8, 2]),
                                                ALU.mult))


STREAMS = ((1, 0, CTX), (0, CTX, T))


def stage_norm(nc, g, layer, which, t0, h_t, latents_first=False):
    n = T - t0

    def cols(b, e):
        if latents_first:
            b, e = ((b + LAT, e + LAT) if b < CTX else (b - CTX, e - CTX))
            return slice(b, e)
        return slice(b - t0, e - t0)

    parts = [(s, e) for s, e in ((t0, CTX), (CTX, T)) if e > s]
    streams = [(s, max(b, t0), e) for s, b, e in STREAMS if e > t0]
    shift = 8 * 3 * which
    with ExitStack() as stack:
        a = Arena(nc, stack)
        sq = a.sb("sq", [P, DK, n])
        rstd = a.sb("rstd", [P, n])
        squared, summed, root_in, rooted, scaled = a.sem("squared", "summed", "root_in", "rooted", "scaled")
        own_v = a.sem("own_v")
        block = a.block()
        ps = g.ps

        @block.scalar
        def _(act):
            for k in range(DK):
                nc.scalar.activation(sq[:, k], g.x_t[:, k, t0:T], ACT.Square).then_inc(squared, 1)
            act.wait_ge(root_in, 1)
            nc.scalar.activation(rstd[:], rstd[:], ACT.Sqrt).then_inc(rooted, 1)
            for k in range(DK):
                for i, (s, b, e) in enumerate(streams):
                    act.wait_ge(scaled, len(streams) * k + i + 1)
                    nc.scalar.activation(h_t[:, k, cols(b, e)], h_t[:, k, cols(b, e)], ACT.Identity,
                                         bias=g.mod[:, layer, shift + k, s:s + 1])

        @block.tensor
        def _(pe):
            for k in range(DK):
                pe.wait_ge(squared, k + 1)
                for i, (b, e) in enumerate(parts):
                    last = nc.tensor.matmul(ps[:, i * BANK:i * BANK + e - b], g.ones_d[:], sq[:, k, b - t0:e - t0],
                                            start=(k == 0), stop=(k == DK - 1))
            last.then_inc(summed, 1)

        @block.vector
        def _(dve):
            own = Steps(dve, own_v)
            dve.wait_ge(summed, 1)
            for i, (b, e) in enumerate(parts):
                last = nc.vector.tensor_scalar(rstd[:, b - t0:e - t0], ps[:, i * BANK:i * BANK + e - b], EPS, None,
                                               ALU.add)
            last.then_inc(root_in, 1)
            dve.wait_ge(rooted, 1)
            own(nc.vector.reciprocal(rstd[:], rstd[:]))
            own.settle()
            for k in range(DK):
                for s, b, e in streams:
                    nc.vector.scalar_tensor_tensor(out=h_t[:, k, cols(b, e)], in0=g.x_t[:, k, b:e],
                                                   scalar=g.gs[:, layer, which, k, s:s + 1],
                                                   in1=rstd[:, b - t0:e - t0],
                                                   op0=ALU.mult, op1=ALU.mult).then_inc(scaled, 1)


def halves(n):
    return [(b, min(b + BANK, n)) for b in range(0, n, BANK)]


def stage_project(nc, g, name, h_t, w_view, blocks, kc=DK):
    RING, SLOTS_PS = 3, 4
    widest = max(cols for _, cols, _ in blocks)
    units = [(b, kind, place, out) for b, (_, _, us) in enumerate(blocks) for kind, place, out in us]
    with ExitStack() as stack:
        a = Arena(nc, stack)
        w = a.sb(f"{name}_ring", [P, min(RING, len(blocks)), kc, widest])
        ring = min(RING, len(blocks))
        w_loaded = [a.sem(f"w_loaded{r}") for r in range(ring)]
        w_used, summed, kept_v, kept_s = a.sem("w_used", "summed", "kept_v", "kept_s")
        block = a.block()
        ps = g.ps

        @block.sync
        def _(sp):
            for b, (c0, cols, _) in enumerate(blocks):
                if b >= ring:
                    sp.wait_ge(w_used, b - ring + 1)
                sp.dma_start(w[:, b % ring, :, 0:cols], w_view[:, :, c0:c0 + cols]).then_inc(w_loaded[b % ring], 16)

        @block.tensor
        def _(pe):
            for u, (b, kind, place, _) in enumerate(units):
                cols = blocks[b][1]
                at = (u % SLOTS_PS) * 2 * BANK
                pe.wait_ge(w_loaded[b % ring], 16 * (b // ring + 1))
                if u >= SLOTS_PS:
                    pe.wait_ge(kept_s if u % 2 else kept_v, (u - SLOTS_PS) // 2 + 1)
                for k in range(kc):
                    if kind != "tokens":
                        m = min(P, cols - place)
                        t0 = CTX if kind == "latents" else 0
                        for lo, hi in halves(h_t.shape[2] - t0):
                            last = nc.tensor.matmul(ps[0:m, at + lo:at + hi], w[:, b % ring, k, place:place + m],
                                                    h_t[:, k, t0 + lo:t0 + hi], start=(k == 0), stop=(k == kc - 1))
                    else:
                        last = nc.tensor.matmul(ps[:, at:at + cols], h_t[:, k, place * P:(place + 1) * P],
                                                w[:, b % ring, k, 0:cols], start=(k == 0), stop=(k == kc - 1))
                last.then_inc(summed, 1)
                if u + 1 == len(units) or units[u + 1][0] != b:
                    pe.wait_ge(summed, u + 1)
                    pe.sem_inc(w_used, 1)

        def result(u):
            b, kind, place, _ = units[u]
            at = (u % SLOTS_PS) * 2 * BANK
            cols = blocks[b][1]
            if kind != "tokens":
                return ps[0:min(P, cols - place), at:at + h_t.shape[2] - (CTX if kind == "latents" else 0)]
            if len(units[u][3].shape) == 4:
                _, kv, j, c = units[u][3].shape
                return ps[:, at:at + cols].rearrange("p (kv j c) -> p kv j c", kv=kv, j=j)
            return ps[:, at:at + cols]

        @block.vector
        def _(dve):
            for u in range(0, len(units), 2):
                dve.wait_ge(summed, u + 1)
                nc.vector.tensor_copy(units[u][3], result(u)).then_inc(kept_v, 1)

        @block.scalar
        def _(act):
            for u in range(1, len(units), 2):
                act.wait_ge(summed, u + 1)
                nc.scalar.copy(units[u][3], result(u)).then_inc(kept_s, 1)


def channel_units(out, tiles):
    return [("channels", m * P, out[:, m, :]) for m in range(tiles)]


def token_units(out, tiles):
    return [("tokens", j, out[:, j, :]) for j in range(tiles)]


def stage_gqa_heads(nc, g, proj, q_t, k_t):
    NT, NH, N = T // P, GQA_Q + GQA_KV, (GQA_Q + GQA_KV) * HEAD
    with ExitStack() as stack:
        a = Arena(nc, stack)
        sq = a.sb("sq", [P, NT, N])
        heads = a.sb("heads", [P, NT, N])
        rstd = a.sb("rstd", [P, NT, NH])
        gain = a.sb("gain", [P, 2, HEAD])
        rope = a.sb("rope", [P, 2, 4, 2, 16])
        scratch = a.sb("scratch", [P, 4, NH * 2 * 16])
        loaded, root_in, rooted, ready, transposed, kept, own_v = a.sem(
            "loaded", "root_in", "rooted", "ready", "transposed", "kept", "own_v")
        block = a.block()
        ps = g.ps

        @block.sync
        def _(sp):
            sp.dma_start(gain[:, 0, :], g.d["gqa_qn_g"].to_broadcast([P, HEAD])).then_inc(loaded, 16)
            sp.dma_start(gain[:, 1, :], g.d["gqa_kn_g"].to_broadcast([P, HEAD])).then_inc(loaded, 16)
            sp.dma_start(rope[:], g.d["k_rope_gqa"]).then_inc(loaded, 16)

        @block.vector
        def _(dve):
            own = Steps(dve, own_v)
            own(nc.vector.tensor_tensor(sq[:], proj[:, :, 0:N], proj[:, :, 0:N], ALU.mult))
            own.settle()
            own(nc.vector.tensor_reduce(rstd[:], sq[:].rearrange("p t (h c) -> p t h c", c=HEAD), AX.X, ALU.add))
            own.settle()
            nc.vector.tensor_scalar(rstd[:], rstd[:], 1.0 / HEAD, EPS, ALU.mult, ALU.add).then_inc(root_in, 1)
            dve.wait_ge(rooted, 1)
            own(nc.vector.reciprocal(rstd[:], rstd[:]))
            own.settle()
            own(nc.vector.tensor_scalar(rstd[:, :, 0:GQA_Q], rstd[:, :, 0:GQA_Q], HEAD ** -0.5, None, ALU.mult))
            own.settle()
            for t in range(NT):
                own(nc.vector.tensor_tensor(sq[:, t].rearrange("p (h c) -> p h c", c=HEAD),
                                            proj[:, t, 0:N].rearrange("p (h c) -> p h c", c=HEAD),
                                            rstd[:, t].unsqueeze(2).to_broadcast([P, NH, HEAD]), ALU.mult))
            dve.wait_ge(loaded, 48)
            own.settle()
            for which, h0, nh in ((0, 0, GQA_Q), (1, GQA_Q, GQA_KV)):
                cols = slice(h0 * HEAD, (h0 + nh) * HEAD)
                for out, lo, hi in ((heads, 0, 2), (sq, 2, NT)):
                    for t in range(lo, hi):
                        own(nc.vector.tensor_tensor(out[:, t, cols].rearrange("p (h c) -> p h c", c=HEAD),
                                                    sq[:, t, cols].rearrange("p (h c) -> p h c", c=HEAD),
                                                    gain[:, which, :].unsqueeze(1).to_broadcast([P, nh, HEAD]),
                                                    ALU.mult))
            own.settle()
            dve.sem_inc(ready, 2)
            for t in range(2, NT):
                for axis in range(2):
                    def half(x, i):
                        return x[:, t].rearrange("p (h a i c) -> p h a i c", a=2, i=2, c=16)[:, :, axis, i, :]

                    cos, sin = (rope[:, w, t - 2, axis, :].unsqueeze(1).to_broadcast([P, NH, 16]) for w in range(2))
                    parts = [scratch[:, 2 * axis + w, 0:NH * 16].rearrange("p (h c) -> p h c", c=16)
                             for w in range(2)]
                    parts += [scratch[:, 2 * axis + w, NH * 16:].rearrange("p (h c) -> p h c", c=16)
                              for w in range(2)]
                    own(nc.vector.tensor_tensor(parts[0], half(sq, 0), cos, ALU.mult))
                    own(nc.vector.tensor_tensor(parts[1], half(sq, 1), sin, ALU.mult))
                    own(nc.vector.tensor_tensor(parts[2], half(sq, 0), sin, ALU.mult))
                    own(nc.vector.tensor_tensor(parts[3], half(sq, 1), cos, ALU.mult))
                    own.settle()
                    own(nc.vector.tensor_tensor(half(heads, 0), parts[0], parts[1], ALU.subtract))
                    own(nc.vector.tensor_tensor(half(heads, 1), parts[2], parts[3], ALU.add))
                own.settle()
                dve.sem_inc(ready, 1)

        @block.tensor
        def _(pe):
            for t in range(NT):
                pe.wait_ge(ready, t + 1)
                if t >= 4:
                    pe.wait_ge(kept, t - 3)
                at = (t % 4) * 1024
                for j in range(4):
                    nc.tensor.transpose(ps[:, at + j * P:at + (j + 1) * P], heads[:, t, j * P:(j + 1) * P], g.ident[:])
                nc.tensor.transpose(ps[:, at + 4 * P:at + 5 * P], heads[:, t, GQA_Q * HEAD:N], g.ident[:])\
                    .then_inc(transposed, 1)

        @block.scalar
        def _(act):
            act.wait_ge(root_in, 1)
            nc.scalar.activation(rstd[:], rstd[:], ACT.Sqrt).then_inc(rooted, 1)
            for t in range(NT):
                act.wait_ge(transposed, t + 1)
                at = (t % 4) * 1024
                nc.scalar.copy(q_t[:, :, t * P:(t + 1) * P],
                               ps[:, at:at + 4 * P].rearrange("p (j t) -> p j t", t=P))
                nc.scalar.copy(k_t[:, t * P:(t + 1) * P], ps[:, at + 4 * P:at + 5 * P]).then_inc(kept, 1)


def stage_attention(nc, g, units):
    widest = max(u[1].shape[1] for u in units)
    with ExitStack() as stack:
        a = Arena(nc, stack)
        probs = a.sb("probs", [P, 2, widest])
        probs_t = a.sb("probs_t", [P, 2, widest])
        neg_max = a.sb("neg_max", [P, 2, 1])
        sums = a.sb("sums", [P, 2, 1])
        inverse = a.sb("inverse", [P, 2, 1])
        scores_ready, max_ready, exps_ready, probs_ready, transposed, probs_t_ready, mixed, out_kept, own_v = a.sem(
            "scores_ready", "max_ready", "exps_ready", "probs_ready", "transposed", "probs_t_ready", "mixed",
            "out_kept", "own_v")
        block = a.block()
        ps = g.ps
        T_AT, O_AT = 4 * BANK, 6 * BANK
        n_units = len(units)

        @block.tensor
        def _(pe):
            def scores(u):
                q, k = units[u][0], units[u][1]
                n = k.shape[1]
                if u >= 2:
                    pe.wait_ge(exps_ready, u - 1)
                for lo, hi in halves(n):
                    last = nc.tensor.matmul(ps[:, (u % 2) * 1024 + lo:(u % 2) * 1024 + hi], q, k[:, lo:hi],
                                            start=True, stop=True)
                last.then_inc(scores_ready, 1)

            def mix(u):
                _, k, v, p0, _ = units[u]
                tiles = k.shape[1] // P
                pe.wait_ge(probs_ready, u + 1)
                if u >= 1:
                    pe.wait_ge(probs_t_ready, u)
                for i in range(tiles):
                    last = nc.tensor.transpose(ps[:, T_AT + i * P:T_AT + (i + 1) * P],
                                               probs[:, u % 2, i * P:(i + 1) * P], g.ident[:])
                last.then_inc(transposed, 1)
                pe.wait_ge(probs_t_ready, u + 1)
                if u >= 4:
                    pe.wait_ge(out_kept, (u // 2) - 1)
                at = O_AT + (u // 2 % 2) * BANK
                for i in range(tiles):
                    last = nc.tensor.matmul(ps[p0:p0 + 64, at:at + P], v(i), probs_t[:, u % 2, i * P:(i + 1) * P],
                                            start=(i == 0), stop=(i == tiles - 1))
                last.then_inc(mixed, 1)

            scores(0)
            for u in range(n_units):
                if u + 1 < n_units:
                    scores(u + 1)
                mix(u)

        @block.vector
        def _(dve):
            own = Steps(dve, own_v)

            def maximum(u):
                n = units[u][1].shape[1]
                dve.wait_ge(scores_ready, u + 1)
                if u >= 2:
                    dve.wait_ge(exps_ready, u - 1)
                nc.vector.tensor_reduce(neg_max[:, u % 2], ps[:, (u % 2) * 1024:(u % 2) * 1024 + n], AX.X, ALU.max,
                                        negate=True).then_inc(max_ready, 1)

            def output(u):
                if u % 2 == 0:
                    return
                dve.wait_ge(mixed, u + 1)
                at = O_AT + (u // 2 % 2) * BANK
                nc.vector.tensor_copy(units[u][4], ps[:, at:at + P]).then_inc(out_kept, 1)

            maximum(0)
            for u in range(n_units):
                n = units[u][1].shape[1]
                if u + 1 < n_units:
                    maximum(u + 1)
                dve.wait_ge(exps_ready, u + 1)
                own(nc.vector.reciprocal(inverse[:, u % 2], sums[:, u % 2]))
                own.settle()
                nc.vector.tensor_scalar(probs[:, u % 2, 0:n], probs[:, u % 2, 0:n], inverse[:, u % 2], None,
                                        ALU.mult).then_inc(probs_ready, 1)
                if u >= 1:
                    output(u - 1)
            output(n_units - 1)

        @block.scalar
        def _(act):
            def exps(u):
                n = units[u][1].shape[1]
                act.wait_ge(max_ready, u + 1)
                if u >= 2:
                    act.wait_ge(transposed, u - 1)
                    act.wait_ge(probs_ready, u - 1)
                nc.scalar.activation(probs[:, u % 2, 0:n], ps[:, (u % 2) * 1024:(u % 2) * 1024 + n], ACT.Exp,
                                     bias=neg_max[:, u % 2], accum_out=sums[:, u % 2]).then_inc(exps_ready, 1)

            exps(0)
            for u in range(n_units):
                n = units[u][1].shape[1]
                if u + 1 < n_units:
                    exps(u + 1)
                act.wait_ge(transposed, u + 1)
                if u >= 2:
                    act.wait_ge(mixed, u - 1)
                nc.scalar.copy(probs_t[:, u % 2, 0:n], ps[:, T_AT:T_AT + n]).then_inc(probs_t_ready, 1)


def build(nc, d, out, until=99, keep=None):
    class G:
        pass

    g = G()
    Arena.uses.clear()
    Arena.stages = 0
    g.d, g.out = d, out
    g.keep = keep
    with ExitStack() as stack:
        a = Arena(nc, stack)
        psum = stack.enter_context(nc.psum_tensor("banks", [P, 8 * BANK], F32))
        g.ps = psum
        g.ident = a.sb("ident", [P, P])
        g.ones_d = a.sb("ones_d", [P, P])
        g.vec = a.sb("vec", [P, VEC_ROWS])
        g.ada_b = a.sb("ada_bias", [P, 96])
        g.mod = a.sb("mod", [P, 2, 48, 2])
        g.gs = a.sb("gs", [P, 2, 2, DK, 2])
        g.x_t = a.sb("x_t", [P, DK, T])
        stage_load_tokens(nc, g)
        stage_modulation(nc, g)
        if until >= 1:
            layer_even(nc, g, until)
        if until >= 8:
            layer_odd(nc, g, until)


HG_LEVELS = (64, 32, 16, 8, 4, 2, 1)
NL = len(HG_LEVELS) + 1


def stage_hgrn2_gates(nc, g, hg, forget, keep_k, cum):
    N = HG_HEADS * T
    with ExitStack() as stack:
        a = Arena(nc, stack)
        lb = a.sb("lb", [P, 5, 2, HG_HEADS])
        restart = a.sb("restart", [P, 2, T])
        gate_ready, sig_ready, f_ready, log_ready, lb_in, lb_exp, own_v, cum_done = a.sem(
            "gate_ready", "sig_ready", "f_ready", "log_ready", "lb_in", "lb_exp", "own_v", "cum_done")
        block = a.block()
        at = VEC["lb"][0]
        logits = g.vec[:, at:at + 16].rearrange("p (d e h) -> p d e h", d=2, e=2)

        @block.scalar
        def _(act):
            act.wait_ge(lb_in, 2)
            nc.scalar.activation(lb[:, 0:2], lb[:, 0:2], ACT.Exp).then_inc(lb_exp, 1)
            for d in range(2):
                nc.scalar.activation(keep_k[:, d * 4:d * 4 + 4], hg[:, 1 + d], ACT.Sigmoid).then_inc(sig_ready, 1)
            for d in range(2):
                act.wait_ge(f_ready, d + 1)
                if d:
                    act.wait_ge(cum_done, 1)
                nc.scalar.activation(forget[:], keep_k[:, d * 4:d * 4 + 4], ACT.Ln).then_inc(log_ready, 1)

        @block.vector
        def _(dve):
            own = Steps(dve, own_v)
            own(nc.vector.tensor_tensor(lb[:, 2], logits[:, :, 0], logits[:, :, 1], ALU.max))
            own.settle()
            for e in range(2):
                nc.vector.tensor_tensor(lb[:, e], logits[:, :, e], lb[:, 2], ALU.subtract).then_inc(lb_in, 1)
            for d in range(2):
                own(nc.vector.memset(restart[:, d], 1.0))
            own.settle()
            own(nc.vector.memset(restart[:, 0].rearrange("p (n t) -> p n t", t=P)[:, :, 0:1], 0.0))
            own(nc.vector.memset(restart[:, 1].rearrange("p (n t) -> p n t", t=P)[:, :, P - 1:P], 0.0))
            dve.wait_ge(lb_exp, 1)
            own(nc.vector.tensor_tensor(lb[:, 3], lb[:, 0], lb[:, 1], ALU.add))
            own.settle()
            own(nc.vector.reciprocal(lb[:, 3], lb[:, 3]))
            own.settle()
            own(nc.vector.tensor_tensor(lb[:, 4], lb[:, 0], lb[:, 3], ALU.mult))
            own.settle()
            own(nc.vector.tensor_scalar(lb[:, 3], lb[:, 4], -1.0, 1.0, ALU.mult, ALU.add))
            own.settle()
            for d in range(2):
                dve.wait_ge(sig_ready, d + 1)
                for h in range(HG_HEADS):
                    own(nc.vector.tensor_scalar(keep_k[:, d * 4 + h], keep_k[:, d * 4 + h], lb[:, 3, d, h:h + 1],
                                                lb[:, 4, d, h:h + 1], ALU.mult, ALU.add))
                own.settle()
                nc.vector.tensor_scalar(keep_k[:, d * 4:d * 4 + 4], keep_k[:, d * 4:d * 4 + 4], 1e-19, None,
                                        ALU.max).then_inc(f_ready, 1)
            for d in range(2):
                dve.wait_ge(log_ready, d + 1)
                own(nc.vector.tensor_scalar(keep_k[:, d * 4:d * 4 + 4], keep_k[:, d * 4:d * 4 + 4], -1.0, 1.0,
                                            ALU.mult, ALU.add))
                for h in range(HG_HEADS):
                    src, out = forget[:, h], cum[:, d * 4 + h]
                    if d:
                        src, out = src[:, ::-1], out[:, ::-1]
                    last = nc.vector.tensor_tensor_scan(out, restart[:, d][:, ::-1] if d else restart[:, d], src,
                                                        0.0, ALU.mult, ALU.add)
                    if h < HG_HEADS - 1:
                        own(last)
                last.then_inc(cum_done, 1)


def stage_hgrn2_scan(nc, g, hg, hg_v, keep_k, cum, y_t):
    NC = T // P
    units = [(d, h) for h in range(HG_HEADS) for d in range(2)]
    orders = [list(range(NC)), [1, 0] + list(range(NC - 1, 1, -1))]
    with ExitStack() as stack:
        a = Arena(nc, stack)
        masks = a.sb("masks", [P, NL * P])
        z = a.sb("z", [P, len(HG_LEVELS), T])
        expo = a.sb("expo", [P, 2, T])
        q_dec = a.sb("q_dec", [P, T])
        k_dec = a.sb("k_dec", [P, T])
        k_tok = a.sb("k_tok", [P, T])
        last_dec = a.sb("last_dec", [P, NC])
        state = a.sb("state", [P, 2, P])
        pairs = a.sb("pairs", [P, 2, NL * P])
        (mask_loaded, expo_in, expo_out, z_ready, dec_ready, k_turned, k_tok_ready, gram_ready, pairs_ready,
         out_ready, out_kept, update_ready, state_ready, own_v) = a.sem(
            "mask_loaded", "expo_in", "expo_out", "z_ready", "dec_ready", "k_turned", "k_tok_ready", "gram_ready",
            "pairs_ready", "out_ready", "out_kept", "update_ready", "state_ready", "own_v")
        block = a.block()
        ps = g.ps
        E = len(HG_LEVELS) + 2
        GRAM, TURN, OUT, UPD = 0, 4 * BANK, 6 * BANK, 7 * BANK

        def sides(m, x, d):
            v = x.rearrange("p (b i t) -> p b i t", i=2, t=m)
            r = v[:, :, d, m - 1:m] if d == 0 else v[:, :, d, 0:1]
            r = v[:, :, 0, m - 1:m] if d == 0 else v[:, :, 1, 0:1]
            return v[:, :, 1 - d, :], v[:, :, d, :], r.to_broadcast([P, T // (2 * m), m])

        @block.sync
        def _(sp):
            for u in range(len(units)):
                d, h = units[u]
                if u:
                    sp.wait_ge(pairs_ready, NC * u)
                sp.dma_start(masks[:], g.d["k_hg_masks"][d]).then_inc(mask_loaded, 16)

        @block.scalar
        def _(act):
            n = 0
            for u, (d, h) in enumerate(units):
                for e in range(E):
                    act.wait_ge(expo_in, u * E + e + 1)
                    nc.scalar.activation(expo[:, e % 2], expo[:, e % 2], ACT.Exp).then_inc(expo_out, 1)
                act.wait_ge(k_turned, u + 1)
                nc.scalar.copy(k_tok[:], ps[:, TURN:TURN + T]).then_inc(k_tok_ready, 1)
                for i, c in enumerate(orders[d]):
                    act.wait_ge(out_ready, u * NC + i + 1)
                    out = y_t[:, 4 + h, c * P:(c + 1) * P]
                    if d == 0:
                        nc.scalar.copy(out, ps[:, OUT:OUT + P]).then_inc(out_kept, 1)

        @block.vector
        def _(dve):
            own = Steps(dve, own_v)
            for u, (d, h) in enumerate(units):
                unit = d * 4 + h
                q, k, c = hg[:, 0, h], keep_k[:, unit], cum[:, unit]
                last_of = c.rearrange("p (n t) -> p n t", t=P)[:, :, 0:1] if d else \
                    c.rearrange("p (n t) -> p n t", t=P)[:, :, P - 1:P]

                def differences(e, u=u, c=c, d=d, last_of=last_of):
                    if e >= 2:
                        own.settle()
                    x = expo[:, e % 2]
                    if e < len(HG_LEVELS):
                        m = HG_LEVELS[e]
                        cq, ck, r = sides(m, c, d)
                        xq, xk, _ = sides(m, x, d)
                        own(nc.vector.tensor_tensor(xq, cq, r, ALU.subtract))
                        nc.vector.tensor_tensor(xk, r, ck, ALU.subtract).then_inc(expo_in, 1)
                    elif e == len(HG_LEVELS):
                        nc.vector.tensor_copy(x, c).then_inc(expo_in, 1)
                    else:
                        nc.vector.tensor_tensor(x.rearrange("p (n t) -> p n t", t=P), last_of.to_broadcast([P, NC, P]),
                                                c.rearrange("p (n t) -> p n t", t=P), ALU.subtract).then_inc(expo_in, 1)

                if u:
                    dve.wait_ge(out_ready, u * NC)
                differences(0)
                for e in range(E):
                    if e + 1 < E:
                        differences(e + 1)
                    dve.wait_ge(expo_out, u * E + e + 1)
                    x = expo[:, e % 2]
                    if e < len(HG_LEVELS):
                        m = HG_LEVELS[e]
                        xq, xk, _ = sides(m, x, d)
                        zq, zk, _ = sides(m, z[:, e], d)
                        own(nc.vector.tensor_tensor(zq, xq, sides(m, q, d)[0], ALU.mult))
                        own(nc.vector.tensor_tensor(zk, xk, sides(m, k, d)[1], ALU.mult))
                        if e == len(HG_LEVELS) - 1:
                            own.settle()
                            dve.sem_inc(z_ready, 1)
                    elif e == len(HG_LEVELS):
                        own(nc.vector.tensor_tensor(q_dec[:], x, q, ALU.mult))
                        own(nc.vector.tensor_copy(last_dec[:].unsqueeze(2),
                                                  x.rearrange("p (n t) -> p n t", t=P)[:, :, 0:1] if d else
                                                  x.rearrange("p (n t) -> p n t", t=P)[:, :, P - 1:P]))
                    else:
                        own(nc.vector.tensor_tensor(k_dec[:], x, k, ALU.mult))
                        own.settle()
                        dve.sem_inc(dec_ready, 1)

                def mask_pairs(i, u=u):
                    n = u * NC + i
                    dve.wait_ge(gram_ready, n + 1)
                    if n >= 2:
                        dve.wait_ge(out_ready, n - 1)
                    nc.vector.tensor_tensor(pairs[:, n % 2], ps[:, GRAM + (n % 2) * 1024:GRAM + (n % 2) * 1024 + 1024],
                                            masks[:], ALU.mult).then_inc(pairs_ready, 1)

                dve.wait_ge(mask_loaded, 16 * (u + 1))
                mask_pairs(0)
                for i, ch in enumerate(orders[d]):
                    n = u * NC + i
                    if i + 1 < NC:
                        mask_pairs(i + 1)
                    dve.wait_ge(update_ready, n + 1)
                    if i >= 1:
                        dve.wait_ge(state_ready, n)
                    if i == 0:
                        nc.vector.tensor_copy(state[:, i % 2], ps[:, UPD:UPD + P]).then_inc(state_ready, 1)
                    else:
                        nc.vector.scalar_tensor_tensor(out=state[:, i % 2], in0=state[:, 1 - i % 2],
                                                       scalar=last_dec[:, ch:ch + 1], in1=ps[:, UPD:UPD + P],
                                                       op0=ALU.mult, op1=ALU.add).then_inc(state_ready, 1)
                    if d == 1:
                        dve.wait_ge(out_ready, n + 1)
                        out = y_t[:, 4 + h, ch * P:(ch + 1) * P]
                        nc.vector.tensor_tensor(out, out, ps[:, OUT:OUT + P], ALU.add).then_inc(out_kept, 1)

        @block.tensor
        def _(pe):
            for u, (d, h) in enumerate(units):
                unit = d * 4 + h
                pe.wait_ge(dec_ready, u + 1)
                if u:
                    pe.wait_ge(k_tok_ready, u)
                for c in range(NC):
                    last = nc.tensor.transpose(ps[:, TURN + c * P:TURN + (c + 1) * P], k_dec[:, c * P:(c + 1) * P],
                                               g.ident[:])
                last.then_inc(k_turned, 1)

                def gram(i, u=u, d=d, h=h, unit=unit):
                    n = u * NC + i
                    t = slice(orders[d][i] * P, (orders[d][i] + 1) * P)
                    at = GRAM + (n % 2) * 1024
                    if n >= 2:
                        pe.wait_ge(pairs_ready, n - 1)
                    for e in range(len(HG_LEVELS)):
                        nc.tensor.matmul(ps[:, at + e * P:at + (e + 1) * P], z[:, e, t], z[:, e, t],
                                         start=True, stop=True)
                    e = NL - 1
                    nc.tensor.matmul(ps[:, at + e * P:at + (e + 1) * P], keep_k[:, unit, t], hg[:, 0, h, t],
                                     start=True, stop=True).then_inc(gram_ready, 1)

                pe.wait_ge(z_ready, u + 1)
                gram(0)
                pe.wait_ge(k_tok_ready, u + 1)
                for i, c in enumerate(orders[d]):
                    n = u * NC + i
                    if i + 1 < NC:
                        gram(i + 1)
                    v = hg_v[:, c, h * P:(h + 1) * P]
                    if n:
                        pe.wait_ge(state_ready, n)
                    nc.tensor.matmul(ps[:, UPD:UPD + P], k_tok[:, c * P:(c + 1) * P], v, start=True, stop=True)\
                        .then_inc(update_ready, 1)
                    pe.wait_ge(pairs_ready, n + 1)
                    if n:
                        pe.wait_ge(out_kept, n)
                    if i:
                        nc.tensor.matmul(ps[:, OUT:OUT + P], state[:, 1 - i % 2], q_dec[:, c * P:(c + 1) * P],
                                         start=True, stop=False)
                    for e in range(NL):
                        last = nc.tensor.matmul(ps[:, OUT:OUT + P], v, pairs[:, n % 2, e * P:(e + 1) * P],
                                                start=(i == 0 and e == 0), stop=(e == NL - 1))
                    last.then_inc(out_ready, 1)


def stage_hgrn2_readout(nc, g, hg, y_t):
    with ExitStack() as stack:
        a = Arena(nc, stack)
        sq = a.sb("sq", [P, HG_HEADS, T])
        silu = a.sb("silu", [P, HG_HEADS, T])
        rstd = a.sb("rstd", [P, 2, T])
        squared, summed, root_in, rooted, silu_ready, own_v, slot_free = a.sem(
            "squared", "summed", "root_in", "rooted", "silu_ready", "own_v", "slot_free")
        block = a.block()
        ps = g.ps
        gain = g.vec[:, VEC["onorm"][0]:VEC["onorm"][0] + 1]

        @block.scalar
        def _(act):
            for h in range(HG_HEADS):
                nc.scalar.activation(sq[:, h], y_t[:, 4 + h], ACT.Square).then_inc(squared, 1)
            nc.scalar.activation(silu[:], hg[:, 3], ACT.Silu).then_inc(silu_ready, 1)
            for h in range(HG_HEADS):
                act.wait_ge(root_in, h + 1)
                nc.scalar.activation(rstd[:, h % 2], rstd[:, h % 2], ACT.Sqrt).then_inc(rooted, 1)

        @block.tensor
        def _(pe):
            for h in range(HG_HEADS):
                pe.wait_ge(squared, h + 1)
                for lo, hi in halves(T):
                    last = nc.tensor.matmul(ps[:, h * 1024 + lo:h * 1024 + hi], g.ones_d[:], sq[:, h, lo:hi],
                                            start=True, stop=True)
                last.then_inc(summed, 1)

        @block.vector
        def _(dve):
            own = Steps(dve, own_v)
            dve.wait_ge(silu_ready, 1)
            for h in range(HG_HEADS):
                dve.wait_ge(summed, h + 1)
                own.settle()
                nc.vector.tensor_scalar(rstd[:, h % 2], ps[:, h * 1024:h * 1024 + T], float(D // P), EPS,
                                        ALU.mult, ALU.add).then_inc(root_in, 1)
                dve.wait_ge(rooted, h + 1)
                own(nc.vector.reciprocal(rstd[:, h % 2], rstd[:, h % 2]))
                own.settle()
                own(nc.vector.scalar_tensor_tensor(out=y_t[:, 4 + h], in0=y_t[:, 4 + h], scalar=gain,
                                                   in1=rstd[:, h % 2], op0=ALU.mult, op1=ALU.mult))
                own.settle()
                own(nc.vector.tensor_tensor(y_t[:, 4 + h], y_t[:, 4 + h], silu[:, h], ALU.mult))


def stage_mix_out(nc, g, layer, y_t, t0, w_rows):
    n = T - t0
    with ExitStack() as stack:
        a = Arena(nc, stack)
        w = a.sb("w_out", [P, DK, D])
        loaded, summed, kept = a.sem("loaded", "summed", "kept")
        block = a.block()
        ps = g.ps

        @block.sync
        def _(sp):
            for parts, k, rows in w_rows:
                sp.dma_start(w[parts, k, :], rows).then_inc(loaded, 16)

        @block.tensor
        def _(pe):
            pe.wait_ge(loaded, 16 * len(w_rows))
            for m in range(DK):
                if m >= 4:
                    pe.wait_ge(kept, m - 3)
                at = (m % 4) * 1024
                for k in range(DK):
                    for lo, hi in halves(n):
                        last = nc.tensor.matmul(ps[:, at + lo:at + hi], w[:, k, m * P:(m + 1) * P], y_t[:, k, lo:hi],
                                                start=(k == 0), stop=(k == DK - 1))
                last.then_inc(summed, 1)

        @block.vector
        def _(dve):
            for m in range(DK):
                dve.wait_ge(summed, m + 1)
                at = (m % 4) * 1024
                for s, b, e in STREAMS:
                    if e > t0:
                        b = max(b, t0)
                        last = nc.vector.scalar_tensor_tensor(
                            out=g.x_t[:, m, b:e], in0=ps[:, at + b - t0:at + e - t0],
                            scalar=g.mod[:, layer, 16 + m, s:s + 1], in1=g.x_t[:, m, b:e],
                            op0=ALU.mult, op1=ALU.add)
                last.then_inc(kept, 1)


TB = 64


def stage_split(nc, g, h_t, hi, lo):
    with ExitStack() as stack:
        a = Arena(nc, stack)
        rounded = a.sem("rounded")
        block = a.block()

        @block.scalar
        def _(act):
            for k in range(DK):
                nc.scalar.copy(hi[:, k], h_t[:, k]).then_inc(rounded, 1)

        @block.vector
        def _(dve):
            for k in range(DK):
                dve.wait_ge(rounded, k + 1)
                nc.vector.tensor_tensor(lo[:, k], h_t[:, k], hi[:, k].bitcast(F32), ALU.subtract)


def stage_route(nc, g, layer, q_t, slots, n):
    NT, G2 = n // P, 2 * PEER_H
    with ExitStack() as stack:
        a = Arena(nc, stack)
        keys = a.sb("keys", [P, G2, P])
        keys_t = a.sb("keys_t", [P, G2, P])
        score = a.sb("score", [P, 2, G2, P])
        rest = a.sb("rest", [P, G2, P])
        best = a.sb("best", [P, G2, TOPK])
        best_at = a.sb("best_at", [P, G2, TOPK], U32)
        best_key = a.sb("best_key", [P, G2, TOPK])
        cand = a.sb("cand", [P, PEER_H, TOPK * TOPK])
        cand_rest = rest[:].rearrange("p (h s) n -> p h (s n)", s=2)
        top = a.sb("top", [P, PEER_H, TOPK])
        top_at = a.sb("top_at", [P, PEER_H, TOPK], U32)
        pick = a.sb("pick", [P, 2, SLOTS], U32)
        pick_f = a.sb("pick_f", [P, 2, SLOTS])
        total = a.sb("total", [P, PEER_H, 1])
        found = a.sb("found", [P, 3, SLOTS])
        iota16 = a.sb("iota16", [P, TOPK])
        hot = a.sb("hot", [P, 2, SLOTS, TOPK])
        loaded, keys_turned, keys_ready, scored, score_ready, score_used, soft_in, soft_out, found_ready, turned, \
            found_used, own_v = a.sem("loaded", "keys_turned", "keys_ready", "scored", "score_ready", "score_used",
                                      "soft_in", "soft_out", "found_ready", "turned", "found_used", "own_v")
        block = a.block()
        ps = g.ps
        TURN = 4 * BANK

        @block.sync
        def _(sp):
            sp.dma_start(keys[:], g.d["peer_keys"][layer].rearrange("h s n k -> n (h s) k")).then_inc(loaded, 16)
            sp.dma_start(iota16[:], g.d["k_iota"][:, 0:TOPK]).then_inc(loaded, 16)

        @block.tensor
        def _(pe):
            pe.wait_ge(loaded, 32)
            for i in range(G2):
                last = nc.tensor.transpose(ps[:, i * P:(i + 1) * P], keys[:, i], g.ident[:])
            last.then_inc(keys_turned, 1)

            def turn(t):
                pe.wait_ge(found_ready, t + 1)
                if t:
                    pe.wait_ge(found_used, t)
                for i in range(3):
                    last = nc.tensor.transpose(ps[:, TURN + i * P:TURN + (i + 1) * P], found[:, i], g.ident[:])
                last.then_inc(turned, 1)

            pe.wait_ge(keys_ready, 1)
            for t in range(NT):
                if t:
                    pe.wait_ge(score_ready, t)
                for i in range(G2):
                    last = nc.tensor.matmul(ps[:, i * P:(i + 1) * P], q_t[:, i, t * P:(t + 1) * P], keys_t[:, i],
                                            start=True, stop=True)
                last.then_inc(scored, 1)
                if t:
                    turn(t - 1)
            turn(NT - 1)

        @block.scalar
        def _(act):
            act.wait_ge(keys_turned, 1)
            nc.scalar.copy(keys_t[:], ps[:, 0:4 * BANK].rearrange("p (g n) -> p g n", n=P)).then_inc(keys_ready, 1)

            def scores_out(t):
                act.wait_ge(scored, t + 1)
                if t >= 2:
                    act.wait_ge(score_used, t - 1)
                nc.scalar.copy(score[:, t % 2], ps[:, 0:4 * BANK].rearrange("p (g n) -> p g n", n=P))\
                    .then_inc(score_ready, 1)

            scores_out(0)
            for t in range(NT):
                if t + 1 < NT:
                    scores_out(t + 1)
                act.wait_ge(soft_in, t + 1)
                nc.scalar.activation(top[:], top[:], ACT.Exp).then_inc(soft_out, 1)
                act.wait_ge(turned, t + 1)
                nc.scalar.copy(slots[:, :, t * P:(t + 1) * P],
                               ps[:, TURN:TURN + 3 * P].rearrange("p (i t) -> p i t", t=P)).then_inc(found_used, 1)

        @block.vector
        def _(dve):
            own = Steps(dve, own_v)

            def sixteen(values, without, out, at, groups):
                for i in range(groups):
                    own(nc.vector.max(out[:, i, 0:8], values[:, i]))
                own.settle()
                for i in range(groups):
                    own(nc.vector.match_replace(without[:, i], out[:, i, 0:8], values[:, i], LOWEST))
                    own(nc.vector.max_index(at[:, i, 0:8], out[:, i, 0:8], values[:, i]))
                own.settle()
                for i in range(groups):
                    own(nc.vector.max(out[:, i, 8:16], without[:, i]))
                own.settle()
                for i in range(groups):
                    own(nc.vector.max_index(at[:, i, 8:16], out[:, i, 8:16], without[:, i]))
                own.settle()

            dve.wait_ge(loaded, 32)
            for t in range(NT):
                dve.wait_ge(score_ready, t + 1)
                sixteen(score[:, t % 2], rest, best, best_at, G2)
                dve.sem_inc(score_used, 1)
                own(nc.vector.tensor_copy(best_key[:], best_at[:]))
                halves_of = best[:].rearrange("p (h s) k -> p h s k", s=2)
                own(nc.vector.tensor_tensor(cand[:].rearrange("p h (a b) -> p h a b", a=TOPK),
                                            halves_of[:, :, 0, :].unsqueeze(3).to_broadcast([P, PEER_H, TOPK, TOPK]),
                                            halves_of[:, :, 1, :].unsqueeze(2).to_broadcast([P, PEER_H, TOPK, TOPK]),
                                            ALU.add))
                own.settle()
                sixteen(cand, cand_rest, top, top_at, PEER_H)
                nc.vector.tensor_tensor(cand_rest[:, :, 0:TOPK], top[:], top[:, :, 0:1].to_broadcast([P, PEER_H, TOPK]),
                                        ALU.subtract).then_inc(own_v, 1)
                own.n += 1
                at = top_at[:].rearrange("p h k -> p (h k)")
                own(nc.vector.tensor_scalar(pick[:, 0], at, 4, None, ALU.logical_shift_right))
                own(nc.vector.tensor_scalar(pick[:, 1], at, 15, None, ALU.bitwise_and))
                own.settle()
                nc.vector.tensor_copy(top[:], cand_rest[:, :, 0:TOPK]).then_inc(soft_in, 1)
                own(nc.vector.tensor_copy(pick_f[:], pick[:]))
                own.settle()
                for i in range(2):
                    own(nc.vector.tensor_tensor(hot[:, i], pick_f[:, i].unsqueeze(2).to_broadcast([P, SLOTS, TOPK]),
                                                iota16[:].unsqueeze(1).to_broadcast([P, SLOTS, TOPK]), ALU.is_equal))
                own.settle()
                keys_of = best_key[:].rearrange("p (h s) k -> p h s k", s=2)
                for i in range(2):
                    h4 = hot[:, i].rearrange("p (h k) a -> p h k a", h=PEER_H)
                    own(nc.vector.tensor_tensor(h4, h4, keys_of[:, :, i, :].unsqueeze(2)
                                                .to_broadcast([P, PEER_H, TOPK, TOPK]), ALU.mult))
                own.settle()
                if t:
                    dve.wait_ge(turned, t)
                for i in range(2):
                    own(nc.vector.tensor_reduce(found[:, i], hot[:, i], AX.X, ALU.add))
                dve.wait_ge(soft_out, t + 1)
                own(nc.vector.tensor_reduce(total[:, :, 0], top[:], AX.X, ALU.add))
                own.settle()
                own(nc.vector.reciprocal(total[:], total[:]))
                own.settle()
                own(nc.vector.tensor_tensor(found[:, 2].rearrange("p (h k) -> p h k", h=PEER_H), top[:],
                                            total[:].to_broadcast([P, PEER_H, TOPK]), ALU.mult))
                own.settle()
                dve.sem_inc(found_ready, 1)


def stage_gate_table(nc, g, slots, table, n):
    QUAD = 4
    TURNS = TB // (2 * QUAD)
    with ExitStack() as stack:
        a = Arena(nc, stack)
        iota = a.sb("iota", [P, P])
        first_hot = a.sb("first_hot", [P, 2, QUAD, P])
        second_hot = a.sb("second_hot", [P, 2, QUAD, P])
        part = a.sb("part", [P, 2, P, TB])
        loaded = a.sem("loaded")
        hot_ready = [a.sem(f"hot_ready{b}") for b in range(2)]
        multiplied = [a.sem(f"multiplied{b}") for b in range(2)]
        kept = [a.sem(f"kept{b}") for b in range(2)]
        stored = [a.sem(f"stored{b}") for b in range(2)]
        block = a.block()
        ps = g.ps

        @block.sync
        def _(sp):
            sp.dma_start(iota[:], g.d["k_iota"]).then_inc(loaded, 16)
            with sp.Fori(0, n // TB // 2) as i:
                for r in range(2):
                    sp.wait_ge(kept[0], (i * 2 + r + 1) * TURNS)
                    sp.wait_ge(kept[1], (i * 2 + r + 1) * TURNS)
                    sp.dma_start(table[:, bass.ds(i * 2 + r, 1)], part[:, r:r + 1]).then_inc(stored[r], 16)
            for r in range(2):
                sp.wait_ge(stored[r], 16 * (n // TB // 2))

        @block.vector
        def _(dve):
            dve.wait_ge(loaded, 16)

            def octet(i, first):
                for b in range(2):
                    if not first:
                        dve.wait_ge(multiplied[b], i)
                    for q in range(QUAD):
                        t = i * (2 * QUAD) + (b * QUAD + q)
                        nc.vector.tensor_scalar(first_hot[:, b, q], iota[:], slots[:, 0, bass.ds(t, 1)], None,
                                                ALU.is_equal)
                        last = nc.vector.tensor_scalar(second_hot[:, b, q], iota[:], slots[:, 1, bass.ds(t, 1)],
                                                       slots[:, 2, bass.ds(t, 1)], ALU.is_equal, ALU.mult)
                    last.then_inc(hot_ready[b], 1)

            octet(0, True)
            with dve.Fori(1, n // (2 * QUAD)) as i:
                octet(i, False)

        @block.tensor
        def _(pe):
            def octet(i, first):
                for b in range(2):
                    pe.wait_ge(hot_ready[b], i + 1)
                    if not first:
                        pe.wait_ge(kept[b], i)
                    for q in range(QUAD):
                        last = nc.tensor.matmul(ps[:, b * BANK + q * P:b * BANK + (q + 1) * P], first_hot[:, b, q],
                                                second_hot[:, b, q], start=True, stop=True)
                    last.then_inc(multiplied[b], 1)

            octet(0, True)
            with pe.Fori(1, n // (2 * QUAD)) as i:
                octet(i, False)

        @block.scalar
        def _(act):
            def pair(i, first):
                for r in range(2):
                    if not first:
                        act.wait_ge(stored[r], i * 16)
                    with act.Fori(0, TURNS) as j:
                        for b in range(2):
                            act.wait_ge(multiplied[b], (i * 2 + r) * TURNS + j + 1)
                            nc.scalar.copy(part[:, r, :, bass.ds(j * (2 * QUAD) + b * QUAD, QUAD)],
                                           ps[:, b * BANK:(b + 1) * BANK].rearrange("p (t m) -> p m t", m=P))\
                                .then_inc(kept[b], 1)

            pair(0, True)
            with act.Fori(1, n // TB // 2) as i:
                pair(i, False)


def stage_experts(nc, g, layer, hi, lo, table, n, spans):
    BODIES = KEYS // 4
    tables = [g.d[name][layer].rearrange("(a b) d -> a b d", b=KEYS) for name in ("peer_u", "peer_v")]
    Y_UNITS = [(m, s) for m in range(DK) for s in range(len(spans))]
    PER_BANK = len(Y_UNITS) // 2
    with ExitStack() as stack:
        a = Arena(nc, stack)
        u_raw = a.sb("u_raw", [P, 2, D])
        v_raw = a.sb("v_raw", [P, 2, D])
        u_hi = a.sb("u_hi", [P, 2, DK, P], F32R)
        u_lo = a.sb("u_lo", [P, 2, DK, P], F32R)
        v_hi = a.sb("v_hi", [P, 4, D], F32R)
        v_lo = a.sb("v_lo", [P, 4, D], F32R)
        gates = a.sb("gates", [P, 2, n // TB, 2, TB])
        acts = a.sb("acts", [P, 2, n])
        w_hi = a.sb("w_hi", [P, 4, n], F32R)
        w_lo = a.sb("w_lo", [P, 4, n], F32R)

        def four(name):
            return [a.sem(f"{name}{r}") for r in range(4)]

        u_loaded, v_loaded, turned, u_hi_ready, u_lo_ready = map(four, ("u_loaded", "v_loaded", "turned", "u_hi_ready",
                                                                        "u_lo_ready"))
        acted, gelued, weighted, w_hi_ready, w_lo_ready = map(four, ("acted", "gelued", "weighted", "w_hi_ready",
                                                                     "w_lo_ready"))
        v_hi_ready, v_lo_ready = map(four, ("v_hi_ready", "v_lo_ready"))
        gates_loaded = [a.sem(f"gates_loaded{q}") for q in range(2)]
        y_done = [a.sem(f"y_done{b}") for b in range(2)]
        y_added = [a.sem(f"y_added{b}") for b in range(2)]
        block = a.block()
        ps = g.ps
        TURN, ACTS, Y = 0, 2 * BANK, 6 * BANK

        def former(r, back, body):
            return ((r - back, body + 1) if r >= back else (r - back + 4, body))

        def bodies(engine, emit):
            emit(0, True, False)
            with engine.Fori(1, BODIES - 1) as i:
                emit(i, False, False)
            emit(BODIES - 1, False, True)

        @block.sync
        def _(sp):
            def body(i, first, last):
                for r in range(4):
                    step = i * 4 + r
                    s, count = former(r, 2, i)
                    if not (first and r < 2):
                        sp.wait_ge(turned[s], count)
                    sp.dma_start(u_raw[:, r % 2:r % 2 + 1], tables[0][:, bass.ds(step, 1), :]).then_inc(u_loaded[r], 16)
                    if r % 2 == 0:
                        q = r // 2
                        if not first:
                            sp.wait_ge(weighted[r], i)
                            sp.wait_ge(weighted[r + 1], i)
                        sp.dma_start(gates[:, q], table[:, :, bass.ds(step, 2), :]).then_inc(gates_loaded[q], 16)
                    if not (first and r < 2):
                        sp.wait_ge(v_lo_ready[s], count)
                    sp.dma_start(v_raw[:, r % 2:r % 2 + 1], tables[1][:, bass.ds(step, 1), :]).then_inc(v_loaded[r], 16)

            bodies(sp, body)

        @block.tensor
        def _(pe):
            def turn(r, i, first):
                if r == 4:
                    r, i = 0, i + 1
                pe.wait_ge(u_loaded[r], (i + 1) * 16)
                if not (first and r == 0):
                    s, count = former(r, 1, i)
                    pe.wait_ge(u_lo_ready[s], count)
                for k in range(DK):
                    last = nc.tensor.transpose(ps[:, TURN + k * P:TURN + (k + 1) * P],
                                               u_raw[:, r % 2, k * P:(k + 1) * P], g.ident[:])
                last.then_inc(turned[r], 1)

            def act_products(r, i, first):
                at = ACTS + (r % 2) * 1024
                pe.wait_ge(u_lo_ready[r], i + 1)
                if not (first and r < 2):
                    s, count = former(r, 2, i)
                    pe.wait_ge(gelued[s], count)
                for k in range(DK):
                    for w, h in ((u_hi, hi), (u_hi, lo), (u_lo, hi)):
                        for b, e, _, _ in spans:
                            last = nc.tensor.matmul(ps[:, at + b:at + e], w[:, r % 2, k], h[:, k, b:e],
                                                    start=(k == 0 and w is u_hi and h is hi),
                                                    stop=(k == DK - 1 and w is u_lo))
                last.then_inc(acted[r], 1)

            def mix(q, i, first):
                for r in (2 * q, 2 * q + 1):
                    pe.wait_ge(w_lo_ready[r], i + 1)
                    pe.wait_ge(v_lo_ready[r], i + 1)
                for c, (m, s) in enumerate(Y_UNITS):
                    b, e, _, _ = spans[s]
                    at = Y + (c % 2) * BANK
                    done = i * (2 * PER_BANK) + (q * PER_BANK + c // 2)
                    if not (first and q == 0 and c < 2):
                        pe.wait_ge(y_added[c % 2], done)
                    for r in (2 * q, 2 * q + 1):
                        for v, w in ((v_hi, w_hi), (v_hi, w_lo), (v_lo, w_hi)):
                            last = nc.tensor.matmul(ps[:, at:at + e - b], v[:, r, m * P:(m + 1) * P], w[:, r, b:e],
                                                    start=(r == 2 * q and v is v_hi and w is w_hi),
                                                    stop=(r == 2 * q + 1 and v is v_lo))
                    last.then_inc(y_done[c % 2], 1)

            def body(i, first, last):
                turn(1, i, False)
                act_products(0, i, first)
                turn(2, i, False)
                act_products(1, i, first)
                if not first:
                    mix(1, i - 1, False)
                turn(3, i, False)
                act_products(2, i, first)
                if not last:
                    turn(4, i, False)
                act_products(3, i, first)
                mix(0, i, first)
                if last:
                    mix(1, i, False)

            turn(0, 0, True)
            bodies(pe, body)

        @block.scalar
        def _(act):
            def round_u(r, i, first):
                act.wait_ge(turned[r], i + 1)
                if not (first and r < 2):
                    s, count = former(r, 2, i)
                    act.wait_ge(acted[s], count)
                nc.scalar.copy(u_hi[:, r % 2].rearrange("p k n -> p (k n)"), ps[:, TURN:TURN + D])\
                    .then_inc(u_hi_ready[r], 1)

            def gelu(r, i, first):
                act.wait_ge(acted[r], i + 1)
                if not (first and r < 2):
                    s, count = former(r, 2, i)
                    act.wait_ge(w_lo_ready[s], count)
                at = ACTS + (r % 2) * 1024
                nc.scalar.activation(acts[:, r % 2], ps[:, at:at + n], ACT.Gelu).then_inc(gelued[r], 1)

            def round_v(r, i, first):
                act.wait_ge(v_loaded[r], (i + 1) * 16)
                if not first:
                    act.wait_ge(y_done[1], i * (2 * PER_BANK) + (r // 2 + 1) * PER_BANK - 2 * PER_BANK)
                nc.scalar.copy(v_hi[:, r], v_raw[:, r % 2]).then_inc(v_hi_ready[r], 1)

            def body(i, first, last):
                for r in range(4):
                    if r < 3:
                        round_u(r + 1, i, first)
                    elif not last:
                        round_u(0, i + 1, False)
                    round_v(r, i, first)
                    gelu(r, i, first)

            round_u(0, 0, True)
            bodies(act, body)

        @block.vector
        def _(dve):
            def split_u(r, i, first):
                dve.wait_ge(u_hi_ready[r], i + 1)
                nc.vector.tensor_tensor(u_lo[:, r % 2].rearrange("p k n -> p (k n)"), ps[:, TURN:TURN + D],
                                        u_hi[:, r % 2].rearrange("p k n -> p (k n)").bitcast(F32), ALU.subtract)\
                    .then_inc(u_lo_ready[r], 1)

            def weigh(r, i, first):
                q = r // 2
                dve.wait_ge(gelued[r], i + 1)
                dve.wait_ge(gates_loaded[q], (i + 1) * 16)
                x = acts[:, r % 2]
                x3 = x.rearrange("p (b t) -> p b t", t=TB)
                nc.vector.tensor_tensor(x3, x3, gates[:, q, :, r % 2, :], ALU.mult).then_inc(weighted[r], 1)
                if not first:
                    dve.wait_ge(y_done[1], i * (2 * PER_BANK) + (q + 1) * PER_BANK - 2 * PER_BANK)
                dve.wait_ge(weighted[r], i + 1)
                nc.vector.tensor_copy(w_hi[:, r], x).then_inc(w_hi_ready[r], 1)
                dve.wait_ge(w_hi_ready[r], i + 1)
                nc.vector.tensor_tensor(w_lo[:, r], x, w_hi[:, r].bitcast(F32), ALU.subtract)\
                    .then_inc(w_lo_ready[r], 1)

            def add(q, i):
                for c, (m, s) in enumerate(Y_UNITS):
                    b, e, t, stream = spans[s]
                    dve.wait_ge(y_done[c % 2], i * (2 * PER_BANK) + (q * PER_BANK + c // 2 + 1))
                    x = g.x_t[:, m, t:t + e - b]
                    at = Y + (c % 2) * BANK
                    nc.vector.scalar_tensor_tensor(out=x, in0=ps[:, at:at + e - b],
                                                   scalar=g.mod[:, layer, 40 + m, stream:stream + 1], in1=x,
                                                   op0=ALU.mult, op1=ALU.add).then_inc(y_added[c % 2], 1)

            def body(i, first, last):
                split_u(1, i, first)
                weigh(0, i, first)
                split_u(2, i, first)
                weigh(1, i, first)
                if not first:
                    add(1, i - 1)
                split_u(3, i, first)
                weigh(2, i, first)
                if not last:
                    split_u(0, i + 1, first)
                weigh(3, i, first)
                add(0, i)
                if last:
                    add(1, i)

            split_u(0, 0, True)
            bodies(dve, body)

        @block.gpsimd
        def _(pool):
            def body(i, first, last):
                for r in range(4):
                    pool.wait_ge(v_hi_ready[r], i + 1)
                    nc.gpsimd.tensor_tensor(v_lo[:, r], v_raw[:, r % 2], v_hi[:, r].bitcast(F32), ALU.subtract)\
                        .then_inc(v_lo_ready[r], 1)

            bodies(pool, body)


def stage_rms_channels(nc, g, x, kc, gain, factor=1.0):
    n = x.shape[2]
    with ExitStack() as stack:
        a = Arena(nc, stack)
        sq = a.sb("sq", [P, kc, n])
        rstd = a.sb("rstd", [P, n])
        squared, summed, root_in, rooted, own_v = a.sem("squared", "summed", "root_in", "rooted", "own_v")
        block = a.block()
        ps = g.ps

        @block.scalar
        def _(act):
            for k in range(kc):
                nc.scalar.activation(sq[:, k], x[:, k], ACT.Square).then_inc(squared, 1)
            act.wait_ge(root_in, 1)
            nc.scalar.activation(rstd[:], rstd[:], ACT.Sqrt).then_inc(rooted, 1)

        @block.tensor
        def _(pe):
            for k in range(kc):
                pe.wait_ge(squared, k + 1)
                for lo, hi in halves(n):
                    last = nc.tensor.matmul(ps[:, lo:hi], g.ones_d[:], sq[:, k, lo:hi],
                                            start=(k == 0), stop=(k == kc - 1))
            last.then_inc(summed, 1)

        @block.vector
        def _(dve):
            own = Steps(dve, own_v)
            dve.wait_ge(summed, 1)
            nc.vector.tensor_scalar(rstd[:], ps[:, 0:n], D / (kc * P), EPS, ALU.mult, ALU.add).then_inc(root_in, 1)
            dve.wait_ge(rooted, 1)
            own(nc.vector.reciprocal(rstd[:], rstd[:]))
            own.settle()
            if factor != 1.0:
                own(nc.vector.tensor_scalar(rstd[:], rstd[:], factor, None, ALU.mult))
                own.settle()
            for k in range(kc):
                own(nc.vector.scalar_tensor_tensor(out=x[:, k], in0=x[:, k], scalar=gain[:, k:k + 1], in1=rstd[:],
                                                   op0=ALU.mult, op1=ALU.mult))


def stage_mla_heads(nc, g, q_a, kv_a, k_rope, q_t, k_t, v_tok):
    QH, KH = MLA_NOPE + MLA_ROPE, MLA_NOPE + MLA_V
    NQ, NK = MLA_QR // P, MLA_KVR // P
    with ExitStack() as stack:
        a = Arena(nc, stack)
        w_q = a.sb("w_qup", [P, NQ, MLA_H * QH])
        w_kv = a.sb("w_kvup", [P, NK, MLA_H * KH])
        q_rope = a.sb("q_rope", [MLA_ROPE, MLA_H, LAT])
        rope = a.sb("rope", [MLA_ROPE, 2, LAT])
        swap = a.sb("swap", [MLA_ROPE, MLA_ROPE])
        direct_cos = a.sb("direct_cos", [MLA_ROPE, 2, LAT])
        swapped_sin = a.sb("swapped_sin", [MLA_ROPE, 2, LAT])
        k_turned = a.sb("k_turned", [MLA_ROPE, T])
        loaded, product, kept, swapped, swap_free, k_ready, own_v = a.sem(
            "loaded", "product", "kept", "swapped", "swap_free", "k_ready", "own_v")
        block = a.block()
        ps = g.ps
        SWAP = 6 * BANK
        units = []
        for h in range(MLA_H):
            units.append(([(w_q[:, k, h * QH:h * QH + 64], q_a[:, k, :]) for k in range(NQ)], 64, LAT,
                          q_t[0:64, h, :]))
            units.append(([(w_q[:, k, h * QH + 64:(h + 1) * QH], q_a[:, k, :]) for k in range(NQ)], MLA_ROPE, LAT,
                          q_rope[:, h, :]))
            units.append(([(w_kv[:, k, h * KH:h * KH + 64], kv_a[:, k, :]) for k in range(NK)], 64, T,
                          k_t[0:64, h, :]))
        for t in range(T // P):
            values = [w_kv[:, k].rearrange("p (h c) -> p h c", c=KH)[:, :, MLA_NOPE:] for k in range(NK)]
            units.append(([(kv_a[:, k, t * P:(t + 1) * P], values[k]) for k in range(NK)], P, 512, v_tok[:, t, :]))

        @block.sync
        def _(sp):
            sp.dma_start(w_q[:], g.d["mla_w_qup"][0].rearrange("(k p) n -> p k n", p=P)).then_inc(loaded, 16)
            sp.dma_start(w_kv[:], g.d["mla_w_kvup"][0].rearrange("(k p) n -> p k n", p=P)).then_inc(loaded, 16)
            sp.dma_start(rope[:], g.d["k_rope_mla"]).then_inc(loaded, 16)
            sp.dma_start(swap[:], g.d["k_rope_swap"]).then_inc(loaded, 16)

        @block.tensor
        def _(pe):
            pe.wait_ge(loaded, 64)
            for u, (pairs, m, n, _) in enumerate(units):
                at = (u % 3) * 1024
                if u >= 3:
                    pe.wait_ge(kept, u - 2)
                for i, (left, right) in enumerate(pairs):
                    if len(right.shape) == 3:
                        last = nc.tensor.matmul(ps[0:m, at:at + n], left, right, start=(i == 0),
                                                stop=(i == len(pairs) - 1))
                    else:
                        for lo, hi in halves(n):
                            last = nc.tensor.matmul(ps[0:m, at + lo:at + hi], left, right[:, lo:hi], start=(i == 0),
                                                    stop=(i == len(pairs) - 1))
                last.then_inc(product, 1)
            pe.wait_ge(kept, len(units))
            for h in range(MLA_H + 1):
                if h >= 2:
                    pe.wait_ge(swap_free, h - 1)
                x = q_rope[:, h, :] if h < MLA_H else k_rope[:, CTX:T]
                nc.tensor.matmul(ps[0:MLA_ROPE, SWAP + (h % 2) * BANK:SWAP + (h % 2 + 1) * BANK], swap[:], x,
                                 start=True, stop=True).then_inc(swapped, 1)

        @block.scalar
        def _(act):
            for u, (pairs, m, n, out) in enumerate(units):
                act.wait_ge(product, u + 1)
                nc.scalar.copy(out, ps[0:m, (u % 3) * 1024:(u % 3) * 1024 + n]).then_inc(kept, 1)
            act.wait_ge(k_ready, 1)
            for h in range(MLA_H):
                nc.scalar.copy(k_t[64:96, h, :], k_turned[:])

        @block.vector
        def _(dve):
            own = Steps(dve, own_v)
            dve.wait_ge(kept, len(units))
            dve.wait_ge(loaded, 64)
            for h in range(MLA_H + 1):
                x = q_rope[:, h, :] if h < MLA_H else k_rope[:, CTX:T]
                out = q_t[64:96, h, :] if h < MLA_H else k_turned[:, CTX:T]
                own(nc.vector.tensor_tensor(direct_cos[:, h % 2], x, rope[:, 0], ALU.mult))
                dve.wait_ge(swapped, h + 1)
                nc.vector.tensor_tensor(swapped_sin[:, h % 2], rope[:, 1],
                                        ps[0:MLA_ROPE, SWAP + (h % 2) * BANK:SWAP + (h % 2 + 1) * BANK],
                                        ALU.mult).then_inc(swap_free, 1)
                dve.wait_ge(swap_free, h + 1)
                own.settle()
                own(nc.vector.tensor_tensor(out, direct_cos[:, h % 2], swapped_sin[:, h % 2], ALU.add))
            own(nc.vector.tensor_copy(k_turned[:, 0:CTX], k_rope[:, 0:CTX]))
            own.settle()
            dve.sem_inc(k_ready, 1)


S5_TILES = S5_G // 2
TWO_PI = 6.283185
ROUND = 1.5 * 2.0 ** 23


def stage_s5_parameters(nc, g, rate, turns, b_t, c_t):
    N = 2 * S5_TILES
    with ExitStack() as stack:
        a = Arena(nc, stack)
        rows = a.sb("s5_rows", [3 * N, P])
        dt_rows = a.sb("dt_rows", [3 * N, 2])
        par = a.sb("par", [P, 3, N])
        f = a.sb("s5_f", [P, 12, N])
        b_nat = a.sb("b_nat", [P, 2, N, S5_C])
        b_eff = a.sb("b_eff", [P, 2, N, S5_C])
        tmp = a.sb("tmp", [P, N, S5_C])
        c_nat = a.sb("c_nat", [P, 2, 8, S5_P])
        b_mask = a.sb("b_mask", [P, 4, 8])
        c_mask = a.sb("c_mask", [P, 8])
        padded = a.sb("padded", [P, 2, 4, P])
        loaded, spread, turned, par_ready, trig_in, trig_out, own_v, pad_ready, pad_turned, pad_kept = a.sem(
            "loaded", "spread", "turned", "par_ready", "trig_in", "trig_out", "own_v", "pad_ready", "pad_turned",
            "pad_kept")
        block = a.block()
        ps = g.ps
        jobs = [(m, part, d, j) for m in "bc" for part in range(2) for d in range(2) for j in range(4)]

        @block.sync
        def _(sp):
            d = g.d
            sp.dma_start(rows[0:N, :], d["s5_a_re"][0].rearrange("d (i g) p -> (d i) (g p)", g=2)).then_inc(loaded, 16)
            sp.dma_start(rows[N:2 * N, :], d["s5_a_im"][0].rearrange("d (i g) p -> (d i) (g p)", g=2))\
                .then_inc(loaded, 16)
            sp.dma_start(dt_rows[2 * N:3 * N, :], d["s5_log_dt"][0].rearrange("d (i g) -> (d i) g", g=2))\
                .then_inc(loaded, 16)
            sp.dma_start(b_mask[:], d["k_s5_bmask"]).then_inc(loaded, 16)
            sp.dma_start(c_mask[:], d["k_s5_cmask"]).then_inc(loaded, 16)
            for part, name in enumerate(("s5_b_re", "s5_b_im")):
                for dr in range(2):
                    src = d[name][0, dr].rearrange("(i g) p c -> (g p) i c", g=2)
                    sp.dma_start(b_nat[:, part, dr * S5_TILES:(dr + 1) * S5_TILES, :], src).then_inc(loaded, 16)
            for part, name in enumerate(("s5_c_re", "s5_c_im")):
                for dr in range(2):
                    src = d[name][0, dr].rearrange("(j g) c p -> (g c) j p", g=8)
                    sp.dma_start(c_nat[:, part, dr * 4:(dr + 1) * 4, :], src).then_inc(loaded, 16)

        n_loads = 16 * 13

        @block.tensor
        def _(pe):
            pe.wait_ge(spread, 1)
            nc.tensor.transpose(ps[:, 0:3 * N], rows[:], g.ident[:3 * N, :3 * N]).then_inc(turned, 1)
            for n in range(len(jobs)):
                pe.wait_ge(pad_ready, n + 1)
                if n >= 2:
                    pe.wait_ge(pad_kept, n - 1)
                at = (2 + n % 2) * BANK
                for i in range(4):
                    last = nc.tensor.transpose(ps[:, at + i * P:at + (i + 1) * P], padded[:, n % 2, i], g.ident[:])
                last.then_inc(pad_turned, 1)

        @block.scalar
        def _(act):
            act.wait_ge(par_ready, 1)
            nc.scalar.activation(f[:, 0], par[:, 2], ACT.Exp).then_inc(trig_out, 1)
            act.wait_ge(trig_in, 1)
            nc.scalar.activation(rate[:], f[:, 1], ACT.Exp).then_inc(trig_out, 1)
            nc.scalar.activation(f[:, 4], turns[:], ACT.Sin, scale=TWO_PI).then_inc(trig_out, 1)
            nc.scalar.activation(f[:, 5], turns[:], ACT.Sin, scale=TWO_PI / 2).then_inc(trig_out, 1)
            for n, (m, part, d, j) in enumerate(jobs):
                act.wait_ge(pad_turned, n + 1)
                src = ps[:, (2 + n % 2) * BANK:(3 + n % 2) * BANK].rearrange("p (i n) -> p i n", i=4)
                tiles = slice(d * S5_TILES + 4 * j, d * S5_TILES + 4 * j + 4)
                if m == "b":
                    nc.scalar.copy(b_t[:, part, tiles, :], src).then_inc(pad_kept, 1)
                elif part == 0:
                    nc.scalar.copy(c_t[:, 0, tiles, :], src)
                    nc.scalar.mul(c_t[:, 1, tiles, :], src, -1.0).then_inc(pad_kept, 1)
                else:
                    nc.scalar.mul(c_t[:, 2, tiles, :], src, -1.0).then_inc(pad_kept, 1)

        @block.vector
        def _(dve):
            own = Steps(dve, own_v)
            dve.wait_ge(loaded, n_loads)
            nc.vector.tensor_copy(rows[2 * N:3 * N, :].rearrange("r (g p) -> r g p", g=2),
                                  dt_rows[2 * N:3 * N, :].unsqueeze(2).to_broadcast([N, 2, S5_P])).then_inc(spread, 1)
            dve.wait_ge(turned, 1)
            nc.vector.tensor_copy(par[:], ps[:, 0:3 * N].rearrange("p (i n) -> p i n", i=3)).then_inc(par_ready, 1)
            dve.wait_ge(par_ready, 1)
            dve.wait_ge(trig_out, 1)
            lam_re, lam_im = par[:, 0], par[:, 1]
            tt, ts = nc.vector.tensor_tensor, nc.vector.tensor_scalar
            own(tt(f[:, 1], lam_re, f[:, 0], ALU.mult))
            own(tt(f[:, 2], lam_im, f[:, 0], ALU.mult))
            own.settle()
            own(ts(f[:, 2], f[:, 2], float(1 / (2 * np.pi)), None, ALU.mult))
            own.settle()
            own(ts(f[:, 3], f[:, 2], ROUND, ROUND, ALU.add, ALU.subtract))
            own.settle()
            own(tt(turns[:], f[:, 2], f[:, 3], ALU.subtract))
            own.settle()
            dve.sem_inc(trig_in, 1)
            dve.wait_ge(trig_out, 4)
            own(tt(f[:, 6], f[:, 5], f[:, 5], ALU.mult))
            own.settle()
            own(ts(f[:, 6], f[:, 6], -2.0, 1.0, ALU.mult, ALU.add))
            own(tt(f[:, 7], rate[:], f[:, 4], ALU.mult))
            own.settle()
            own(tt(f[:, 6], rate[:], f[:, 6], ALU.mult))
            own(tt(f[:, 8], lam_re, lam_re, ALU.mult))
            own(tt(f[:, 9], lam_im, lam_im, ALU.mult))
            own.settle()
            own(ts(f[:, 6], f[:, 6], 1.0, None, ALU.subtract))
            own(tt(f[:, 8], f[:, 8], f[:, 9], ALU.add))
            own.settle()
            own(nc.vector.reciprocal(f[:, 8], f[:, 8]))
            own(tt(f[:, 9], f[:, 6], lam_re, ALU.mult))
            own(tt(f[:, 10], f[:, 7], lam_im, ALU.mult))
            own(tt(f[:, 11], f[:, 7], lam_re, ALU.mult))
            own(tt(f[:, 5], f[:, 6], lam_im, ALU.mult))
            own.settle()
            own(tt(f[:, 9], f[:, 9], f[:, 10], ALU.add))
            own(tt(f[:, 11], f[:, 11], f[:, 5], ALU.subtract))
            own.settle()
            own(tt(f[:, 9], f[:, 9], f[:, 8], ALU.mult))
            own(tt(f[:, 11], f[:, 11], f[:, 8], ALU.mult))
            own.settle()
            re = f[:, 9].unsqueeze(2).to_broadcast([P, N, S5_C])
            im = f[:, 11].unsqueeze(2).to_broadcast([P, N, S5_C])
            for part, (x, y, op) in enumerate(((re, im, ALU.subtract), (im, re, ALU.add))):
                own(tt(b_eff[:, part], b_nat[:, 0], x, ALU.mult))
                own(tt(tmp[:], b_nat[:, 1], y, ALU.mult))
                own.settle()
                own(tt(b_eff[:, part], b_eff[:, part], tmp[:], op))
                own.settle()
            for n, (m, part, d, j) in enumerate(jobs):
                if n >= 2:
                    dve.wait_ge(pad_turned, n - 1)
                if m == "b":
                    tiles = slice(d * S5_TILES + 4 * j, d * S5_TILES + 4 * j + 4)
                    last = tt(padded[:, n % 2].rearrange("p i (g c) -> p i g c", g=8),
                              b_eff[:, part, tiles].unsqueeze(2).to_broadcast([P, 4, 8, S5_C]),
                              b_mask[:].unsqueeze(3).to_broadcast([P, 4, 8, S5_C]), ALU.mult)
                else:
                    last = tt(padded[:, n % 2].rearrange("p i (g s) -> p (i g) s", g=2),
                              c_nat[:, part, d * 4 + j].unsqueeze(1).to_broadcast([P, 8, S5_P]),
                              c_mask[:].unsqueeze(2).to_broadcast([P, 8, S5_P]), ALU.mult)
                last.then_inc(pad_ready, 1)


def stage_s5_scan(nc, g, u_t, rate, turns, b_t, c_t, z_t):
    units = [(j, i, d) for j in range(4) for i in range(4) for d in range(2)]
    with ExitStack() as stack:
        a = Arena(nc, stack)
        tau = a.sb("tau", [P, 2, T])
        phase = a.sb("phase", [P, 2, T])
        whole = a.sb("whole", [P, T])
        sin = a.sb("sin", [P, 2, T])
        cos = a.sb("cos", [P, 2, T])
        x2 = a.sb("x2", [P, 2, T])
        v = a.sb("v", [P, 2, T])
        s = a.sb("s", [P, 2, 2, T])
        prods = a.sb("prods", [P, 2, 4, LAT])
        (loaded, phase_ready, half_ready, sq_ready, trig_ready, bu_ready, bu_used, scanned, prods_ready, y_ready,
         y_read, own_v, phase_used, d_added) = a.sem(
            "loaded", "phase_ready", "half_ready", "sq_ready", "trig_ready", "bu_ready", "bu_used", "scanned",
            "prods_ready", "y_ready", "y_read", "own_v", "phase_used", "d_added")
        block = a.block()
        ps = g.ps
        BU, YB = 0, 6 * BANK

        @block.sync
        def _(sp):
            sp.dma_start(tau[:], g.d["k_s5_tau"]).then_inc(loaded, 16)

        @block.tensor
        def _(pe):
            def inputs(n):
                j, i, d = units[n]
                unit = d * S5_TILES + 4 * j + i
                if n:
                    pe.wait_ge(bu_used, n)
                for part in range(2):
                    for lo, hi in halves(T):
                        last = nc.tensor.matmul(ps[:, BU + part * 1024 + lo:BU + part * 1024 + hi],
                                                b_t[:, part, unit], u_t[:, j, lo:hi], start=True, stop=True)
                last.then_inc(bu_ready, 1)

            inputs(0)
            for n, (j, i, d) in enumerate(units):
                if n + 1 < len(units):
                    inputs(n + 1)
                unit = d * S5_TILES + 4 * j + i
                pe.wait_ge(prods_ready, n + 1)
                if i == 0 and d == 0 and j >= 2:
                    pe.wait_ge(y_read, j - 1)
                out = ps[:, YB + (j % 2) * BANK:YB + (j % 2 + 1) * BANK]
                for c, which in enumerate((0, 1, 2, 2)):
                    last = nc.tensor.matmul(out, c_t[:, which, unit], prods[:, n % 2, c],
                                            start=(i == 0 and d == 0 and c == 0), stop=(i == 3 and d == 1 and c == 3))
                last.then_inc(y_ready, 1)

        @block.scalar
        def _(act):
            for n in range(len(units)):
                b = n % 2
                act.wait_ge(phase_ready, n + 1)
                if n >= 2:
                    act.wait_ge(prods_ready, n - 1)
                nc.scalar.activation(sin[:, b], phase[:, b], ACT.Sin, scale=TWO_PI)
                nc.scalar.activation(cos[:, b], phase[:, b], ACT.Sin, scale=TWO_PI / 2).then_inc(half_ready, 1)
                act.wait_ge(half_ready, n + 1)
                nc.scalar.activation(cos[:, b], cos[:, b], ACT.Square).then_inc(sq_ready, 1)
                act.wait_ge(sq_ready, n + 1)
                nc.scalar.activation(cos[:, b], cos[:, b], ACT.Identity, bias=1.0, scale=-2.0)\
                    .then_inc(trig_ready, 1)
            for j in range(4):
                act.wait_ge(d_added, j + 1)
                nc.scalar.activation(z_t[:, j], z_t[:, j], ACT.Gelu)

        @block.vector
        def _(dve):
            own = Steps(dve, own_v)
            tt = nc.vector.tensor_tensor

            def phases(n):
                j, i, d = units[n]
                unit = d * S5_TILES + 4 * j + i
                b = n % 2
                if n >= 2:
                    dve.wait_ge(half_ready, n - 1)
                own(nc.vector.tensor_scalar(phase[:, b], tau[:, d], turns[:, unit:unit + 1], None, ALU.mult))
                own.settle()
                own(nc.vector.tensor_scalar(whole[:], phase[:, b], ROUND, ROUND, ALU.add, ALU.subtract))
                own.settle()
                tt(phase[:, b], phase[:, b], whole[:], ALU.subtract).then_inc(phase_ready, 1)

            def readout(j):
                dve.wait_ge(y_ready, 8 * (j + 1))
                at = VEC["s5_d"][0] + j
                nc.vector.scalar_tensor_tensor(out=z_t[:, j], in0=u_t[:, j, CTX:T], scalar=g.vec[:, at:at + 1],
                                               in1=ps[:, YB + (j % 2) * BANK:YB + (j % 2 + 1) * BANK],
                                               op0=ALU.mult, op1=ALU.add).then_inc(y_read, 1)
                dve.wait_ge(y_read, j + 1)
                dve.sem_inc(d_added, 1)

            dve.wait_ge(loaded, 16)
            phases(0)
            for n, (j, i, d) in enumerate(units):
                unit = d * S5_TILES + 4 * j + i
                b = n % 2
                if n + 1 < len(units):
                    phases(n + 1)
                re, im = ps[:, BU:BU + T], ps[:, BU + 1024:BU + 1024 + T]
                dve.wait_ge(trig_ready, n + 1)
                dve.wait_ge(bu_ready, n + 1)
                own(tt(v[:, 0], cos[:, b], re, ALU.mult))
                own(tt(x2[:, 0], sin[:, b], im, ALU.mult))
                own(tt(v[:, 1], cos[:, b], im, ALU.mult))
                own(tt(x2[:, 1], sin[:, b], re, ALU.mult))
                own.settle()
                dve.sem_inc(bu_used, 1)
                own(tt(v[:, 0], v[:, 0], x2[:, 0], ALU.add))
                own(tt(v[:, 1], v[:, 1], x2[:, 1], ALU.subtract))
                own.settle()
                if n >= 2:
                    dve.wait_ge(prods_ready, n - 1)
                r = rate[:, unit:unit + 1]
                for part in range(2):
                    x, out = v[:, part], s[:, b, part]
                    if d == 0:
                        own(nc.vector.tensor_tensor_scan(out, r.to_broadcast([P, T]), x, 0.0, ALU.mult, ALU.add))
                    else:
                        own(nc.vector.tensor_tensor_scan(out[:, 0:CTX][:, ::-1], r.to_broadcast([P, CTX]),
                                                         x[:, 0:CTX][:, ::-1], 0.0, ALU.mult, ALU.add))
                if d == 1:
                    own.settle()
                    for part in range(2):
                        x, out = v[:, part], s[:, b, part]
                        own(nc.vector.tensor_tensor_scan(out[:, CTX:T][:, ::-1], r.to_broadcast([P, LAT]),
                                                         x[:, CTX:T][:, ::-1], out[:, 0:1], ALU.mult, ALU.add))
                own.settle()
                dve.sem_inc(scanned, 1)
                if i == 0 and d == 0 and j:
                    readout(j - 1)
            readout(3)

        @block.gpsimd
        def _(pool):
            for n in range(len(units)):
                b = n % 2
                pool.wait_ge(scanned, n + 1)
                pool.wait_ge(trig_ready, n + 1)
                if n >= 2:
                    pool.wait_ge(y_ready, n - 1)
                for c, (part, table) in enumerate(((0, cos), (1, sin), (0, sin), (1, cos))):
                    last = nc.gpsimd.tensor_tensor(prods[:, b, c], s[:, b, part, CTX:T], table[:, b, CTX:T], ALU.mult)
                last.then_inc(prods_ready, 1)


def stage_s5_glu(nc, g, z_t):
    with ExitStack() as stack:
        a = Arena(nc, stack)
        w = a.sb("w_glu", [P, 4, 512])
        gate = a.sb("gate", [P, 4, LAT])
        loaded, summed, gated = a.sem("loaded", "summed", "gated")
        block = a.block()
        ps = g.ps

        @block.sync
        def _(sp):
            sp.dma_start(w[:], g.d["s5_w_glu"][0].rearrange("(k p) n -> p k n", p=P)).then_inc(loaded, 16)

        @block.tensor
        def _(pe):
            pe.wait_ge(loaded, 16)
            for m in range(4):
                for k in range(4):
                    last = nc.tensor.matmul(ps[:, m * BANK:(m + 1) * BANK], w[:, k, m * P:(m + 1) * P], z_t[:, k],
                                            start=(k == 0), stop=(k == 3))
                last.then_inc(summed, 1)

        @block.scalar
        def _(act):
            for m in range(4):
                act.wait_ge(summed, m + 1)
                at = VEC["s5_bglu"][0] + m
                nc.scalar.activation(gate[:, m], ps[:, m * BANK:(m + 1) * BANK], ACT.Sigmoid,
                                     bias=g.vec[:, at:at + 1]).then_inc(gated, 1)

        @block.vector
        def _(dve):
            dve.wait_ge(summed, 4)
            for m in range(4):
                dve.wait_ge(gated, m + 1)
                nc.vector.tensor_tensor(z_t[:, m], z_t[:, m], gate[:, m], ALU.mult)


def stage_output(nc, g):
    x = g.x_t[:, :, CTX:T]
    at = VEC["final"][0]
    stage_rms_channels(nc, g, x, DK, g.vec[:, at:at + 8])
    with ExitStack() as stack:
        a = Arena(nc, stack)
        rows = a.sb("out_rows", [P, LAT // P, D])
        turned, kept, stored = a.sem("turned", "kept", "stored")
        block = a.block()
        ps = g.ps

        @block.tensor
        def _(pe):
            for t in range(LAT // P):
                for k in range(DK):
                    last = nc.tensor.transpose(ps[:, t * 1024 + k * P:t * 1024 + (k + 1) * P],
                                               x[:, k, t * P:(t + 1) * P], g.ident[:])
                last.then_inc(turned, 1)

        @block.vector
        def _(dve):
            for t in range(LAT // P):
                dve.wait_ge(turned, t + 1)
                nc.vector.tensor_copy(rows[:, t], ps[:, t * 1024:(t + 1) * 1024]).then_inc(kept, 1)

        @block.sync
        def _(sp):
            for t in range(LAT // P):
                sp.wait_ge(kept, t + 1)
                sp.dma_start(g.out[0, t * P:(t + 1) * P, :], rows[:, t]).then_inc(stored, 16)
            sp.wait_ge(stored, 16 * (LAT // P))


def peer(nc, g, layer, t0, until=99):
    n = T - t0
    spans = [(0, LAT, CTX, 0)] + ([(LAT, T, 0, 1)] if t0 == 0 else [])
    with ExitStack() as stack:
        a = Arena(nc, stack)
        table = nc.dram_tensor(f"gate_table{layer}", (P, n // TB, KEYS, TB), F32).ap()
        hi = a.sb("h_hi", [P, DK, n], F32R)
        lo = a.sb("h_lo", [P, DK, n], F32R)
        with ExitStack() as inner:
            b = Arena(nc, inner)
            slots = b.sb("slots", [P, 3, n])
            with ExitStack() as scope:
                c = Arena(nc, scope)
                q_t = c.sb("peer_q", [P, 2 * PEER_H, n])
                with ExitStack() as early:
                    h_t = Arena(nc, early).sb("h_t", [P, DK, n])
                    stage_norm(nc, g, layer, 1, t0, h_t, latents_first=True)
                    stage_split(nc, g, h_t, hi, lo)
                    wq = g.d["peer_wq"][layer].rearrange("(k p) n -> p k n", p=P)
                    stage_project(nc, g, "peer_wq", h_t, wq,
                                  [(512 * i, 512, channel_units(q_t[:, 4 * i:4 * i + 4], 4)) for i in range(4)])
                stage_route(nc, g, layer, q_t, slots, n)
            stage_gate_table(nc, g, slots, table, n)
        if until >= 7:
            stage_experts(nc, g, layer, hi, lo, table, n, spans)


def layer_even(nc, g, until):
    w_in = g.d["ev_w_in"][0].rearrange("(k p) n -> p k n", p=P)
    with ExitStack() as stack:
        a = Arena(nc, stack)
        y_t = a.sb("y_t", [P, DK, T])
        with ExitStack() as inner:
            b = Arena(nc, inner)
            hg = b.sb("hg", [P, 4, HG_HEADS, T])
            hg_v = b.sb("hg_v", [P, T // P, 512])
            with ExitStack() as scope:
                c = Arena(nc, scope)
                proj = c.sb("gqa_proj", [P, T // P, GQA_IN])
                with ExitStack() as early:
                    h_t = Arena(nc, early).sb("h_t", [P, DK, T])
                    stage_norm(nc, g, 0, 0, 0, h_t)
                    at = GQA_IN
                    pairs = proj[:, :, 0:512].rearrange("p t (j kv c) -> p t kv j c", j=4, kv=2)
                    blocks = [(0, 512, [("tokens", t, pairs[:, t]) for t in range(T // P)]),
                              (512, 256, token_units(proj[:, :, 512:768], T // P)),
                              (at, 512, channel_units(hg[:, 0], 4)), (at + 512, 512, channel_units(hg[:, 1], 4)),
                              (at + 1024, 512, channel_units(hg[:, 2], 4)),
                              (at + 1536, 512, token_units(hg_v[:], T // P)),
                              (at + 2048, 512, channel_units(hg[:, 3], 4))]
                    stage_project(nc, g, "ev_in", h_t, w_in, blocks)
                if until >= 2:
                    q_t = c.sb("q_t", [P, 4, T])
                    k_t = c.sb("k_t", [P, T])
                    stage_gqa_heads(nc, g, proj, q_t, k_t)
                if until >= 3:
                    units = []
                    for t in range(T // P):
                        keys = CTX if t < CTX // P else T
                        for j in range(4):
                            for kv in range(2):
                                rows = slice(64 * kv, 64 * kv + 64)
                                at = (GQA_Q + GQA_KV + kv) * HEAD

                                def v(i, at=at):
                                    return proj[:, i, at:at + HEAD]

                                units.append((q_t[rows, j, t * P:(t + 1) * P], k_t[rows, 0:keys], v, 64 * kv,
                                              y_t[:, j, t * P:(t + 1) * P]))
                    stage_attention(nc, g, units)
            if until >= 4:
                keep_k = b.sb("keep_k", [P, 2 * HG_HEADS, T])
                cum = b.sb("cum", [P, 2 * HG_HEADS, T])
                with ExitStack() as scope:
                    forget = Arena(nc, scope).sb("forget", [P, HG_HEADS, T])
                    stage_hgrn2_gates(nc, g, hg, forget, keep_k, cum)
                stage_hgrn2_scan(nc, g, hg, hg_v, keep_k, cum, y_t)
                stage_hgrn2_readout(nc, g, hg, y_t)
        if until >= 5:
            w_out = g.d["ev_w_out"][0]
            rows = [(slice(64 * kv, 64 * kv + 64), j, w_out[256 * kv + 64 * j:256 * kv + 64 * j + 64, :])
                    for kv in range(2) for j in range(4)]
            rows += [(slice(0, P), k, w_out[k * P:(k + 1) * P, :]) for k in range(4, DK)]
            stage_mix_out(nc, g, 0, y_t, 0, rows)
    if until >= 6:
        peer(nc, g, 0, 0, until)


def layer_odd(nc, g, until):
    w_in = g.d["od_w_in"][0].rearrange("(k p) n -> p k n", p=P)
    with ExitStack() as stack:
        a = Arena(nc, stack)
        y_t = a.sb("y_t", [P, DK, LAT])
        with ExitStack() as inner:
            b = Arena(nc, inner)
            u_t = b.sb("u_t", [P, 4, T])
            with ExitStack() as scope:
                c = Arena(nc, scope)
                q_a = c.sb("q_a", [P, MLA_QR // P, LAT])
                kv_a = c.sb("kv_a", [P, MLA_KVR // P, T])
                k_rope = c.sb("k_rope", [MLA_ROPE, T])
                with ExitStack() as early:
                    h_t = Arena(nc, early).sb("h_t", [P, DK, T])
                    stage_norm(nc, g, 1, 0, 0, h_t)
                    blocks = [(0, MLA_QR, [("latents", m * P, q_a[:, m, :]) for m in range(MLA_QR // P)]),
                              (MLA_QR, MLA_KVR, channel_units(kv_a, MLA_KVR // P)),
                              (MLA_QR + MLA_KVR, MLA_ROPE, [("channels", 0, k_rope[:])]),
                              (MLA_IN, 512, channel_units(u_t, 4))]
                    stage_project(nc, g, "od_in", h_t, w_in, blocks)
                at, _ = VEC["mla_qa"]
                stage_rms_channels(nc, g, q_a, MLA_QR // P, g.vec[:, at:at + 3], (MLA_NOPE + MLA_ROPE) ** -0.5)
                at, _ = VEC["mla_kva"]
                stage_rms_channels(nc, g, kv_a, MLA_KVR // P, g.vec[:, at:at + 2])
                q_t = c.sb("mla_q", [P, MLA_H, LAT])
                k_t = c.sb("mla_k", [P, MLA_H, T])
                v_tok = c.sb("mla_v", [P, T // P, MLA_H * MLA_V])
                stage_mla_heads(nc, g, q_a, kv_a, k_rope, q_t, k_t, v_tok)
                units = []
                for t in range(LAT // P):
                    for h in range(MLA_H):
                        def v(i, h=h):
                            return v_tok[:, i, h * MLA_V:(h + 1) * MLA_V]

                        units.append((q_t[0:96, h, t * P:(t + 1) * P], k_t[0:96, h, :], v, 64 * (h % 2),
                                      y_t[:, h // 2, t * P:(t + 1) * P]))
                stage_attention(nc, g, units)
            if until >= 9:
                N = 2 * S5_TILES
                rate = b.sb("rate", [P, N])
                turns = b.sb("turns", [P, N])
                b_t = b.sb("b_t", [P, 2, N, P])
                c_t = b.sb("c_t", [P, 3, N, P])
                z_t = y_t[:, 4:DK]
                stage_s5_parameters(nc, g, rate, turns, b_t, c_t)
                stage_s5_scan(nc, g, u_t, rate, turns, b_t, c_t, z_t)
                stage_s5_glu(nc, g, z_t)
        if until >= 10:
            w_out = g.d["od_w_out"][0]
            stage_mix_out(nc, g, 1, y_t, CTX, [(slice(0, P), k, w_out[k * P:(k + 1) * P, :]) for k in range(DK)])
    if until >= 11:
        peer(nc, g, 1, CTX)
    if until >= 12:
        stage_output(nc, g)


def rope_table(rot_dim):
    axis_dim = rot_dim // 2
    inv = np.float32(10000.0) ** (-np.arange(0, axis_dim, 2, dtype=np.float32) / np.float32(axis_dim))
    t = np.arange(LAT)
    angle = np.stack([(t // GRID_W).astype(np.float32)[:, None] * inv,
                      (t % GRID_W).astype(np.float32)[:, None] * inv], 1)
    return np.stack([np.cos(angle), np.sin(angle)]).astype(np.float32)


def constants():
    gqa = rope_table(HEAD).reshape(2, 4, P, 2, 16).transpose(2, 0, 1, 3, 4)
    masks = np.zeros((2, P, NL, P), np.float32)
    key, query = np.arange(P)[:, None], np.arange(P)[None, :]
    for e, m in enumerate(HG_LEVELS):
        same = key // (2 * m) == query // (2 * m)
        masks[0, :, e] = same & (key // m % 2 == 0) & (query // m % 2 == 1)
        masks[1, :, e] = same & (key // m % 2 == 1) & (query // m % 2 == 0)
    masks[:, :, NL - 1] = np.eye(P)
    mla = rope_table(MLA_ROPE)
    cos, sin = (np.stack([mla[w], mla[w]], 2).reshape(LAT, MLA_ROPE).T for w in range(2))
    channel = np.arange(MLA_ROPE)
    sin = sin * np.where(channel // 8 % 2 == 0, -1.0, 1.0).astype(np.float32)[:, None]
    swap = np.zeros((MLA_ROPE, MLA_ROPE), np.float32)
    swap[channel ^ 8, channel] = 1.0
    part = np.arange(P)
    tile, group = np.arange(4)[:, None], np.arange(8)[None, :]
    bmask = (group[None] == 2 * tile[None] + (part // S5_P)[:, None, None]).astype(np.float32)
    cmask = (part[:, None] // S5_C == np.arange(8)[None, :]).astype(np.float32)
    t = np.arange(T)
    tau = np.stack([t, np.where(t < CTX, CTX - 1 - t, CTX + T - 1 - t)]).astype(np.float32)
    return {"k_rope_mla": np.ascontiguousarray(np.stack([cos, sin], 1)), "k_rope_swap": swap,
            "k_s5_bmask": bmask, "k_s5_cmask": cmask, "k_s5_tau": np.tile(tau[None], (P, 1, 1)),
            "k_hg_masks": masks.reshape(2, P, NL * P), "k_ident": np.eye(P, dtype=np.float32),
            "k_iota": np.tile(np.arange(P, dtype=np.float32), (P, 1)), "k_rope_gqa": np.ascontiguousarray(gqa)}


def kernel(**inputs):
    import concourse.bacc as bacc
    from concourse.bass_utils import run_bass_kernel_spmd

    nc = bacc.Bacc("TRN2", target_bir_lowering=False, num_devices=1)
    arrays = {name: np.ascontiguousarray(v) for name, v in inputs.items()}
    arrays.update(constants())
    d = {name: nc.dram_tensor(name, v.shape, mybir.dt.from_np(v.dtype), kind="ExternalInput").ap()
         for name, v in arrays.items()}
    out = nc.dram_tensor("out", (1, LAT, D), F32, kind="ExternalOutput").ap()
    build(nc, d, out)
    result = run_bass_kernel_spmd(nc, [arrays], core_ids=[0])
    return result.results[0]["out"]
```

```python
from contextlib import ExitStack

import numpy as np

import concourse.bass as bass
from concourse import mybir

F32 = mybir.dt.float32
F32R = mybir.dt.float32r
U32 = mybir.dt.uint32
ACT = mybir.ActivationFunctionType
ALU = mybir.AluOpType
AX = mybir.AxisListType

P = 128
D = 1024
DK = D // P
CTX, LAT = 256, 512
T = CTX + LAT
GRID_W = 64
EPS = 1e-6
BANK = 512

GQA_Q, GQA_KV, HEAD = 8, 2, 64
GQA_IN = (GQA_Q + 2 * GQA_KV) * HEAD
HG_HEADS = 4
EVEN_IN = GQA_IN + 5 * 512
MLA_H, MLA_NOPE, MLA_ROPE, MLA_V = 8, 64, 32, 64
MLA_QR, MLA_KVR = 384, 256
MLA_IN = MLA_QR + MLA_KVR + MLA_ROPE
ODD_IN = MLA_IN + 512
S5_G, S5_P, S5_C = 32, 64, 16

PEER_H, KEYS, TOPK, QDIM = 8, 128, 16, 256
SLOTS = PEER_H * TOPK
EXPERTS = KEYS * KEYS
LOWEST = -3.0e38
FIRST_SEM, SEM_BANK = 100, 77

VEC = {}
for _name, _n in (("c", 8), ("c_ctx", 8), ("norm1", 16), ("norm2", 16), ("final", 8), ("lb", 16), ("onorm", 1),
                  ("s5_d", 4), ("s5_bglu", 4), ("mla_qa", 3), ("mla_kva", 2)):
    VEC[_name] = (sum(n for _, n in VEC.values()), _n)
VEC_ROWS = sum(n for _, n in VEC.values())


class Steps:

    def __init__(self, engine, sem):
        self.engine, self.sem, self.n = engine, sem, 0

    def __call__(self, instruction):
        instruction.then_inc(self.sem, 1)
        self.n += 1

    def settle(self):
        self.engine.wait_ge(self.sem, self.n)


class Arena:

    uses = {}
    stages = 0

    def __init__(self, nc, stack):
        self.nc, self.stack, self.sems = nc, stack, []

    @staticmethod
    def fresh(name):
        Arena.uses[name] = n = Arena.uses.get(name, 0) + 1
        return name if n == 1 else f"{name}_{n}"

    def sb(self, name, shape, dt=F32):
        return self.stack.enter_context(self.nc.sbuf_tensor(Arena.fresh(name), shape, dt))

    def sem(self, *names):
        if not self.sems:
            Arena.stages += 1
            self.stack.callback(self.clear)
        base = FIRST_SEM + (Arena.stages % 2) * SEM_BANK
        for name in names:
            assert len(self.sems) < SEM_BANK
            self.sems.append(self.nc.alloc_semaphore(Arena.fresh(name), num=base + len(self.sems)))
        got = self.sems[-len(names):]
        return got[0] if len(got) == 1 else got

    def clear(self):
        base = FIRST_SEM + (Arena.stages % 2) * SEM_BANK
        self.nc.gpsimd.sem_clear(range(base, base + len(self.sems)))
        for sem in self.sems:
            self.nc.release_semaphore(sem)

    def block(self):
        return self.stack.enter_context(self.nc.Block())


def stage_load_tokens(nc, g):
    with ExitStack() as stack:
        a = Arena(nc, stack)
        tokens = a.sb("tokens", [P, T // P, D])
        rows = a.sb("rows", [VEC_ROWS, P])
        ada_rows = a.sb("ada_rows", [96, P])
        const_loaded, rows_loaded, tile_loaded = a.sem("const_loaded", "rows_loaded", "tile_loaded")
        transposed, evacuated_v, evacuated_s = a.sem("transposed", "evacuated_v", "evacuated_s")
        block = a.block()
        ps = g.ps

        @block.sync
        def _(sp):
            sp.dma_start(g.ident[:], g.d["k_ident"]).then_inc(const_loaded, 16)
            for j in range(T // P):
                src = g.d["ctx"][0, j * P:(j + 1) * P, :] if j < 2 else g.d["x"][0, (j - 2) * P:(j - 1) * P, :]
                if j:
                    sp.wait_ge(tile_loaded, 16 * j)
                sp.dma_start(tokens[:, j, :], src).then_inc(tile_loaded, 16)

        n_rows = 16 * (len(VEC) + 1)

        @block.tensor
        def _(pe):
            pe.wait_ge(const_loaded, 16)
            for j in range(T // P):
                pe.wait_ge(tile_loaded, 16 * (j + 1))
                slot = j % 3
                if j >= 3:
                    pe.wait_ge(evacuated_v, j - 2)
                    pe.wait_ge(evacuated_s, j - 2)
                for k in range(DK):
                    last = nc.tensor.transpose(ps[:, (slot * 8 + k) * P:(slot * 8 + k + 1) * P],
                                               tokens[:, j, k * P:(k + 1) * P], g.ident[:])
                last.then_inc(transposed, 1)
            pe.wait_ge(rows_loaded, n_rows)
            nc.tensor.transpose(ps[:, 6 * BANK:6 * BANK + VEC_ROWS], rows[:], g.ident[:VEC_ROWS, :VEC_ROWS])
            nc.tensor.transpose(ps[:, 7 * BANK:7 * BANK + 96], ada_rows[:], g.ident[:96, :96]).then_inc(transposed, 1)

        @block.vector
        def _(dve):
            nc.vector.memset(g.ones_d[:], 1.0 / D)
            for j in range(T // P):
                dve.wait_ge(transposed, j + 1)
                src = ps[:, (j % 3) * 1024:(j % 3) * 1024 + 512].rearrange("p (k t) -> p k t", t=P)
                nc.vector.tensor_copy(g.x_t[:, 0:4, j * P:(j + 1) * P], src).then_inc(evacuated_v, 1)
            dve.wait_ge(transposed, T // P + 1)
            nc.vector.tensor_copy(g.vec[:], ps[:, 6 * BANK:6 * BANK + VEC_ROWS])
            nc.vector.tensor_copy(g.ada_b[:], ps[:, 7 * BANK:7 * BANK + 96])

        @block.scalar
        def _(act):
            d = g.d
            loads = [("c", d["c"].rearrange("o (k p) -> (o k) p", p=P)),
                     ("c_ctx", d["c_ctx"].rearrange("(k p) -> k p", p=P)),
                     ("norm1", d["norm1_g"].rearrange("l (k p) -> (l k) p", p=P)),
                     ("norm2", d["norm2_g"].rearrange("l (k p) -> (l k) p", p=P)),
                     ("final", d["final_g"].rearrange("(k p) -> k p", p=P)),
                     ("lb", d["hg_lb_logits"].rearrange("d e (k p) -> (d e k) p", p=P)),
                     ("onorm", d["hg_onorm_g"]),
                     ("s5_d", d["s5_d"].rearrange("o (k p) -> (o k) p", p=P)),
                     ("s5_bglu", d["s5_b_glu"].rearrange("o (k p) -> (o k) p", p=P)),
                     ("mla_qa", d["mla_qa_g"].rearrange("o (k p) -> (o k) p", p=P)),
                     ("mla_kva", d["mla_kva_g"].rearrange("o (k p) -> (o k) p", p=P))]
            for name, src in loads:
                at, n = VEC[name]
                act.dma_start(rows[at:at + n, :], src).then_inc(rows_loaded, 16)
            act.dma_start(ada_rows[:], d["ada_b"].rearrange("l (k p) -> (l k) p", p=P)).then_inc(rows_loaded, 16)
            for j in range(T // P):
                act.wait_ge(transposed, j + 1)
                src = ps[:, (j % 3) * 1024 + 512:(j % 3) * 1024 + 1024].rearrange("p (k t) -> p k t", t=P)
                nc.scalar.copy(g.x_t[:, 4:8, j * P:(j + 1) * P], src).then_inc(evacuated_s, 1)


def stage_modulation(nc, g):
    COLS, RING = 512, 3
    with ExitStack() as stack:
        a = Arena(nc, stack)
        w = a.sb("ada_ring", [P, RING, DK, COLS])
        cond = a.sb("cond", [P, 2, DK])
        w_loaded = [a.sem(f"w_loaded{r}") for r in range(RING)]
        summed = [a.sem(f"summed{r}") for r in range(RING)]
        kept = [a.sem(f"kept{r}") for r in range(RING)]
        cond_ready, scaled = a.sem("cond_ready", "scaled")
        block = a.block()
        ps = g.ps
        tiles = COLS // P
        ada = [g.d["ada_w"][layer].rearrange("(k p) n -> p k n", p=P) for layer in range(2)]
        turns = 6 * D // COLS // RING

        def ring_turns(engine, emit):
            emit(0, 0, True)
            for layer in range(2):
                with engine.Fori(1 - layer, turns) as i:
                    emit(layer, i, False)

        @block.sync
        def _(sp):
            def turn(layer, i, first):
                for r in range(RING):
                    if not first:
                        sp.wait_ge(summed[r], i + layer * turns)
                    sp.dma_start(w[:, r], ada[layer][:, :, bass.ds((i * RING + r) * COLS, COLS)])\
                        .then_inc(w_loaded[r], 16)

            ring_turns(sp, turn)

        @block.scalar
        def _(act):
            nc.scalar.activation(cond[:], g.vec[:, 0:16].rearrange("p (s k) -> p s k", s=2), ACT.Silu)\
                .then_inc(cond_ready, 1)

        @block.tensor
        def _(pe):
            def turn(layer, i, first):
                for r in range(RING):
                    pe.wait_ge(w_loaded[r], i * 16 + (layer * turns + 1) * 16)
                    if not first:
                        pe.wait_ge(kept[r], i + layer * turns)
                    for m in range(tiles):
                        for k in range(DK):
                            last = nc.tensor.matmul(ps[:, r * BANK + 2 * m:r * BANK + 2 * m + 2],
                                                    w[:, r, k, m * P:(m + 1) * P], cond[:, :, k],
                                                    start=(k == 0), stop=(k == DK - 1))
                    last.then_inc(summed[r], 1)

            pe.wait_ge(cond_ready, 1)
            ring_turns(pe, turn)

        @block.vector
        def _(dve):
            def turn(layer, i, first):
                bias = g.ada_b[:, 48 * layer:48 * (layer + 1)]
                for r in range(RING):
                    dve.wait_ge(summed[r], i + layer * turns + 1)
                    sums = ps[:, r * BANK:r * BANK + 2 * tiles].rearrange("p (m s) -> p m s", s=2)
                    for s in range(2):
                        last = nc.vector.tensor_tensor(g.mod[:, layer, bass.ds((i * RING + r) * tiles, tiles), s],
                                                       sums[:, :, s],
                                                       bias[:, bass.ds((i * RING + r) * tiles, tiles)], ALU.add)
                    last.then_inc(kept[r], 1)

            ring_turns(dve, turn)
            for r in range(RING):
                dve.wait_ge(kept[r], 2 * turns)
            own = Steps(dve, scaled)
            for layer in range(2):
                for which, (norm, part) in enumerate((("norm1", 1), ("norm2", 4))):
                    at = VEC[norm][0] + 8 * layer
                    gs = g.gs[:, layer, which]
                    own(nc.vector.tensor_scalar(gs, g.mod[:, layer, 8 * part:8 * part + 8, :], 1.0, None, ALU.add))
                    own.settle()
                    own(nc.vector.tensor_tensor(gs, gs, g.vec[:, at:at + 8].unsqueeze(2).to_broadcast([P, 8, 2]),
                                                ALU.mult))


STREAMS = ((1, 0, CTX), (0, CTX, T))


def stage_norm(nc, g, layer, which, t0, h_t, latents_first=False):
    n = T - t0

    def cols(b, e):
        if latents_first:
            b, e = ((b + LAT, e + LAT) if b < CTX else (b - CTX, e - CTX))
            return slice(b, e)
        return slice(b - t0, e - t0)

    parts = [(s, e) for s, e in ((t0, CTX), (CTX, T)) if e > s]
    streams = [(s, max(b, t0), e) for s, b, e in STREAMS if e > t0]
    shift = 8 * 3 * which
    with ExitStack() as stack:
        a = Arena(nc, stack)
        sq = a.sb("sq", [P, DK, n])
        rstd = a.sb("rstd", [P, n])
        squared, summed, root_in, rooted, scaled = a.sem("squared", "summed", "root_in", "rooted", "scaled")
        own_v = a.sem("own_v")
        block = a.block()
        ps = g.ps

        @block.scalar
        def _(act):
            for k in range(DK):
                nc.scalar.activation(sq[:, k], g.x_t[:, k, t0:T], ACT.Square).then_inc(squared, 1)
            act.wait_ge(root_in, 1)
            nc.scalar.activation(rstd[:], rstd[:], ACT.Sqrt).then_inc(rooted, 1)
            for k in range(DK):
                for i, (s, b, e) in enumerate(streams):
                    act.wait_ge(scaled, len(streams) * k + i + 1)
                    nc.scalar.activation(h_t[:, k, cols(b, e)], h_t[:, k, cols(b, e)], ACT.Identity,
                                         bias=g.mod[:, layer, shift + k, s:s + 1])

        @block.tensor
        def _(pe):
            for k in range(DK):
                pe.wait_ge(squared, k + 1)
                for i, (b, e) in enumerate(parts):
                    last = nc.tensor.matmul(ps[:, i * BANK:i * BANK + e - b], g.ones_d[:], sq[:, k, b - t0:e - t0],
                                            start=(k == 0), stop=(k == DK - 1))
            last.then_inc(summed, 1)

        @block.vector
        def _(dve):
            own = Steps(dve, own_v)
            dve.wait_ge(summed, 1)
            for i, (b, e) in enumerate(parts):
                last = nc.vector.tensor_scalar(rstd[:, b - t0:e - t0], ps[:, i * BANK:i * BANK + e - b], EPS, None,
                                               ALU.add)
            last.then_inc(root_in, 1)
            dve.wait_ge(rooted, 1)
            own(nc.vector.reciprocal(rstd[:], rstd[:]))
            own.settle()
            for k in range(DK):
                for s, b, e in streams:
                    nc.vector.scalar_tensor_tensor(out=h_t[:, k, cols(b, e)], in0=g.x_t[:, k, b:e],
                                                   scalar=g.gs[:, layer, which, k, s:s + 1],
                                                   in1=rstd[:, b - t0:e - t0],
                                                   op0=ALU.mult, op1=ALU.mult).then_inc(scaled, 1)


def halves(n):
    return [(b, min(b + BANK, n)) for b in range(0, n, BANK)]


def stage_project(nc, g, name, h_t, w_view, blocks, kc=DK):
    RING, SLOTS_PS = 3, 4
    widest = max(cols for _, cols, _ in blocks)
    units = [(b, kind, place, out) for b, (_, _, us) in enumerate(blocks) for kind, place, out in us]
    with ExitStack() as stack:
        a = Arena(nc, stack)
        w = a.sb(f"{name}_ring", [P, min(RING, len(blocks)), kc, widest])
        ring = min(RING, len(blocks))
        w_loaded = [a.sem(f"w_loaded{r}") for r in range(ring)]
        w_used, summed, kept_v, kept_s = a.sem("w_used", "summed", "kept_v", "kept_s")
        block = a.block()
        ps = g.ps

        @block.sync
        def _(sp):
            for b, (c0, cols, _) in enumerate(blocks):
                if b >= ring:
                    sp.wait_ge(w_used, b - ring + 1)
                sp.dma_start(w[:, b % ring, :, 0:cols], w_view[:, :, c0:c0 + cols]).then_inc(w_loaded[b % ring], 16)

        @block.tensor
        def _(pe):
            for u, (b, kind, place, _) in enumerate(units):
                cols = blocks[b][1]
                at = (u % SLOTS_PS) * 2 * BANK
                pe.wait_ge(w_loaded[b % ring], 16 * (b // ring + 1))
                if u >= SLOTS_PS:
                    pe.wait_ge(kept_s if u % 2 else kept_v, (u - SLOTS_PS) // 2 + 1)
                for k in range(kc):
                    if kind != "tokens":
                        m = min(P, cols - place)
                        t0 = CTX if kind == "latents" else 0
                        for lo, hi in halves(h_t.shape[2] - t0):
                            last = nc.tensor.matmul(ps[0:m, at + lo:at + hi], w[:, b % ring, k, place:place + m],
                                                    h_t[:, k, t0 + lo:t0 + hi], start=(k == 0), stop=(k == kc - 1))
                    else:
                        last = nc.tensor.matmul(ps[:, at:at + cols], h_t[:, k, place * P:(place + 1) * P],
                                                w[:, b % ring, k, 0:cols], start=(k == 0), stop=(k == kc - 1))
                last.then_inc(summed, 1)
                if u + 1 == len(units) or units[u + 1][0] != b:
                    pe.wait_ge(summed, u + 1)
                    pe.sem_inc(w_used, 1)

        def result(u):
            b, kind, place, _ = units[u]
            at = (u % SLOTS_PS) * 2 * BANK
            cols = blocks[b][1]
            if kind != "tokens":
                return ps[0:min(P, cols - place), at:at + h_t.shape[2] - (CTX if kind == "latents" else 0)]
            if len(units[u][3].shape) == 4:
                _, kv, j, c = units[u][3].shape
                return ps[:, at:at + cols].rearrange("p (kv j c) -> p kv j c", kv=kv, j=j)
            return ps[:, at:at + cols]

        @block.vector
        def _(dve):
            for u in range(0, len(units), 2):
                dve.wait_ge(summed, u + 1)
                nc.vector.tensor_copy(units[u][3], result(u)).then_inc(kept_v, 1)

        @block.scalar
        def _(act):
            for u in range(1, len(units), 2):
                act.wait_ge(summed, u + 1)
                nc.scalar.copy(units[u][3], result(u)).then_inc(kept_s, 1)


def channel_units(out, tiles):
    return [("channels", m * P, out[:, m, :]) for m in range(tiles)]


def token_units(out, tiles):
    return [("tokens", j, out[:, j, :]) for j in range(tiles)]


def stage_gqa_heads(nc, g, proj, q_t, k_t):
    NT, NH, N = T // P, GQA_Q + GQA_KV, (GQA_Q + GQA_KV) * HEAD
    with ExitStack() as stack:
        a = Arena(nc, stack)
        sq = a.sb("sq", [P, NT, N])
        heads = a.sb("heads", [P, NT, N])
        rstd = a.sb("rstd", [P, NT, NH])
        gain = a.sb("gain", [P, 2, HEAD])
        rope = a.sb("rope", [P, 2, 4, 2, 16])
        scratch = a.sb("scratch", [P, 4, NH * 2 * 16])
        loaded, root_in, rooted, ready, transposed, kept, own_v = a.sem(
            "loaded", "root_in", "rooted", "ready", "transposed", "kept", "own_v")
        block = a.block()
        ps = g.ps

        @block.sync
        def _(sp):
            sp.dma_start(gain[:, 0, :], g.d["gqa_qn_g"].to_broadcast([P, HEAD])).then_inc(loaded, 16)
            sp.dma_start(gain[:, 1, :], g.d["gqa_kn_g"].to_broadcast([P, HEAD])).then_inc(loaded, 16)
            sp.dma_start(rope[:], g.d["k_rope_gqa"]).then_inc(loaded, 16)

        @block.vector
        def _(dve):
            own = Steps(dve, own_v)
            own(nc.vector.tensor_tensor(sq[:], proj[:, :, 0:N], proj[:, :, 0:N], ALU.mult))
            own.settle()
            own(nc.vector.tensor_reduce(rstd[:], sq[:].rearrange("p t (h c) -> p t h c", c=HEAD), AX.X, ALU.add))
            own.settle()
            nc.vector.tensor_scalar(rstd[:], rstd[:], 1.0 / HEAD, EPS, ALU.mult, ALU.add).then_inc(root_in, 1)
            dve.wait_ge(rooted, 1)
            own(nc.vector.reciprocal(rstd[:], rstd[:]))
            own.settle()
            own(nc.vector.tensor_scalar(rstd[:, :, 0:GQA_Q], rstd[:, :, 0:GQA_Q], HEAD ** -0.5, None, ALU.mult))
            own.settle()
            for t in range(NT):
                own(nc.vector.tensor_tensor(sq[:, t].rearrange("p (h c) -> p h c", c=HEAD),
                                            proj[:, t, 0:N].rearrange("p (h c) -> p h c", c=HEAD),
                                            rstd[:, t].unsqueeze(2).to_broadcast([P, NH, HEAD]), ALU.mult))
            dve.wait_ge(loaded, 48)
            own.settle()
            for which, h0, nh in ((0, 0, GQA_Q), (1, GQA_Q, GQA_KV)):
                cols = slice(h0 * HEAD, (h0 + nh) * HEAD)
                for out, lo, hi in ((heads, 0, 2), (sq, 2, NT)):
                    for t in range(lo, hi):
                        own(nc.vector.tensor_tensor(out[:, t, cols].rearrange("p (h c) -> p h c", c=HEAD),
                                                    sq[:, t, cols].rearrange("p (h c) -> p h c", c=HEAD),
                                                    gain[:, which, :].unsqueeze(1).to_broadcast([P, nh, HEAD]),
                                                    ALU.mult))
            own.settle()
            dve.sem_inc(ready, 2)
            for t in range(2, NT):
                for axis in range(2):
                    def half(x, i):
                        return x[:, t].rearrange("p (h a i c) -> p h a i c", a=2, i=2, c=16)[:, :, axis, i, :]

                    cos, sin = (rope[:, w, t - 2, axis, :].unsqueeze(1).to_broadcast([P, NH, 16]) for w in range(2))
                    parts = [scratch[:, 2 * axis + w, 0:NH * 16].rearrange("p (h c) -> p h c", c=16)
                             for w in range(2)]
                    parts += [scratch[:, 2 * axis + w, NH * 16:].rearrange("p (h c) -> p h c", c=16)
                              for w in range(2)]
                    own(nc.vector.tensor_tensor(parts[0], half(sq, 0), cos, ALU.mult))
                    own(nc.vector.tensor_tensor(parts[1], half(sq, 1), sin, ALU.mult))
                    own(nc.vector.tensor_tensor(parts[2], half(sq, 0), sin, ALU.mult))
                    own(nc.vector.tensor_tensor(parts[3], half(sq, 1), cos, ALU.mult))
                    own.settle()
                    own(nc.vector.tensor_tensor(half(heads, 0), parts[0], parts[1], ALU.subtract))
                    own(nc.vector.tensor_tensor(half(heads, 1), parts[2], parts[3], ALU.add))
                own.settle()
                dve.sem_inc(ready, 1)

        @block.tensor
        def _(pe):
            for t in range(NT):
                pe.wait_ge(ready, t + 1)
                if t >= 4:
                    pe.wait_ge(kept, t - 3)
                at = (t % 4) * 1024
                for j in range(4):
                    nc.tensor.transpose(ps[:, at + j * P:at + (j + 1) * P], heads[:, t, j * P:(j + 1) * P], g.ident[:])
                nc.tensor.transpose(ps[:, at + 4 * P:at + 5 * P], heads[:, t, GQA_Q * HEAD:N], g.ident[:])\
                    .then_inc(transposed, 1)

        @block.scalar
        def _(act):
            act.wait_ge(root_in, 1)
            nc.scalar.activation(rstd[:], rstd[:], ACT.Sqrt).then_inc(rooted, 1)
            for t in range(NT):
                act.wait_ge(transposed, t + 1)
                at = (t % 4) * 1024
                nc.scalar.copy(q_t[:, :, t * P:(t + 1) * P],
                               ps[:, at:at + 4 * P].rearrange("p (j t) -> p j t", t=P))
                nc.scalar.copy(k_t[:, t * P:(t + 1) * P], ps[:, at + 4 * P:at + 5 * P]).then_inc(kept, 1)


def stage_attention(nc, g, units):
    widest = max(u[1].shape[1] for u in units)
    with ExitStack() as stack:
        a = Arena(nc, stack)
        probs = a.sb("probs", [P, 2, widest])
        probs_t = a.sb("probs_t", [P, 2, widest])
        neg_max = a.sb("neg_max", [P, 2, 1])
        sums = a.sb("sums", [P, 2, 1])
        inverse = a.sb("inverse", [P, 2, 1])
        scores_ready, max_ready, exps_ready, probs_ready, transposed, probs_t_ready, mixed, out_kept, own_v = a.sem(
            "scores_ready", "max_ready", "exps_ready", "probs_ready", "transposed", "probs_t_ready", "mixed",
            "out_kept", "own_v")
        block = a.block()
        ps = g.ps
        T_AT, O_AT = 4 * BANK, 6 * BANK
        n_units = len(units)

        @block.tensor
        def _(pe):
            def scores(u):
                q, k = units[u][0], units[u][1]
                n = k.shape[1]
                if u >= 2:
                    pe.wait_ge(exps_ready, u - 1)
                for lo, hi in halves(n):
                    last = nc.tensor.matmul(ps[:, (u % 2) * 1024 + lo:(u % 2) * 1024 + hi], q, k[:, lo:hi],
                                            start=True, stop=True)
                last.then_inc(scores_ready, 1)

            def mix(u):
                _, k, v, p0, _ = units[u]
                tiles = k.shape[1] // P
                pe.wait_ge(probs_ready, u + 1)
                if u >= 1:
                    pe.wait_ge(probs_t_ready, u)
                for i in range(tiles):
                    last = nc.tensor.transpose(ps[:, T_AT + i * P:T_AT + (i + 1) * P],
                                               probs[:, u % 2, i * P:(i + 1) * P], g.ident[:])
                last.then_inc(transposed, 1)
                pe.wait_ge(probs_t_ready, u + 1)
                if u >= 4:
                    pe.wait_ge(out_kept, (u // 2) - 1)
                at = O_AT + (u // 2 % 2) * BANK
                for i in range(tiles):
                    last = nc.tensor.matmul(ps[p0:p0 + 64, at:at + P], v(i), probs_t[:, u % 2, i * P:(i + 1) * P],
                                            start=(i == 0), stop=(i == tiles - 1))
                last.then_inc(mixed, 1)

            scores(0)
            for u in range(n_units):
                if u + 1 < n_units:
                    scores(u + 1)
                mix(u)

        @block.vector
        def _(dve):
            own = Steps(dve, own_v)

            def maximum(u):
                n = units[u][1].shape[1]
                dve.wait_ge(scores_ready, u + 1)
                if u >= 2:
                    dve.wait_ge(exps_ready, u - 1)
                nc.vector.tensor_reduce(neg_max[:, u % 2], ps[:, (u % 2) * 1024:(u % 2) * 1024 + n], AX.X, ALU.max,
                                        negate=True).then_inc(max_ready, 1)

            def output(u):
                if u % 2 == 0:
                    return
                dve.wait_ge(mixed, u + 1)
                at = O_AT + (u // 2 % 2) * BANK
                nc.vector.tensor_copy(units[u][4], ps[:, at:at + P]).then_inc(out_kept, 1)

            maximum(0)
            for u in range(n_units):
                n = units[u][1].shape[1]
                if u + 1 < n_units:
                    maximum(u + 1)
                dve.wait_ge(exps_ready, u + 1)
                own(nc.vector.reciprocal(inverse[:, u % 2], sums[:, u % 2]))
                own.settle()
                nc.vector.tensor_scalar(probs[:, u % 2, 0:n], probs[:, u % 2, 0:n], inverse[:, u % 2], None,
                                        ALU.mult).then_inc(probs_ready, 1)
                if u >= 1:
                    output(u - 1)
            output(n_units - 1)

        @block.scalar
        def _(act):
            def exps(u):
                n = units[u][1].shape[1]
                act.wait_ge(max_ready, u + 1)
                if u >= 2:
                    act.wait_ge(transposed, u - 1)
                    act.wait_ge(probs_ready, u - 1)
                nc.scalar.activation(probs[:, u % 2, 0:n], ps[:, (u % 2) * 1024:(u % 2) * 1024 + n], ACT.Exp,
                                     bias=neg_max[:, u % 2], accum_out=sums[:, u % 2]).then_inc(exps_ready, 1)

            exps(0)
            for u in range(n_units):
                n = units[u][1].shape[1]
                if u + 1 < n_units:
                    exps(u + 1)
                act.wait_ge(transposed, u + 1)
                if u >= 2:
                    act.wait_ge(mixed, u - 1)
                nc.scalar.copy(probs_t[:, u % 2, 0:n], ps[:, T_AT:T_AT + n]).then_inc(probs_t_ready, 1)


def build(nc, d, out, until=99, keep=None):
    class G:
        pass

    g = G()
    Arena.uses.clear()
    Arena.stages = 0
    g.d, g.out = d, out
    g.keep = keep
    with ExitStack() as stack:
        a = Arena(nc, stack)
        psum = stack.enter_context(nc.psum_tensor("banks", [P, 8 * BANK], F32))
        g.ps = psum
        g.ident = a.sb("ident", [P, P])
        g.ones_d = a.sb("ones_d", [P, P])
        g.vec = a.sb("vec", [P, VEC_ROWS])
        g.ada_b = a.sb("ada_bias", [P, 96])
        g.mod = a.sb("mod", [P, 2, 48, 2])
        g.gs = a.sb("gs", [P, 2, 2, DK, 2])
        g.x_t = a.sb("x_t", [P, DK, T])
        stage_load_tokens(nc, g)
        stage_modulation(nc, g)
        if until >= 1:
            layer_even(nc, g, until)
        if until >= 8:
            layer_odd(nc, g, until)


HG_LEVELS = (64, 32, 16, 8, 4, 2, 1)
NL = len(HG_LEVELS) + 1


def stage_hgrn2_gates(nc, g, hg, forget, keep_k, cum):
    N = HG_HEADS * T
    with ExitStack() as stack:
        a = Arena(nc, stack)
        lb = a.sb("lb", [P, 5, 2, HG_HEADS])
        restart = a.sb("restart", [P, 2, T])
        gate_ready, sig_ready, f_ready, log_ready, lb_in, lb_exp, own_v, cum_done = a.sem(
            "gate_ready", "sig_ready", "f_ready", "log_ready", "lb_in", "lb_exp", "own_v", "cum_done")
        block = a.block()
        at = VEC["lb"][0]
        logits = g.vec[:, at:at + 16].rearrange("p (d e h) -> p d e h", d=2, e=2)

        @block.scalar
        def _(act):
            act.wait_ge(lb_in, 2)
            nc.scalar.activation(lb[:, 0:2], lb[:, 0:2], ACT.Exp).then_inc(lb_exp, 1)
            for d in range(2):
                nc.scalar.activation(keep_k[:, d * 4:d * 4 + 4], hg[:, 1 + d], ACT.Sigmoid).then_inc(sig_ready, 1)
            for d in range(2):
                act.wait_ge(f_ready, d + 1)
                if d:
                    act.wait_ge(cum_done, 1)
                nc.scalar.activation(forget[:], keep_k[:, d * 4:d * 4 + 4], ACT.Ln).then_inc(log_ready, 1)

        @block.vector
        def _(dve):
            own = Steps(dve, own_v)
            own(nc.vector.tensor_tensor(lb[:, 2], logits[:, :, 0], logits[:, :, 1], ALU.max))
            own.settle()
            for e in range(2):
                nc.vector.tensor_tensor(lb[:, e], logits[:, :, e], lb[:, 2], ALU.subtract).then_inc(lb_in, 1)
            for d in range(2):
                own(nc.vector.memset(restart[:, d], 1.0))
            own.settle()
            own(nc.vector.memset(restart[:, 0].rearrange("p (n t) -> p n t", t=P)[:, :, 0:1], 0.0))
            own(nc.vector.memset(restart[:, 1].rearrange("p (n t) -> p n t", t=P)[:, :, P - 1:P], 0.0))
            dve.wait_ge(lb_exp, 1)
            own(nc.vector.tensor_tensor(lb[:, 3], lb[:, 0], lb[:, 1], ALU.add))
            own.settle()
            own(nc.vector.reciprocal(lb[:, 3], lb[:, 3]))
            own.settle()
            own(nc.vector.tensor_tensor(lb[:, 4], lb[:, 0], lb[:, 3], ALU.mult))
            own.settle()
            own(nc.vector.tensor_scalar(lb[:, 3], lb[:, 4], -1.0, 1.0, ALU.mult, ALU.add))
            own.settle()
            for d in range(2):
                dve.wait_ge(sig_ready, d + 1)
                for h in range(HG_HEADS):
                    own(nc.vector.tensor_scalar(keep_k[:, d * 4 + h], keep_k[:, d * 4 + h], lb[:, 3, d, h:h + 1],
                                                lb[:, 4, d, h:h + 1], ALU.mult, ALU.add))
                own.settle()
                nc.vector.tensor_scalar(keep_k[:, d * 4:d * 4 + 4], keep_k[:, d * 4:d * 4 + 4], 1e-19, None,
                                        ALU.max).then_inc(f_ready, 1)
            for d in range(2):
                dve.wait_ge(log_ready, d + 1)
                own(nc.vector.tensor_scalar(keep_k[:, d * 4:d * 4 + 4], keep_k[:, d * 4:d * 4 + 4], -1.0, 1.0,
                                            ALU.mult, ALU.add))
                for h in range(HG_HEADS):
                    src, out = forget[:, h], cum[:, d * 4 + h]
                    if d:
                        src, out = src[:, ::-1], out[:, ::-1]
                    last = nc.vector.tensor_tensor_scan(out, restart[:, d][:, ::-1] if d else restart[:, d], src,
                                                        0.0, ALU.mult, ALU.add)
                    if h < HG_HEADS - 1:
                        own(last)
                last.then_inc(cum_done, 1)


def stage_hgrn2_scan(nc, g, hg, hg_v, keep_k, cum, y_t):
    NC = T // P
    units = [(d, h) for h in range(HG_HEADS) for d in range(2)]
    orders = [list(range(NC)), [1, 0] + list(range(NC - 1, 1, -1))]
    with ExitStack() as stack:
        a = Arena(nc, stack)
        masks = a.sb("masks", [P, NL * P])
        z = a.sb("z", [P, len(HG_LEVELS), T])
        expo = a.sb("expo", [P, 2, T])
        q_dec = a.sb("q_dec", [P, T])
        k_dec = a.sb("k_dec", [P, T])
        k_tok = a.sb("k_tok", [P, T])
        last_dec = a.sb("last_dec", [P, NC])
        state = a.sb("state", [P, 2, P])
        pairs = a.sb("pairs", [P, 2, NL * P])
        (mask_loaded, expo_in, expo_out, z_ready, dec_ready, k_turned, k_tok_ready, gram_ready, pairs_ready,
         out_ready, out_kept, update_ready, state_ready, own_v) = a.sem(
            "mask_loaded", "expo_in", "expo_out", "z_ready", "dec_ready", "k_turned", "k_tok_ready", "gram_ready",
            "pairs_ready", "out_ready", "out_kept", "update_ready", "state_ready", "own_v")
        block = a.block()
        ps = g.ps
        E = len(HG_LEVELS) + 2
        GRAM, TURN, OUT, UPD = 0, 4 * BANK, 6 * BANK, 7 * BANK

        def sides(m, x, d):
            v = x.rearrange("p (b i t) -> p b i t", i=2, t=m)
            r = v[:, :, d, m - 1:m] if d == 0 else v[:, :, d, 0:1]
            r = v[:, :, 0, m - 1:m] if d == 0 else v[:, :, 1, 0:1]
            return v[:, :, 1 - d, :], v[:, :, d, :], r.to_broadcast([P, T // (2 * m), m])

        @block.sync
        def _(sp):
            for u in range(len(units)):
                d, h = units[u]
                if u:
                    sp.wait_ge(pairs_ready, NC * u)
                sp.dma_start(masks[:], g.d["k_hg_masks"][d]).then_inc(mask_loaded, 16)

        @block.scalar
        def _(act):
            n = 0
            for u, (d, h) in enumerate(units):
                for e in range(E):
                    act.wait_ge(expo_in, u * E + e + 1)
                    nc.scalar.activation(expo[:, e % 2], expo[:, e % 2], ACT.Exp).then_inc(expo_out, 1)
                act.wait_ge(k_turned, u + 1)
                nc.scalar.copy(k_tok[:], ps[:, TURN:TURN + T]).then_inc(k_tok_ready, 1)
                for i, c in enumerate(orders[d]):
                    act.wait_ge(out_ready, u * NC + i + 1)
                    out = y_t[:, 4 + h, c * P:(c + 1) * P]
                    if d == 0:
                        nc.scalar.copy(out, ps[:, OUT:OUT + P]).then_inc(out_kept, 1)

        @block.vector
        def _(dve):
            own = Steps(dve, own_v)
            for u, (d, h) in enumerate(units):
                unit = d * 4 + h
                q, k, c = hg[:, 0, h], keep_k[:, unit], cum[:, unit]
                last_of = c.rearrange("p (n t) -> p n t", t=P)[:, :, 0:1] if d else \
                    c.rearrange("p (n t) -> p n t", t=P)[:, :, P - 1:P]

                def differences(e, u=u, c=c, d=d, last_of=last_of):
                    if e >= 2:
                        own.settle()
                    x = expo[:, e % 2]
                    if e < len(HG_LEVELS):
                        m = HG_LEVELS[e]
                        cq, ck, r = sides(m, c, d)
                        xq, xk, _ = sides(m, x, d)
                        own(nc.vector.tensor_tensor(xq, cq, r, ALU.subtract))
                        nc.vector.tensor_tensor(xk, r, ck, ALU.subtract).then_inc(expo_in, 1)
                    elif e == len(HG_LEVELS):
                        nc.vector.tensor_copy(x, c).then_inc(expo_in, 1)
                    else:
                        nc.vector.tensor_tensor(x.rearrange("p (n t) -> p n t", t=P), last_of.to_broadcast([P, NC, P]),
                                                c.rearrange("p (n t) -> p n t", t=P), ALU.subtract).then_inc(expo_in, 1)

                if u:
                    dve.wait_ge(out_ready, u * NC)
                differences(0)
                for e in range(E):
                    if e + 1 < E:
                        differences(e + 1)
                    dve.wait_ge(expo_out, u * E + e + 1)
                    x = expo[:, e % 2]
                    if e < len(HG_LEVELS):
                        m = HG_LEVELS[e]
                        xq, xk, _ = sides(m, x, d)
                        zq, zk, _ = sides(m, z[:, e], d)
                        own(nc.vector.tensor_tensor(zq, xq, sides(m, q, d)[0], ALU.mult))
                        own(nc.vector.tensor_tensor(zk, xk, sides(m, k, d)[1], ALU.mult))
                        if e == len(HG_LEVELS) - 1:
                            own.settle()
                            dve.sem_inc(z_ready, 1)
                    elif e == len(HG_LEVELS):
                        own(nc.vector.tensor_tensor(q_dec[:], x, q, ALU.mult))
                        own(nc.vector.tensor_copy(last_dec[:].unsqueeze(2),
                                                  x.rearrange("p (n t) -> p n t", t=P)[:, :, 0:1] if d else
                                                  x.rearrange("p (n t) -> p n t", t=P)[:, :, P - 1:P]))
                    else:
                        own(nc.vector.tensor_tensor(k_dec[:], x, k, ALU.mult))
                        own.settle()
                        dve.sem_inc(dec_ready, 1)

                def mask_pairs(i, u=u):
                    n = u * NC + i
                    dve.wait_ge(gram_ready, n + 1)
                    if n >= 2:
                        dve.wait_ge(out_ready, n - 1)
                    nc.vector.tensor_tensor(pairs[:, n % 2], ps[:, GRAM + (n % 2) * 1024:GRAM + (n % 2) * 1024 + 1024],
                                            masks[:], ALU.mult).then_inc(pairs_ready, 1)

                dve.wait_ge(mask_loaded, 16 * (u + 1))
                mask_pairs(0)
                for i, ch in enumerate(orders[d]):
                    n = u * NC + i
                    if i + 1 < NC:
                        mask_pairs(i + 1)
                    dve.wait_ge(update_ready, n + 1)
                    if i >= 1:
                        dve.wait_ge(state_ready, n)
                    if i == 0:
                        nc.vector.tensor_copy(state[:, i % 2], ps[:, UPD:UPD + P]).then_inc(state_ready, 1)
                    else:
                        nc.vector.scalar_tensor_tensor(out=state[:, i % 2], in0=state[:, 1 - i % 2],
                                                       scalar=last_dec[:, ch:ch + 1], in1=ps[:, UPD:UPD + P],
                                                       op0=ALU.mult, op1=ALU.add).then_inc(state_ready, 1)
                    if d == 1:
                        dve.wait_ge(out_ready, n + 1)
                        out = y_t[:, 4 + h, ch * P:(ch + 1) * P]
                        nc.vector.tensor_tensor(out, out, ps[:, OUT:OUT + P], ALU.add).then_inc(out_kept, 1)

        @block.tensor
        def _(pe):
            for u, (d, h) in enumerate(units):
                unit = d * 4 + h
                pe.wait_ge(dec_ready, u + 1)
                if u:
                    pe.wait_ge(k_tok_ready, u)
                for c in range(NC):
                    last = nc.tensor.transpose(ps[:, TURN + c * P:TURN + (c + 1) * P], k_dec[:, c * P:(c + 1) * P],
                                               g.ident[:])
                last.then_inc(k_turned, 1)

                def gram(i, u=u, d=d, h=h, unit=unit):
                    n = u * NC + i
                    t = slice(orders[d][i] * P, (orders[d][i] + 1) * P)
                    at = GRAM + (n % 2) * 1024
                    if n >= 2:
                        pe.wait_ge(pairs_ready, n - 1)
                    for e in range(len(HG_LEVELS)):
                        nc.tensor.matmul(ps[:, at + e * P:at + (e + 1) * P], z[:, e, t], z[:, e, t],
                                         start=True, stop=True)
                    e = NL - 1
                    nc.tensor.matmul(ps[:, at + e * P:at + (e + 1) * P], keep_k[:, unit, t], hg[:, 0, h, t],
                                     start=True, stop=True).then_inc(gram_ready, 1)

                pe.wait_ge(z_ready, u + 1)
                gram(0)
                pe.wait_ge(k_tok_ready, u + 1)
                for i, c in enumerate(orders[d]):
                    n = u * NC + i
                    if i + 1 < NC:
                        gram(i + 1)
                    v = hg_v[:, c, h * P:(h + 1) * P]
                    if n:
                        pe.wait_ge(state_ready, n)
                    nc.tensor.matmul(ps[:, UPD:UPD + P], k_tok[:, c * P:(c + 1) * P], v, start=True, stop=True)\
                        .then_inc(update_ready, 1)
                    pe.wait_ge(pairs_ready, n + 1)
                    if n:
                        pe.wait_ge(out_kept, n)
                    if i:
                        nc.tensor.matmul(ps[:, OUT:OUT + P], state[:, 1 - i % 2], q_dec[:, c * P:(c + 1) * P],
                                         start=True, stop=False)
                    for e in range(NL):
                        last = nc.tensor.matmul(ps[:, OUT:OUT + P], v, pairs[:, n % 2, e * P:(e + 1) * P],
                                                start=(i == 0 and e == 0), stop=(e == NL - 1))
                    last.then_inc(out_ready, 1)


def stage_hgrn2_readout(nc, g, hg, y_t):
    with ExitStack() as stack:
        a = Arena(nc, stack)
        sq = a.sb("sq", [P, HG_HEADS, T])
        silu = a.sb("silu", [P, HG_HEADS, T])
        rstd = a.sb("rstd", [P, 2, T])
        squared, summed, root_in, rooted, silu_ready, own_v, slot_free = a.sem(
            "squared", "summed", "root_in", "rooted", "silu_ready", "own_v", "slot_free")
        block = a.block()
        ps = g.ps
        gain = g.vec[:, VEC["onorm"][0]:VEC["onorm"][0] + 1]

        @block.scalar
        def _(act):
            for h in range(HG_HEADS):
                nc.scalar.activation(sq[:, h], y_t[:, 4 + h], ACT.Square).then_inc(squared, 1)
            nc.scalar.activation(silu[:], hg[:, 3], ACT.Silu).then_inc(silu_ready, 1)
            for h in range(HG_HEADS):
                act.wait_ge(root_in, h + 1)
                nc.scalar.activation(rstd[:, h % 2], rstd[:, h % 2], ACT.Sqrt).then_inc(rooted, 1)

        @block.tensor
        def _(pe):
            for h in range(HG_HEADS):
                pe.wait_ge(squared, h + 1)
                for lo, hi in halves(T):
                    last = nc.tensor.matmul(ps[:, h * 1024 + lo:h * 1024 + hi], g.ones_d[:], sq[:, h, lo:hi],
                                            start=True, stop=True)
                last.then_inc(summed, 1)

        @block.vector
        def _(dve):
            own = Steps(dve, own_v)
            dve.wait_ge(silu_ready, 1)
            for h in range(HG_HEADS):
                dve.wait_ge(summed, h + 1)
                own.settle()
                nc.vector.tensor_scalar(rstd[:, h % 2], ps[:, h * 1024:h * 1024 + T], float(D // P), EPS,
                                        ALU.mult, ALU.add).then_inc(root_in, 1)
                dve.wait_ge(rooted, h + 1)
                own(nc.vector.reciprocal(rstd[:, h % 2], rstd[:, h % 2]))
                own.settle()
                own(nc.vector.scalar_tensor_tensor(out=y_t[:, 4 + h], in0=y_t[:, 4 + h], scalar=gain,
                                                   in1=rstd[:, h % 2], op0=ALU.mult, op1=ALU.mult))
                own.settle()
                own(nc.vector.tensor_tensor(y_t[:, 4 + h], y_t[:, 4 + h], silu[:, h], ALU.mult))


def stage_mix_out(nc, g, layer, y_t, t0, w_rows):
    n = T - t0
    with ExitStack() as stack:
        a = Arena(nc, stack)
        w = a.sb("w_out", [P, DK, D])
        loaded, summed, kept = a.sem("loaded", "summed", "kept")
        block = a.block()
        ps = g.ps

        @block.sync
        def _(sp):
            for parts, k, rows in w_rows:
                sp.dma_start(w[parts, k, :], rows).then_inc(loaded, 16)

        @block.tensor
        def _(pe):
            pe.wait_ge(loaded, 16 * len(w_rows))
            for m in range(DK):
                if m >= 4:
                    pe.wait_ge(kept, m - 3)
                at = (m % 4) * 1024
                for k in range(DK):
                    for lo, hi in halves(n):
                        last = nc.tensor.matmul(ps[:, at + lo:at + hi], w[:, k, m * P:(m + 1) * P], y_t[:, k, lo:hi],
                                                start=(k == 0), stop=(k == DK - 1))
                last.then_inc(summed, 1)

        @block.vector
        def _(dve):
            for m in range(DK):
                dve.wait_ge(summed, m + 1)
                at = (m % 4) * 1024
                for s, b, e in STREAMS:
                    if e > t0:
                        b = max(b, t0)
                        last = nc.vector.scalar_tensor_tensor(
                            out=g.x_t[:, m, b:e], in0=ps[:, at + b - t0:at + e - t0],
                            scalar=g.mod[:, layer, 16 + m, s:s + 1], in1=g.x_t[:, m, b:e],
                            op0=ALU.mult, op1=ALU.add)
                last.then_inc(kept, 1)


TB = 32


def stage_split(nc, g, h_t, hi, lo):
    with ExitStack() as stack:
        a = Arena(nc, stack)
        rounded = a.sem("rounded")
        block = a.block()

        @block.scalar
        def _(act):
            for k in range(DK):
                nc.scalar.copy(hi[:, k], h_t[:, k]).then_inc(rounded, 1)

        @block.vector
        def _(dve):
            for k in range(DK):
                dve.wait_ge(rounded, k + 1)
                nc.vector.tensor_tensor(lo[:, k], h_t[:, k], hi[:, k].bitcast(F32), ALU.subtract)


def stage_scores(nc, g, layer, q_t, scores_d, n):
    NT, G2 = n // P, 2 * PEER_H
    with ExitStack() as stack:
        a = Arena(nc, stack)
        keys = a.sb("keys", [P, G2, P])
        keys_t = a.sb("keys_t", [P, G2, P])
        score = a.sb("score_out", [P, 2, G2, P])
        loaded, keys_turned, keys_ready, scored, score_ready = a.sem(
            "loaded", "keys_turned", "keys_ready", "scored", "score_ready")
        stored = [a.sem(f"stored{b}") for b in range(2)]
        block = a.block()
        ps = g.ps

        @block.sync
        def _(sp):
            sp.dma_start(keys[:], g.d["peer_keys"][layer].rearrange("h s n k -> n (h s) k")).then_inc(loaded, 16)
            for t in range(NT):
                sp.wait_ge(score_ready, t + 1)
                sp.dma_start(scores_d[t], score[:, t % 2]).then_inc(stored[t % 2], 16)
            for b in range(2):
                sp.wait_ge(stored[b], 16 * (NT // 2))

        @block.tensor
        def _(pe):
            pe.wait_ge(loaded, 16)
            for i in range(G2):
                last = nc.tensor.transpose(ps[:, i * P:(i + 1) * P], keys[:, i], g.ident[:])
            last.then_inc(keys_turned, 1)
            pe.wait_ge(keys_ready, 1)
            for t in range(NT):
                if t >= 2:
                    pe.wait_ge(score_ready, t - 1)
                at = (t % 2) * 4 * BANK
                for i in range(G2):
                    last = nc.tensor.matmul(ps[:, at + i * P:at + (i + 1) * P], q_t[:, i, t * P:(t + 1) * P],
                                            keys_t[:, i], start=True, stop=True)
                last.then_inc(scored, 1)

        @block.scalar
        def _(act):
            act.wait_ge(keys_turned, 1)
            nc.scalar.copy(keys_t[:], ps[:, 0:4 * BANK].rearrange("p (g n) -> p g n", n=P)).then_inc(keys_ready, 1)
            for t in range(NT):
                at = (t % 2) * 4 * BANK
                act.wait_ge(scored, t + 1)
                if t >= 2:
                    act.wait_ge(stored[t % 2], 16 * (t // 2))
                nc.scalar.copy(score[:, t % 2], ps[:, at:at + 4 * BANK].rearrange("p (g n) -> p g n", n=P))\
                    .then_inc(score_ready, 1)


def stage_move_x(nc, g, x_d, store):
    with ExitStack() as stack:
        a = Arena(nc, stack)
        moved = a.sem("moved")
        block = a.block()

        @block.sync
        def _(sp):
            if store:
                sp.dma_start(x_d, g.x_t[:]).then_inc(moved, 16)
            else:
                sp.dma_start(g.x_t[:], x_d).then_inc(moved, 16)
            sp.wait_ge(moved, 16)


def stage_route_and_activate(nc, g, layer, hi, lo, scores_d, acts_d, table, n):
    NT, G2 = n // P, 2 * PEER_H
    BODIES = KEYS // 2
    ROUTE_BODIES = 3 if NT > 4 else 4
    QUAD = 4
    GATE_BODIES = n // TB
    cols = halves(n)
    u_rows = g.d["peer_u"][layer].rearrange("(a b) d -> a b d", b=KEYS)
    with ExitStack() as stack:
        a = Arena(nc, stack)
        room = g.x_t[:].rearrange("p k t -> p (k t)")
        score = room[:, 0:2048].rearrange("p (g n) -> p g n", n=P)
        rest = room[:, 2048:4096].rearrange("p (g n) -> p g n", n=P)
        cand = room[:, 4096:6144].rearrange("p (h c) -> p h c", h=PEER_H)
        cand_rest = room[:, 2048:4096].rearrange("p (h c) -> p h c", h=PEER_H)
        hot = room[:, 4096:6144].rearrange("p (s a) -> p s a", a=TOPK)
        best = a.sb("best", [P, G2, TOPK])
        best_at = a.sb("best_at", [P, G2, TOPK], U32)
        best_key = a.sb("best_key", [P, G2, TOPK])
        top = a.sb("top", [P, PEER_H, TOPK])
        top_at = a.sb("top_at", [P, PEER_H, TOPK], U32)
        pick = a.sb("pick", [P, 2, SLOTS], U32)
        pick_f = a.sb("pick_f", [P, 2, SLOTS])
        found = a.sb("found", [P, 3, SLOTS])
        iota = a.sb("iota", [P, P])
        head_ones = a.sb("head_ones", [P, P])
        slots = a.sb("slots", [P, 4, n])
        w_hi = a.sb("slot_hi", [P, n], F32R)
        first_hot = a.sb("first_hot", [P, 2, QUAD, P], F32R)
        hot_hi = a.sb("hot_hi", [P, 2, QUAD, P], F32R)
        hot_lo = a.sb("hot_lo", [P, 2, QUAD, P], F32R)
        part = a.sb("part", [P, 2, P, TB])
        u_raw = a.sb("u_raw", [P, 2, D])
        u_hi = a.sb("u_hi", [P, 2, D], F32R)
        u_lo = a.sb("u_lo", [P, 2, D], F32R)
        ut_hi = a.sb("ut_hi", [P, 2, D], F32R)
        ut_lo = a.sb("ut_lo", [P, 2, D], F32R)
        acts = a.sb("acts", [P, 2, n])
        ident_r = a.sb("ident_r", [P, P], F32R)

        def two(name):
            return [a.sem(f"{name}{r}") for r in range(2)]

        u_loaded, u_hi_ready, u_lo_ready, turned, ut_ready, acted, gelued, acts_stored = map(
            two, ("u_loaded", "u_hi_ready", "u_lo_ready", "turned", "ut_ready", "acted", "gelued", "acts_stored"))
        hot_ready, multiplied, kept, part_stored = map(two, ("hot_ready", "multiplied", "kept", "part_stored"))
        (loaded, ident_ready, score_loaded, score_used, found_ready, found_turned, found_used, soft_ready,
         soft_summed, own_v) = a.sem(
            "loaded", "ident_ready", "score_loaded", "score_used", "found_ready", "found_turned", "found_used",
            "soft_ready", "soft_summed", "own_v")
        block = a.block()
        ps = g.ps
        TURN_HI, TURN_LO, ACTS, GATE = 0, 2 * BANK, 4 * BANK, 6 * BANK

        def nothing(*_):
            pass

        def segments(engine, body, after_tile=nothing, after_soft=nothing, after_gates=nothing):
            body(0, None, True, False)
            body(1, None, False, False)
            at = 1
            for t in range(NT):
                with engine.Fori(at + (t == 0), at + ROUTE_BODIES) as i:
                    body(i, None, False, False)
                at += ROUTE_BODIES
                after_tile(t)
            body(at, None, False, False)
            after_soft()
            body(at + 1, None, False, False)
            at += 2
            for r in range(2):
                body(at + r, (r, r, 0, True), False, False)
            with engine.Fori(1, GATE_BODIES // 2) as i:
                for r in range(2):
                    body(i * 2 + (at + r), (i * 2 + r, r, i, False), False, False)
            at += GATE_BODIES
            after_gates()
            with engine.Fori(at, BODIES - 1) as i:
                body(i, None, False, False)
            body(BODIES - 1, None, False, True)

        @block.sync
        def _(sp):
            sp.dma_start(iota[:], g.d["k_iota"]).then_inc(loaded, 16)
            sp.dma_start(head_ones[:], g.d["k_head_ones"]).then_inc(loaded, 16)
            sp.dma_start(score, scores_d[0]).then_inc(score_loaded, 16)

            def load(r, i):
                sp.dma_start(u_raw[:, r:r + 1], u_rows[:, bass.ds(i * 2 + r, 1), :]).then_inc(u_loaded[r], 16)

            def store(r, i):
                sp.wait_ge(gelued[r], i + 1)
                sp.dma_start(acts_d[bass.ds(i * 2 + r, 1)].rearrange("o p n -> (o p) n"), acts[:, r])\
                    .then_inc(acts_stored[r], 16)

            def store_part(r, index):
                for b in range(2):
                    sp.wait_ge(kept[b], index * 4 + 4)
                sp.dma_start(table[:, bass.ds(index, 1)], part[:, r:r + 1]).then_inc(part_stored[r], 16)

            def body(i, gate, first, last):
                if not last:
                    sp.wait_ge(u_lo_ready[0], i + 1)
                    load(0, i + 1)
                if not first:
                    store(1, i - 1)
                if not last:
                    sp.wait_ge(u_lo_ready[1], i + 1)
                    load(1, i + 1)
                store(0, i)
                if gate and not (gate[3] and gate[1] == 0):
                    store_part(1 - gate[1], gate[0] - 1)
                if last:
                    store(1, i)

            def next_scores(t):
                if t + 1 < NT:
                    sp.wait_ge(score_used, t + 1)
                    sp.dma_start(score, scores_d[t + 1]).then_inc(score_loaded, 16)

            load(0, 0)
            load(1, 0)
            segments(sp, body, after_tile=next_scores, after_gates=lambda: store_part(1, GATE_BODIES - 1))
            for r in range(2):
                sp.wait_ge(acts_stored[r], 16 * BODIES)
                sp.wait_ge(part_stored[r], 16 * (GATE_BODIES // 2))

        @block.tensor
        def _(pe):
            def turn(r, i, first=False):
                pe.wait_ge(u_lo_ready[r], i + 1)
                if not first:
                    pe.wait_ge(ut_ready[1 - r], i + 1 - (1 - r))
                for at, u in ((TURN_HI, u_hi), (TURN_LO, u_lo)):
                    for k in range(DK):
                        last = nc.tensor.transpose(ps[:, at + k * P:at + (k + 1) * P].bitcast(F32R),
                                                   u[:, r, k * P:(k + 1) * P], ident_r[:])
                last.then_inc(turned[r], 1)

            def octet(index, start=False):
                for b in range(2):
                    pe.wait_ge(hot_ready[b], index + 1)
                    if not start:
                        pe.wait_ge(kept[b], index)
                    for q in range(QUAD):
                        out = ps[:, GATE + b * BANK + q * P:GATE + b * BANK + (q + 1) * P]
                        nc.tensor.matmul(out, first_hot[:, b, q], hot_hi[:, b, q], start=True, stop=False)
                        last = nc.tensor.matmul(out, first_hot[:, b, q], hot_lo[:, b, q], start=False, stop=True)
                    last.then_inc(multiplied[b], 1)

            def products(r, ks):
                for k in ks:
                    for u, h in ((ut_hi, hi), (ut_hi, lo), (ut_lo, hi)):
                        for b, e in cols:
                            last = nc.tensor.matmul(ps[:, ACTS + b:ACTS + e], u[:, r, k * P:(k + 1) * P], h[:, k, b:e],
                                                    start=(k == 0 and u is ut_hi and h is hi),
                                                    stop=(k == DK - 1 and u is ut_lo))
                return last

            def body(i, gate, first, last):
                for r in range(2):
                    if r == 0:
                        turn(1, i)
                    elif not last:
                        turn(0, i + 1)
                    if gate:
                        octet(gate[0] * 4 + 2 * r, start=gate[3] and gate[1] == 0 and r == 0)
                    pe.wait_ge(ut_ready[r], i + 1)
                    if not (first and r == 0):
                        pe.wait_ge(gelued[1 - r], i + 1 - (1 - r))
                    products(r, range(0, 4))
                    if gate:
                        octet(gate[0] * 4 + 2 * r + 1)
                    products(r, range(4, DK)).then_inc(acted[r], 1)

            def turn_found(t):
                pe.wait_ge(found_ready, t + 1)
                if t:
                    pe.wait_ge(found_used, t)
                for i in range(3):
                    last = nc.tensor.transpose(ps[:, GATE + i * P:GATE + (i + 1) * P], found[:, i], g.ident[:])
                last.then_inc(found_turned, 1)

            def sum_heads():
                pe.wait_ge(soft_ready, 1)
                for b, e in cols:
                    last = nc.tensor.matmul(ps[:, GATE + b:GATE + e], head_ones[:], slots[:, 2, b:e],
                                            start=True, stop=True)
                last.then_inc(soft_summed, 1)

            pe.wait_ge(ident_ready, 1)
            pe.wait_ge(loaded, 32)
            turn(0, 0, True)
            segments(pe, body, after_tile=turn_found, after_soft=sum_heads)

        @block.scalar
        def _(act):
            def round_u(r, i, first=False):
                act.wait_ge(u_loaded[r], (i + 1) * 16)
                if not first:
                    act.wait_ge(turned[r], i)
                nc.scalar.copy(u_hi[:, r], u_raw[:, r]).then_inc(u_hi_ready[r], 1)

            def turned_out(r, i, first=False):
                act.wait_ge(turned[r], i + 1)
                if not first:
                    act.wait_ge(acted[r], i)
                nc.scalar.copy(ut_hi[:, r], ps[:, TURN_HI:TURN_HI + D])
                nc.scalar.copy(ut_lo[:, r], ps[:, TURN_LO:TURN_LO + D]).then_inc(ut_ready[r], 1)

            def gelu(r, i, first=False):
                act.wait_ge(acted[r], i + 1)
                if not first:
                    act.wait_ge(acts_stored[r], i * 16)
                nc.scalar.activation(acts[:, r], ps[:, ACTS:ACTS + n], ACT.Gelu).then_inc(gelued[r], 1)

            def gates_out(gate, octet):
                for b in range(2):
                    act.wait_ge(multiplied[b], gate[0] * 4 + octet + 1)
                    t = (2 * octet + b) * QUAD
                    nc.scalar.copy(part[:, gate[1], :, t:t + QUAD],
                                   ps[:, GATE + b * BANK:GATE + (b + 1) * BANK].rearrange("p (t m) -> p m t", m=P))\
                        .then_inc(kept[b], 1)

            def body(i, gate, first, last):
                for r in range(2):
                    if r == 0:
                        if not first:
                            gelu(1, i - 1, isinstance(i, int) and i == 1)
                    else:
                        gelu(0, i, first)
                    if gate:
                        if r == 0 and not gate[3]:
                            act.wait_ge(part_stored[gate[1]], gate[2] * 16)
                        gates_out(gate, 2 * r)
                    if r == 0:
                        turned_out(1, i, first)
                    elif not last:
                        turned_out(0, i + 1)
                    if gate:
                        gates_out(gate, 2 * r + 1)
                    if not last:
                        round_u(r, i + 1)
                if last:
                    gelu(1, i)

            def keep_found(t):
                act.wait_ge(found_turned, t + 1)
                nc.scalar.copy(slots[:, 0:3, t * P:(t + 1) * P],
                               ps[:, GATE:GATE + 3 * P].rearrange("p (i t) -> p i t", t=P)).then_inc(found_used, 1)
                if t == NT - 1:
                    act.wait_ge(found_used, NT)
                    nc.scalar.activation(slots[:, 2], slots[:, 2], ACT.Exp).then_inc(soft_ready, 1)

            act.wait_ge(loaded, 32)
            nc.scalar.copy(ident_r[:], g.ident[:]).then_inc(ident_ready, 1)
            round_u(0, 0, True)
            round_u(1, 0, True)
            turned_out(0, 0, True)
            segments(act, body, after_tile=keep_found)

        @block.gpsimd
        def _(pool):
            def body(i):
                for r in range(2):
                    pool.wait_ge(u_hi_ready[r], i + 1)
                    nc.gpsimd.tensor_tensor(u_lo[:, r], u_raw[:, r], u_hi[:, r].bitcast(F32), ALU.subtract)\
                        .then_inc(u_lo_ready[r], 1)

            body(0)
            with pool.Fori(1, BODIES) as i:
                body(i)

        @block.vector
        def _(dve):
            own = Steps(dve, own_v)

            def sixteen(values, without, out, at, groups):
                for i in range(groups):
                    own(nc.vector.max(out[:, i, 0:8], values[:, i]))
                own.settle()
                for i in range(groups):
                    own(nc.vector.match_replace(without[:, i], out[:, i, 0:8], values[:, i], LOWEST))
                    own(nc.vector.max_index(at[:, i, 0:8], out[:, i, 0:8], values[:, i]))
                own.settle()
                for i in range(groups):
                    own(nc.vector.max(out[:, i, 8:16], without[:, i]))
                own.settle()
                for i in range(groups):
                    own(nc.vector.max_index(at[:, i, 8:16], out[:, i, 8:16], without[:, i]))
                own.settle()

            dve.wait_ge(loaded, 32)
            for t in range(NT):
                dve.wait_ge(score_loaded, 16 * (t + 1))
                sixteen(score, rest, best, best_at, G2)
                dve.sem_inc(score_used, 1)
                own(nc.vector.tensor_copy(best_key[:], best_at[:]))
                sides = best[:].rearrange("p (h s) k -> p h s k", s=2)
                own(nc.vector.tensor_tensor(cand.rearrange("p h (a b) -> p h a b", a=TOPK),
                                            sides[:, :, 0, :].unsqueeze(3).to_broadcast([P, PEER_H, TOPK, TOPK]),
                                            sides[:, :, 1, :].unsqueeze(2).to_broadcast([P, PEER_H, TOPK, TOPK]),
                                            ALU.add))
                own.settle()
                sixteen(cand, cand_rest, top, top_at, PEER_H)
                at = top_at[:].rearrange("p h k -> p (h k)")
                own(nc.vector.tensor_scalar(pick[:, 0], at, 4, None, ALU.logical_shift_right))
                own(nc.vector.tensor_scalar(pick[:, 1], at, 15, None, ALU.bitwise_and))
                own.settle()
                own(nc.vector.tensor_copy(pick_f[:], pick[:]))
                if t:
                    dve.wait_ge(found_turned, t)
                own(nc.vector.tensor_tensor(found[:, 2].rearrange("p (h k) -> p h k", h=PEER_H), top[:],
                                            top[:, :, 0:1].to_broadcast([P, PEER_H, TOPK]), ALU.subtract))
                own.settle()
                keys_of = best_key[:].rearrange("p (h s) k -> p h s k", s=2)
                for i in range(2):
                    own(nc.vector.tensor_tensor(hot, pick_f[:, i].unsqueeze(2).to_broadcast([P, SLOTS, TOPK]),
                                                iota[:, 0:TOPK].unsqueeze(1).to_broadcast([P, SLOTS, TOPK]),
                                                ALU.is_equal))
                    own.settle()
                    h4 = hot.rearrange("p (h k) a -> p h k a", h=PEER_H)
                    own(nc.vector.tensor_tensor(h4, h4, keys_of[:, :, i, :].unsqueeze(2)
                                                .to_broadcast([P, PEER_H, TOPK, TOPK]), ALU.mult))
                    own.settle()
                    own(nc.vector.tensor_reduce(found[:, i], hot, AX.X, ALU.add))
                    own.settle()
                dve.sem_inc(found_ready, 1)

            dve.wait_ge(soft_summed, 1)
            own(nc.vector.reciprocal(slots[:, 3], ps[:, GATE:GATE + n]))
            own.settle()
            own(nc.vector.tensor_tensor(slots[:, 2], slots[:, 2], slots[:, 3], ALU.mult))
            own.settle()
            own(nc.vector.tensor_copy(w_hi[:], slots[:, 2]))
            own.settle()
            own(nc.vector.tensor_tensor(slots[:, 3], slots[:, 2], w_hi[:].bitcast(F32), ALU.subtract))
            own.settle()
            own(nc.vector.tensor_copy(slots[:, 2], w_hi[:].bitcast(F32)))
            own.settle()

            def octet(i, first):
                for b in range(2):
                    if not first:
                        dve.wait_ge(multiplied[b], i)
                    for q in range(QUAD):
                        t = i * (2 * QUAD) + (b * QUAD + q)
                        key, w0, w1 = (slots[:, c, bass.ds(t, 1)] for c in (1, 2, 3))
                        nc.vector.tensor_scalar(first_hot[:, b, q], iota[:], slots[:, 0, bass.ds(t, 1)], None,
                                                ALU.is_equal)
                        nc.vector.tensor_scalar(hot_hi[:, b, q], iota[:], key, w0, ALU.is_equal, ALU.mult)
                        last = nc.vector.tensor_scalar(hot_lo[:, b, q], iota[:], key, w1, ALU.is_equal, ALU.mult)
                    last.then_inc(hot_ready[b], 1)

            octet(0, True)
            with dve.Fori(1, n // (2 * QUAD)) as i:
                octet(i, False)


def stage_mix_experts(nc, g, layer, acts_d, table, n, spans):
    GROUP = 4
    BODIES = KEYS // GROUP // 2
    BANKS = 4
    v_rows = g.d["peer_v"][layer].rearrange("(a b) d -> a b d", b=KEYS)
    Y_UNITS = [(m, s) for m in range(DK) for s in range(len(spans))]
    PER = len(Y_UNITS) // BANKS
    with ExitStack() as stack:
        a = Arena(nc, stack)
        v_raw = a.sb("v_raw", [P, GROUP, D])
        v_hi = a.sb("v_hi", [P, 2, GROUP, D], F32R)
        v_lo = a.sb("v_lo", [P, 2, GROUP, D], F32R)
        gates = a.sb("gates", [P, 2, n // TB, GROUP, TB])
        acts = a.sb("acts_in", [P, GROUP, n])
        w_hi = a.sb("w_hi", [P, 2, GROUP, n], F32R)
        w_lo = a.sb("w_lo", [P, 2, GROUP, n], F32R)

        def two(name):
            return [a.sem(f"{name}{q}") for q in range(2)]

        v_loaded, gates_loaded, acts_loaded, v_hi_ready, v_lo_ready, weighted, w_hi_ready, w_lo_ready = map(
            two, ("v_loaded", "gates_loaded", "acts_loaded", "v_hi_ready", "v_lo_ready", "weighted", "w_hi_ready",
                  "w_lo_ready"))
        y_done = [a.sem(f"y_done{b}") for b in range(BANKS)]
        y_added = [a.sem(f"y_added{b}") for b in range(BANKS)]
        block = a.block()
        ps = g.ps

        def bodies(engine, emit):
            emit(0, True, False)
            with engine.Fori(1, BODIES - 1) as i:
                emit(i, False, False)
            emit(BODIES - 1, False, True)

        def before(q, i):
            return (0, i + 1) if q else (1, i)

        @block.sync
        def _(sp):
            def body(i, first, last):
                for q in range(2):
                    at = i * (2 * GROUP) + q * GROUP
                    b, count = before(q, i)
                    start = first and q == 0
                    if not start:
                        sp.wait_ge(v_lo_ready[b], count)
                    sp.dma_start(v_raw[:], v_rows[:, bass.ds(at, GROUP), :]).then_inc(v_loaded[q], 16)
                    if not first:
                        sp.wait_ge(weighted[q], i * GROUP)
                    sp.dma_start(gates[:, q], table[:, :, bass.ds(at, GROUP), :]).then_inc(gates_loaded[q], 16)
                    if not start:
                        sp.wait_ge(w_lo_ready[b], count * GROUP)
                    sp.dma_start(acts[:], acts_d[bass.ds(at, GROUP)].rearrange("s p t -> p s t"))\
                        .then_inc(acts_loaded[q], 16)

            bodies(sp, body)

        @block.scalar
        def _(act):
            def body(i, first, last):
                for q in range(2):
                    act.wait_ge(v_loaded[q], (i + 1) * 16)
                    if not first:
                        act.wait_ge(y_done[BANKS - 1], i * (2 * PER) + (q + 1) * PER - 2 * PER)
                    nc.scalar.copy(v_hi[:, q], v_raw[:]).then_inc(v_hi_ready[q], 1)

            bodies(act, body)

        @block.gpsimd
        def _(pool):
            def body(i, first, last):
                for q in range(2):
                    pool.wait_ge(v_hi_ready[q], i + 1)
                    nc.gpsimd.tensor_tensor(v_lo[:, q], v_raw[:], v_hi[:, q].bitcast(F32), ALU.subtract)\
                        .then_inc(v_lo_ready[q], 1)

            bodies(pool, body)

        @block.vector
        def _(dve):
            def weigh(q, i, first):
                dve.wait_ge(acts_loaded[q], (i + 1) * 16)
                dve.wait_ge(gates_loaded[q], (i + 1) * 16)
                for r in range(GROUP):
                    x = acts[:, r].rearrange("p (b t) -> p b t", t=TB)
                    nc.vector.tensor_tensor(x, x, gates[:, q, :, r, :], ALU.mult).then_inc(weighted[q], 1)
                if not first:
                    dve.wait_ge(y_done[BANKS - 1], i * (2 * PER) + (q + 1) * PER - 2 * PER)
                for r in range(GROUP):
                    dve.wait_ge(weighted[q], i * GROUP + r + 1)
                    nc.vector.tensor_copy(w_hi[:, q, r], acts[:, r]).then_inc(w_hi_ready[q], 1)
                for r in range(GROUP):
                    dve.wait_ge(w_hi_ready[q], i * GROUP + r + 1)
                    nc.vector.tensor_tensor(w_lo[:, q, r], acts[:, r], w_hi[:, q, r].bitcast(F32), ALU.subtract)\
                        .then_inc(w_lo_ready[q], 1)

            def add(q, i):
                for c, (m, s) in enumerate(Y_UNITS):
                    b, e, t, stream = spans[s]
                    bank = c % BANKS
                    dve.wait_ge(y_done[bank], i * (2 * PER) + (q * PER + c // BANKS + 1))
                    x = g.x_t[:, m, t:t + e - b]
                    nc.vector.scalar_tensor_tensor(out=x, in0=ps[:, bank * BANK:bank * BANK + e - b],
                                                   scalar=g.mod[:, layer, 40 + m, stream:stream + 1], in1=x,
                                                   op0=ALU.mult, op1=ALU.add).then_inc(y_added[bank], 1)

            def body(i, first, last):
                weigh(1, i, first)
                add(0, i)
                if not last:
                    weigh(0, i + 1, False)
                add(1, i)

            weigh(0, 0, True)
            bodies(dve, body)

        @block.tensor
        def _(pe):
            def body(i, first, last):
                for q in range(2):
                    pe.wait_ge(v_lo_ready[q], i + 1)
                    pe.wait_ge(w_lo_ready[q], (i + 1) * GROUP)
                    for c, (m, s) in enumerate(Y_UNITS):
                        b, e, _, _ = spans[s]
                        bank = c % BANKS
                        if not (first and q == 0 and c < BANKS):
                            pe.wait_ge(y_added[bank], i * (2 * PER) + (q * PER + c // BANKS))
                        for r in range(GROUP):
                            for v, w in ((v_hi, w_hi), (v_hi, w_lo), (v_lo, w_hi)):
                                last_mm = nc.tensor.matmul(ps[:, bank * BANK:bank * BANK + e - b],
                                                           v[:, q, r, m * P:(m + 1) * P], w[:, q, r, b:e],
                                                           start=(r == 0 and v is v_hi and w is w_hi),
                                                           stop=(r == GROUP - 1 and v is v_lo))
                        last_mm.then_inc(y_done[bank], 1)

            bodies(pe, body)


def stage_rms_channels(nc, g, x, kc, gain, factor=1.0):
    n = x.shape[2]
    with ExitStack() as stack:
        a = Arena(nc, stack)
        sq = a.sb("sq", [P, kc, n])
        rstd = a.sb("rstd", [P, n])
        squared, summed, root_in, rooted, own_v = a.sem("squared", "summed", "root_in", "rooted", "own_v")
        block = a.block()
        ps = g.ps

        @block.scalar
        def _(act):
            for k in range(kc):
                nc.scalar.activation(sq[:, k], x[:, k], ACT.Square).then_inc(squared, 1)
            act.wait_ge(root_in, 1)
            nc.scalar.activation(rstd[:], rstd[:], ACT.Sqrt).then_inc(rooted, 1)

        @block.tensor
        def _(pe):
            for k in range(kc):
                pe.wait_ge(squared, k + 1)
                for lo, hi in halves(n):
                    last = nc.tensor.matmul(ps[:, lo:hi], g.ones_d[:], sq[:, k, lo:hi],
                                            start=(k == 0), stop=(k == kc - 1))
            last.then_inc(summed, 1)

        @block.vector
        def _(dve):
            own = Steps(dve, own_v)
            dve.wait_ge(summed, 1)
            nc.vector.tensor_scalar(rstd[:], ps[:, 0:n], D / (kc * P), EPS, ALU.mult, ALU.add).then_inc(root_in, 1)
            dve.wait_ge(rooted, 1)
            own(nc.vector.reciprocal(rstd[:], rstd[:]))
            own.settle()
            if factor != 1.0:
                own(nc.vector.tensor_scalar(rstd[:], rstd[:], factor, None, ALU.mult))
                own.settle()
            for k in range(kc):
                own(nc.vector.scalar_tensor_tensor(out=x[:, k], in0=x[:, k], scalar=gain[:, k:k + 1], in1=rstd[:],
                                                   op0=ALU.mult, op1=ALU.mult))


def stage_mla_heads(nc, g, q_a, kv_a, k_rope, q_t, k_t, v_tok):
    QH, KH = MLA_NOPE + MLA_ROPE, MLA_NOPE + MLA_V
    NQ, NK = MLA_QR // P, MLA_KVR // P
    with ExitStack() as stack:
        a = Arena(nc, stack)
        w_q = a.sb("w_qup", [P, NQ, MLA_H * QH])
        w_kv = a.sb("w_kvup", [P, NK, MLA_H * KH])
        q_rope = a.sb("q_rope", [MLA_ROPE, MLA_H, LAT])
        rope = a.sb("rope", [MLA_ROPE, 2, LAT])
        swap = a.sb("swap", [MLA_ROPE, MLA_ROPE])
        direct_cos = a.sb("direct_cos", [MLA_ROPE, 2, LAT])
        swapped_sin = a.sb("swapped_sin", [MLA_ROPE, 2, LAT])
        k_turned = a.sb("k_turned", [MLA_ROPE, T])
        loaded, product, kept, swapped, swap_free, k_ready, own_v = a.sem(
            "loaded", "product", "kept", "swapped", "swap_free", "k_ready", "own_v")
        block = a.block()
        ps = g.ps
        SWAP = 6 * BANK
        units = []
        for h in range(MLA_H):
            units.append(([(w_q[:, k, h * QH:h * QH + 64], q_a[:, k, :]) for k in range(NQ)], 64, LAT,
                          q_t[0:64, h, :]))
            units.append(([(w_q[:, k, h * QH + 64:(h + 1) * QH], q_a[:, k, :]) for k in range(NQ)], MLA_ROPE, LAT,
                          q_rope[:, h, :]))
            units.append(([(w_kv[:, k, h * KH:h * KH + 64], kv_a[:, k, :]) for k in range(NK)], 64, T,
                          k_t[0:64, h, :]))
        for t in range(T // P):
            values = [w_kv[:, k].rearrange("p (h c) -> p h c", c=KH)[:, :, MLA_NOPE:] for k in range(NK)]
            units.append(([(kv_a[:, k, t * P:(t + 1) * P], values[k]) for k in range(NK)], P, 512, v_tok[:, t, :]))

        @block.sync
        def _(sp):
            sp.dma_start(w_q[:], g.d["mla_w_qup"][0].rearrange("(k p) n -> p k n", p=P)).then_inc(loaded, 16)
            sp.dma_start(w_kv[:], g.d["mla_w_kvup"][0].rearrange("(k p) n -> p k n", p=P)).then_inc(loaded, 16)
            sp.dma_start(rope[:], g.d["k_rope_mla"]).then_inc(loaded, 16)
            sp.dma_start(swap[:], g.d["k_rope_swap"]).then_inc(loaded, 16)

        @block.tensor
        def _(pe):
            pe.wait_ge(loaded, 64)
            for u, (pairs, m, n, _) in enumerate(units):
                at = (u % 3) * 1024
                if u >= 3:
                    pe.wait_ge(kept, u - 2)
                for i, (left, right) in enumerate(pairs):
                    if len(right.shape) == 3:
                        last = nc.tensor.matmul(ps[0:m, at:at + n], left, right, start=(i == 0),
                                                stop=(i == len(pairs) - 1))
                    else:
                        for lo, hi in halves(n):
                            last = nc.tensor.matmul(ps[0:m, at + lo:at + hi], left, right[:, lo:hi], start=(i == 0),
                                                    stop=(i == len(pairs) - 1))
                last.then_inc(product, 1)
            pe.wait_ge(kept, len(units))
            for h in range(MLA_H + 1):
                if h >= 2:
                    pe.wait_ge(swap_free, h - 1)
                x = q_rope[:, h, :] if h < MLA_H else k_rope[:, CTX:T]
                nc.tensor.matmul(ps[0:MLA_ROPE, SWAP + (h % 2) * BANK:SWAP + (h % 2 + 1) * BANK], swap[:], x,
                                 start=True, stop=True).then_inc(swapped, 1)

        @block.scalar
        def _(act):
            for u, (pairs, m, n, out) in enumerate(units):
                act.wait_ge(product, u + 1)
                nc.scalar.copy(out, ps[0:m, (u % 3) * 1024:(u % 3) * 1024 + n]).then_inc(kept, 1)
            act.wait_ge(k_ready, 1)
            for h in range(MLA_H):
                nc.scalar.copy(k_t[64:96, h, :], k_turned[:])

        @block.vector
        def _(dve):
            own = Steps(dve, own_v)
            dve.wait_ge(kept, len(units))
            dve.wait_ge(loaded, 64)
            for h in range(MLA_H + 1):
                x = q_rope[:, h, :] if h < MLA_H else k_rope[:, CTX:T]
                out = q_t[64:96, h, :] if h < MLA_H else k_turned[:, CTX:T]
                own(nc.vector.tensor_tensor(direct_cos[:, h % 2], x, rope[:, 0], ALU.mult))
                dve.wait_ge(swapped, h + 1)
                nc.vector.tensor_tensor(swapped_sin[:, h % 2], rope[:, 1],
                                        ps[0:MLA_ROPE, SWAP + (h % 2) * BANK:SWAP + (h % 2 + 1) * BANK],
                                        ALU.mult).then_inc(swap_free, 1)
                dve.wait_ge(swap_free, h + 1)
                own.settle()
                own(nc.vector.tensor_tensor(out, direct_cos[:, h % 2], swapped_sin[:, h % 2], ALU.add))
            own(nc.vector.tensor_copy(k_turned[:, 0:CTX], k_rope[:, 0:CTX]))
            own.settle()
            dve.sem_inc(k_ready, 1)


S5_TILES = S5_G // 2
TWO_PI = 6.283185
ROUND = 1.5 * 2.0 ** 23


def stage_s5_parameters(nc, g, rate, turns, b_t, c_t):
    N = 2 * S5_TILES
    with ExitStack() as stack:
        a = Arena(nc, stack)
        rows = a.sb("s5_rows", [3 * N, P])
        dt_rows = a.sb("dt_rows", [3 * N, 2])
        par = a.sb("par", [P, 3, N])
        f = a.sb("s5_f", [P, 12, N])
        b_nat = a.sb("b_nat", [P, 2, N, S5_C])
        b_eff = a.sb("b_eff", [P, 2, N, S5_C])
        tmp = a.sb("tmp", [P, N, S5_C])
        c_nat = a.sb("c_nat", [P, 2, 8, S5_P])
        b_mask = a.sb("b_mask", [P, 4, 8])
        c_mask = a.sb("c_mask", [P, 8])
        padded = a.sb("padded", [P, 2, 4, P])
        loaded, spread, turned, par_ready, trig_in, trig_out, own_v, pad_ready, pad_turned, pad_kept = a.sem(
            "loaded", "spread", "turned", "par_ready", "trig_in", "trig_out", "own_v", "pad_ready", "pad_turned",
            "pad_kept")
        block = a.block()
        ps = g.ps
        jobs = [(m, part, d, j) for m in "bc" for part in range(2) for d in range(2) for j in range(4)]

        @block.sync
        def _(sp):
            d = g.d
            sp.dma_start(rows[0:N, :], d["s5_a_re"][0].rearrange("d (i g) p -> (d i) (g p)", g=2)).then_inc(loaded, 16)
            sp.dma_start(rows[N:2 * N, :], d["s5_a_im"][0].rearrange("d (i g) p -> (d i) (g p)", g=2))\
                .then_inc(loaded, 16)
            sp.dma_start(dt_rows[2 * N:3 * N, :], d["s5_log_dt"][0].rearrange("d (i g) -> (d i) g", g=2))\
                .then_inc(loaded, 16)
            sp.dma_start(b_mask[:], d["k_s5_bmask"]).then_inc(loaded, 16)
            sp.dma_start(c_mask[:], d["k_s5_cmask"]).then_inc(loaded, 16)
            for part, name in enumerate(("s5_b_re", "s5_b_im")):
                for dr in range(2):
                    src = d[name][0, dr].rearrange("(i g) p c -> (g p) i c", g=2)
                    sp.dma_start(b_nat[:, part, dr * S5_TILES:(dr + 1) * S5_TILES, :], src).then_inc(loaded, 16)
            for part, name in enumerate(("s5_c_re", "s5_c_im")):
                for dr in range(2):
                    src = d[name][0, dr].rearrange("(j g) c p -> (g c) j p", g=8)
                    sp.dma_start(c_nat[:, part, dr * 4:(dr + 1) * 4, :], src).then_inc(loaded, 16)

        n_loads = 16 * 13

        @block.tensor
        def _(pe):
            pe.wait_ge(spread, 1)
            nc.tensor.transpose(ps[:, 0:3 * N], rows[:], g.ident[:3 * N, :3 * N]).then_inc(turned, 1)
            for n in range(len(jobs)):
                pe.wait_ge(pad_ready, n + 1)
                if n >= 2:
                    pe.wait_ge(pad_kept, n - 1)
                at = (2 + n % 2) * BANK
                for i in range(4):
                    last = nc.tensor.transpose(ps[:, at + i * P:at + (i + 1) * P], padded[:, n % 2, i], g.ident[:])
                last.then_inc(pad_turned, 1)

        @block.scalar
        def _(act):
            act.wait_ge(par_ready, 1)
            nc.scalar.activation(f[:, 0], par[:, 2], ACT.Exp).then_inc(trig_out, 1)
            act.wait_ge(trig_in, 1)
            nc.scalar.activation(rate[:], f[:, 1], ACT.Exp).then_inc(trig_out, 1)
            nc.scalar.activation(f[:, 4], turns[:], ACT.Sin, scale=TWO_PI).then_inc(trig_out, 1)
            nc.scalar.activation(f[:, 5], turns[:], ACT.Sin, scale=TWO_PI / 2).then_inc(trig_out, 1)
            for n, (m, part, d, j) in enumerate(jobs):
                act.wait_ge(pad_turned, n + 1)
                src = ps[:, (2 + n % 2) * BANK:(3 + n % 2) * BANK].rearrange("p (i n) -> p i n", i=4)
                tiles = slice(d * S5_TILES + 4 * j, d * S5_TILES + 4 * j + 4)
                if m == "b":
                    nc.scalar.copy(b_t[:, part, tiles, :], src).then_inc(pad_kept, 1)
                elif part == 0:
                    nc.scalar.copy(c_t[:, 0, tiles, :], src)
                    nc.scalar.mul(c_t[:, 1, tiles, :], src, -1.0).then_inc(pad_kept, 1)
                else:
                    nc.scalar.mul(c_t[:, 2, tiles, :], src, -1.0).then_inc(pad_kept, 1)

        @block.vector
        def _(dve):
            own = Steps(dve, own_v)
            dve.wait_ge(loaded, n_loads)
            nc.vector.tensor_copy(rows[2 * N:3 * N, :].rearrange("r (g p) -> r g p", g=2),
                                  dt_rows[2 * N:3 * N, :].unsqueeze(2).to_broadcast([N, 2, S5_P])).then_inc(spread, 1)
            dve.wait_ge(turned, 1)
            nc.vector.tensor_copy(par[:], ps[:, 0:3 * N].rearrange("p (i n) -> p i n", i=3)).then_inc(par_ready, 1)
            dve.wait_ge(par_ready, 1)
            dve.wait_ge(trig_out, 1)
            lam_re, lam_im = par[:, 0], par[:, 1]
            tt, ts = nc.vector.tensor_tensor, nc.vector.tensor_scalar
            own(tt(f[:, 1], lam_re, f[:, 0], ALU.mult))
            own(tt(f[:, 2], lam_im, f[:, 0], ALU.mult))
            own.settle()
            own(ts(f[:, 2], f[:, 2], float(1 / (2 * np.pi)), None, ALU.mult))
            own.settle()
            own(ts(f[:, 3], f[:, 2], ROUND, ROUND, ALU.add, ALU.subtract))
            own.settle()
            own(tt(turns[:], f[:, 2], f[:, 3], ALU.subtract))
            own.settle()
            dve.sem_inc(trig_in, 1)
            dve.wait_ge(trig_out, 4)
            own(tt(f[:, 6], f[:, 5], f[:, 5], ALU.mult))
            own.settle()
            own(ts(f[:, 6], f[:, 6], -2.0, 1.0, ALU.mult, ALU.add))
            own(tt(f[:, 7], rate[:], f[:, 4], ALU.mult))
            own.settle()
            own(tt(f[:, 6], rate[:], f[:, 6], ALU.mult))
            own(tt(f[:, 8], lam_re, lam_re, ALU.mult))
            own(tt(f[:, 9], lam_im, lam_im, ALU.mult))
            own.settle()
            own(ts(f[:, 6], f[:, 6], 1.0, None, ALU.subtract))
            own(tt(f[:, 8], f[:, 8], f[:, 9], ALU.add))
            own.settle()
            own(nc.vector.reciprocal(f[:, 8], f[:, 8]))
            own(tt(f[:, 9], f[:, 6], lam_re, ALU.mult))
            own(tt(f[:, 10], f[:, 7], lam_im, ALU.mult))
            own(tt(f[:, 11], f[:, 7], lam_re, ALU.mult))
            own(tt(f[:, 5], f[:, 6], lam_im, ALU.mult))
            own.settle()
            own(tt(f[:, 9], f[:, 9], f[:, 10], ALU.add))
            own(tt(f[:, 11], f[:, 11], f[:, 5], ALU.subtract))
            own.settle()
            own(tt(f[:, 9], f[:, 9], f[:, 8], ALU.mult))
            own(tt(f[:, 11], f[:, 11], f[:, 8], ALU.mult))
            own.settle()
            re = f[:, 9].unsqueeze(2).to_broadcast([P, N, S5_C])
            im = f[:, 11].unsqueeze(2).to_broadcast([P, N, S5_C])
            for part, (x, y, op) in enumerate(((re, im, ALU.subtract), (im, re, ALU.add))):
                own(tt(b_eff[:, part], b_nat[:, 0], x, ALU.mult))
                own(tt(tmp[:], b_nat[:, 1], y, ALU.mult))
                own.settle()
                own(tt(b_eff[:, part], b_eff[:, part], tmp[:], op))
                own.settle()
            for n, (m, part, d, j) in enumerate(jobs):
                if n >= 2:
                    dve.wait_ge(pad_turned, n - 1)
                if m == "b":
                    tiles = slice(d * S5_TILES + 4 * j, d * S5_TILES + 4 * j + 4)
                    last = tt(padded[:, n % 2].rearrange("p i (g c) -> p i g c", g=8),
                              b_eff[:, part, tiles].unsqueeze(2).to_broadcast([P, 4, 8, S5_C]),
                              b_mask[:].unsqueeze(3).to_broadcast([P, 4, 8, S5_C]), ALU.mult)
                else:
                    last = tt(padded[:, n % 2].rearrange("p i (g s) -> p (i g) s", g=2),
                              c_nat[:, part, d * 4 + j].unsqueeze(1).to_broadcast([P, 8, S5_P]),
                              c_mask[:].unsqueeze(2).to_broadcast([P, 8, S5_P]), ALU.mult)
                last.then_inc(pad_ready, 1)


def stage_s5_scan(nc, g, u_t, rate, turns, b_t, c_t, z_t):
    units = [(j, i, d) for j in range(4) for i in range(4) for d in range(2)]
    with ExitStack() as stack:
        a = Arena(nc, stack)
        tau = a.sb("tau", [P, 2, T])
        phase = a.sb("phase", [P, 2, T])
        whole = a.sb("whole", [P, T])
        sin = a.sb("sin", [P, 2, T])
        cos = a.sb("cos", [P, 2, T])
        x2 = a.sb("x2", [P, 2, T])
        v = a.sb("v", [P, 2, T])
        s = a.sb("s", [P, 2, 2, T])
        prods = a.sb("prods", [P, 2, 4, LAT])
        (loaded, phase_ready, half_ready, sq_ready, trig_ready, bu_ready, bu_used, scanned, prods_ready, y_ready,
         y_read, own_v, phase_used, d_added) = a.sem(
            "loaded", "phase_ready", "half_ready", "sq_ready", "trig_ready", "bu_ready", "bu_used", "scanned",
            "prods_ready", "y_ready", "y_read", "own_v", "phase_used", "d_added")
        block = a.block()
        ps = g.ps
        BU, YB = 0, 6 * BANK

        @block.sync
        def _(sp):
            sp.dma_start(tau[:], g.d["k_s5_tau"]).then_inc(loaded, 16)

        @block.tensor
        def _(pe):
            def inputs(n):
                j, i, d = units[n]
                unit = d * S5_TILES + 4 * j + i
                if n:
                    pe.wait_ge(bu_used, n)
                for part in range(2):
                    for lo, hi in halves(T):
                        last = nc.tensor.matmul(ps[:, BU + part * 1024 + lo:BU + part * 1024 + hi],
                                                b_t[:, part, unit], u_t[:, j, lo:hi], start=True, stop=True)
                last.then_inc(bu_ready, 1)

            inputs(0)
            for n, (j, i, d) in enumerate(units):
                if n + 1 < len(units):
                    inputs(n + 1)
                unit = d * S5_TILES + 4 * j + i
                pe.wait_ge(prods_ready, n + 1)
                if i == 0 and d == 0 and j >= 2:
                    pe.wait_ge(y_read, j - 1)
                out = ps[:, YB + (j % 2) * BANK:YB + (j % 2 + 1) * BANK]
                for c, which in enumerate((0, 1, 2, 2)):
                    last = nc.tensor.matmul(out, c_t[:, which, unit], prods[:, n % 2, c],
                                            start=(i == 0 and d == 0 and c == 0), stop=(i == 3 and d == 1 and c == 3))
                last.then_inc(y_ready, 1)

        @block.scalar
        def _(act):
            for n in range(len(units)):
                b = n % 2
                act.wait_ge(phase_ready, n + 1)
                if n >= 2:
                    act.wait_ge(prods_ready, n - 1)
                nc.scalar.activation(sin[:, b], phase[:, b], ACT.Sin, scale=TWO_PI)
                nc.scalar.activation(cos[:, b], phase[:, b], ACT.Sin, scale=TWO_PI / 2).then_inc(half_ready, 1)
                act.wait_ge(half_ready, n + 1)
                nc.scalar.activation(cos[:, b], cos[:, b], ACT.Square).then_inc(sq_ready, 1)
                act.wait_ge(sq_ready, n + 1)
                nc.scalar.activation(cos[:, b], cos[:, b], ACT.Identity, bias=1.0, scale=-2.0)\
                    .then_inc(trig_ready, 1)
            for j in range(4):
                act.wait_ge(d_added, j + 1)
                nc.scalar.activation(z_t[:, j], z_t[:, j], ACT.Gelu)

        @block.vector
        def _(dve):
            own = Steps(dve, own_v)
            tt = nc.vector.tensor_tensor

            def phases(n):
                j, i, d = units[n]
                unit = d * S5_TILES + 4 * j + i
                b = n % 2
                if n >= 2:
                    dve.wait_ge(half_ready, n - 1)
                own(nc.vector.tensor_scalar(phase[:, b], tau[:, d], turns[:, unit:unit + 1], None, ALU.mult))
                own.settle()
                own(nc.vector.tensor_scalar(whole[:], phase[:, b], ROUND, ROUND, ALU.add, ALU.subtract))
                own.settle()
                tt(phase[:, b], phase[:, b], whole[:], ALU.subtract).then_inc(phase_ready, 1)

            def readout(j):
                dve.wait_ge(y_ready, 8 * (j + 1))
                at = VEC["s5_d"][0] + j
                nc.vector.scalar_tensor_tensor(out=z_t[:, j], in0=u_t[:, j, CTX:T], scalar=g.vec[:, at:at + 1],
                                               in1=ps[:, YB + (j % 2) * BANK:YB + (j % 2 + 1) * BANK],
                                               op0=ALU.mult, op1=ALU.add).then_inc(y_read, 1)
                dve.wait_ge(y_read, j + 1)
                dve.sem_inc(d_added, 1)

            dve.wait_ge(loaded, 16)
            phases(0)
            for n, (j, i, d) in enumerate(units):
                unit = d * S5_TILES + 4 * j + i
                b = n % 2
                if n + 1 < len(units):
                    phases(n + 1)
                re, im = ps[:, BU:BU + T], ps[:, BU + 1024:BU + 1024 + T]
                dve.wait_ge(trig_ready, n + 1)
                dve.wait_ge(bu_ready, n + 1)
                own(tt(v[:, 0], cos[:, b], re, ALU.mult))
                own(tt(x2[:, 0], sin[:, b], im, ALU.mult))
                own(tt(v[:, 1], cos[:, b], im, ALU.mult))
                own(tt(x2[:, 1], sin[:, b], re, ALU.mult))
                own.settle()
                dve.sem_inc(bu_used, 1)
                own(tt(v[:, 0], v[:, 0], x2[:, 0], ALU.add))
                own(tt(v[:, 1], v[:, 1], x2[:, 1], ALU.subtract))
                own.settle()
                if n >= 2:
                    dve.wait_ge(prods_ready, n - 1)
                r = rate[:, unit:unit + 1]
                for part in range(2):
                    x, out = v[:, part], s[:, b, part]
                    if d == 0:
                        own(nc.vector.tensor_tensor_scan(out, r.to_broadcast([P, T]), x, 0.0, ALU.mult, ALU.add))
                    else:
                        own(nc.vector.tensor_tensor_scan(out[:, 0:CTX][:, ::-1], r.to_broadcast([P, CTX]),
                                                         x[:, 0:CTX][:, ::-1], 0.0, ALU.mult, ALU.add))
                if d == 1:
                    own.settle()
                    for part in range(2):
                        x, out = v[:, part], s[:, b, part]
                        own(nc.vector.tensor_tensor_scan(out[:, CTX:T][:, ::-1], r.to_broadcast([P, LAT]),
                                                         x[:, CTX:T][:, ::-1], out[:, 0:1], ALU.mult, ALU.add))
                own.settle()
                dve.sem_inc(scanned, 1)
                if i == 0 and d == 0 and j:
                    readout(j - 1)
            readout(3)

        @block.gpsimd
        def _(pool):
            for n in range(len(units)):
                b = n % 2
                pool.wait_ge(scanned, n + 1)
                pool.wait_ge(trig_ready, n + 1)
                if n >= 2:
                    pool.wait_ge(y_ready, n - 1)
                for c, (part, table) in enumerate(((0, cos), (1, sin), (0, sin), (1, cos))):
                    last = nc.gpsimd.tensor_tensor(prods[:, b, c], s[:, b, part, CTX:T], table[:, b, CTX:T], ALU.mult)
                last.then_inc(prods_ready, 1)


def stage_s5_glu(nc, g, z_t):
    with ExitStack() as stack:
        a = Arena(nc, stack)
        w = a.sb("w_glu", [P, 4, 512])
        gate = a.sb("gate", [P, 4, LAT])
        loaded, summed, gated = a.sem("loaded", "summed", "gated")
        block = a.block()
        ps = g.ps

        @block.sync
        def _(sp):
            sp.dma_start(w[:], g.d["s5_w_glu"][0].rearrange("(k p) n -> p k n", p=P)).then_inc(loaded, 16)

        @block.tensor
        def _(pe):
            pe.wait_ge(loaded, 16)
            for m in range(4):
                for k in range(4):
                    last = nc.tensor.matmul(ps[:, m * BANK:(m + 1) * BANK], w[:, k, m * P:(m + 1) * P], z_t[:, k],
                                            start=(k == 0), stop=(k == 3))
                last.then_inc(summed, 1)

        @block.scalar
        def _(act):
            for m in range(4):
                act.wait_ge(summed, m + 1)
                at = VEC["s5_bglu"][0] + m
                nc.scalar.activation(gate[:, m], ps[:, m * BANK:(m + 1) * BANK], ACT.Sigmoid,
                                     bias=g.vec[:, at:at + 1]).then_inc(gated, 1)

        @block.vector
        def _(dve):
            dve.wait_ge(summed, 4)
            for m in range(4):
                dve.wait_ge(gated, m + 1)
                nc.vector.tensor_tensor(z_t[:, m], z_t[:, m], gate[:, m], ALU.mult)


def stage_output(nc, g):
    x = g.x_t[:, :, CTX:T]
    at = VEC["final"][0]
    stage_rms_channels(nc, g, x, DK, g.vec[:, at:at + 8])
    with ExitStack() as stack:
        a = Arena(nc, stack)
        rows = a.sb("out_rows", [P, LAT // P, D])
        turned, kept, stored = a.sem("turned", "kept", "stored")
        block = a.block()
        ps = g.ps

        @block.tensor
        def _(pe):
            for t in range(LAT // P):
                for k in range(DK):
                    last = nc.tensor.transpose(ps[:, t * 1024 + k * P:t * 1024 + (k + 1) * P],
                                               x[:, k, t * P:(t + 1) * P], g.ident[:])
                last.then_inc(turned, 1)

        @block.vector
        def _(dve):
            for t in range(LAT // P):
                dve.wait_ge(turned, t + 1)
                nc.vector.tensor_copy(rows[:, t], ps[:, t * 1024:(t + 1) * 1024]).then_inc(kept, 1)

        @block.sync
        def _(sp):
            for t in range(LAT // P):
                sp.wait_ge(kept, t + 1)
                sp.dma_start(g.out[0, t * P:(t + 1) * P, :], rows[:, t]).then_inc(stored, 16)
            sp.wait_ge(stored, 16 * (LAT // P))


def peer(nc, g, layer, t0, until=99):
    n = T - t0
    spans = [(0, LAT, CTX, 0)] + ([(LAT, T, 0, 1)] if t0 == 0 else [])
    with ExitStack() as stack:
        a = Arena(nc, stack)
        scores_d = nc.dram_tensor(f"scores{layer}", (n // P, P, 2 * PEER_H, KEYS), F32).ap()
        acts_d = nc.dram_tensor(f"activations{layer}", (KEYS, P, n), F32).ap()
        table = nc.dram_tensor(f"gate_table{layer}", (P, n // TB, KEYS, TB), F32).ap()
        x_d = nc.dram_tensor(f"x_kept{layer}", (P, DK, T), F32).ap()
        with ExitStack() as inner:
            b = Arena(nc, inner)
            hi = b.sb("h_hi", [P, DK, n], F32R)
            lo = b.sb("h_lo", [P, DK, n], F32R)
            with ExitStack() as scope:
                c = Arena(nc, scope)
                q_t = c.sb("peer_q", [P, 2 * PEER_H, n])
                with ExitStack() as early:
                    h_t = Arena(nc, early).sb("h_t", [P, DK, n])
                    stage_norm(nc, g, layer, 1, t0, h_t, latents_first=True)
                    stage_split(nc, g, h_t, hi, lo)
                    wq = g.d["peer_wq"][layer].rearrange("(k p) n -> p k n", p=P)
                    stage_project(nc, g, "peer_wq", h_t, wq,
                                  [(512 * i, 512, channel_units(q_t[:, 4 * i:4 * i + 4], 4)) for i in range(4)])
                stage_scores(nc, g, layer, q_t, scores_d, n)
            stage_move_x(nc, g, x_d, True)
            if until >= 7:
                stage_route_and_activate(nc, g, layer, hi, lo, scores_d, acts_d, table, n)
        stage_move_x(nc, g, x_d, False)
        if until >= 7:
            stage_mix_experts(nc, g, layer, acts_d, table, n, spans)


def layer_even(nc, g, until):
    w_in = g.d["ev_w_in"][0].rearrange("(k p) n -> p k n", p=P)
    with ExitStack() as stack:
        a = Arena(nc, stack)
        y_t = a.sb("y_t", [P, DK, T])
        with ExitStack() as inner:
            b = Arena(nc, inner)
            hg = b.sb("hg", [P, 4, HG_HEADS, T])
            hg_v = b.sb("hg_v", [P, T // P, 512])
            with ExitStack() as scope:
                c = Arena(nc, scope)
                proj = c.sb("gqa_proj", [P, T // P, GQA_IN])
                with ExitStack() as early:
                    h_t = Arena(nc, early).sb("h_t", [P, DK, T])
                    stage_norm(nc, g, 0, 0, 0, h_t)
                    at = GQA_IN
                    pairs = proj[:, :, 0:512].rearrange("p t (j kv c) -> p t kv j c", j=4, kv=2)
                    blocks = [(0, 512, [("tokens", t, pairs[:, t]) for t in range(T // P)]),
                              (512, 256, token_units(proj[:, :, 512:768], T // P)),
                              (at, 512, channel_units(hg[:, 0], 4)), (at + 512, 512, channel_units(hg[:, 1], 4)),
                              (at + 1024, 512, channel_units(hg[:, 2], 4)),
                              (at + 1536, 512, token_units(hg_v[:], T // P)),
                              (at + 2048, 512, channel_units(hg[:, 3], 4))]
                    stage_project(nc, g, "ev_in", h_t, w_in, blocks)
                if until >= 2:
                    q_t = c.sb("q_t", [P, 4, T])
                    k_t = c.sb("k_t", [P, T])
                    stage_gqa_heads(nc, g, proj, q_t, k_t)
                if until >= 3:
                    units = []
                    for t in range(T // P):
                        keys = CTX if t < CTX // P else T
                        for j in range(4):
                            for kv in range(2):
                                rows = slice(64 * kv, 64 * kv + 64)
                                at = (GQA_Q + GQA_KV + kv) * HEAD

                                def v(i, at=at):
                                    return proj[:, i, at:at + HEAD]

                                units.append((q_t[rows, j, t * P:(t + 1) * P], k_t[rows, 0:keys], v, 64 * kv,
                                              y_t[:, j, t * P:(t + 1) * P]))
                    stage_attention(nc, g, units)
            if until >= 4:
                keep_k = b.sb("keep_k", [P, 2 * HG_HEADS, T])
                cum = b.sb("cum", [P, 2 * HG_HEADS, T])
                with ExitStack() as scope:
                    forget = Arena(nc, scope).sb("forget", [P, HG_HEADS, T])
                    stage_hgrn2_gates(nc, g, hg, forget, keep_k, cum)
                stage_hgrn2_scan(nc, g, hg, hg_v, keep_k, cum, y_t)
                stage_hgrn2_readout(nc, g, hg, y_t)
        if until >= 5:
            w_out = g.d["ev_w_out"][0]
            rows = [(slice(64 * kv, 64 * kv + 64), j, w_out[256 * kv + 64 * j:256 * kv + 64 * j + 64, :])
                    for kv in range(2) for j in range(4)]
            rows += [(slice(0, P), k, w_out[k * P:(k + 1) * P, :]) for k in range(4, DK)]
            stage_mix_out(nc, g, 0, y_t, 0, rows)
    if until >= 6:
        peer(nc, g, 0, 0, until)


def layer_odd(nc, g, until):
    w_in = g.d["od_w_in"][0].rearrange("(k p) n -> p k n", p=P)
    with ExitStack() as stack:
        a = Arena(nc, stack)
        y_t = a.sb("y_t", [P, DK, LAT])
        with ExitStack() as inner:
            b = Arena(nc, inner)
            u_t = b.sb("u_t", [P, 4, T])
            with ExitStack() as scope:
                c = Arena(nc, scope)
                q_a = c.sb("q_a", [P, MLA_QR // P, LAT])
                kv_a = c.sb("kv_a", [P, MLA_KVR // P, T])
                k_rope = c.sb("k_rope", [MLA_ROPE, T])
                with ExitStack() as early:
                    h_t = Arena(nc, early).sb("h_t", [P, DK, T])
                    stage_norm(nc, g, 1, 0, 0, h_t)
                    blocks = [(0, MLA_QR, [("latents", m * P, q_a[:, m, :]) for m in range(MLA_QR // P)]),
                              (MLA_QR, MLA_KVR, channel_units(kv_a, MLA_KVR // P)),
                              (MLA_QR + MLA_KVR, MLA_ROPE, [("channels", 0, k_rope[:])]),
                              (MLA_IN, 512, channel_units(u_t, 4))]
                    stage_project(nc, g, "od_in", h_t, w_in, blocks)
                at, _ = VEC["mla_qa"]
                stage_rms_channels(nc, g, q_a, MLA_QR // P, g.vec[:, at:at + 3], (MLA_NOPE + MLA_ROPE) ** -0.5)
                at, _ = VEC["mla_kva"]
                stage_rms_channels(nc, g, kv_a, MLA_KVR // P, g.vec[:, at:at + 2])
                q_t = c.sb("mla_q", [P, MLA_H, LAT])
                k_t = c.sb("mla_k", [P, MLA_H, T])
                v_tok = c.sb("mla_v", [P, T // P, MLA_H * MLA_V])
                stage_mla_heads(nc, g, q_a, kv_a, k_rope, q_t, k_t, v_tok)
                units = []
                for t in range(LAT // P):
                    for h in range(MLA_H):
                        def v(i, h=h):
                            return v_tok[:, i, h * MLA_V:(h + 1) * MLA_V]

                        units.append((q_t[0:96, h, t * P:(t + 1) * P], k_t[0:96, h, :], v, 64 * (h % 2),
                                      y_t[:, h // 2, t * P:(t + 1) * P]))
                stage_attention(nc, g, units)
            if until >= 9:
                N = 2 * S5_TILES
                rate = b.sb("rate", [P, N])
                turns = b.sb("turns", [P, N])
                b_t = b.sb("b_t", [P, 2, N, P])
                c_t = b.sb("c_t", [P, 3, N, P])
                z_t = y_t[:, 4:DK]
                stage_s5_parameters(nc, g, rate, turns, b_t, c_t)
                stage_s5_scan(nc, g, u_t, rate, turns, b_t, c_t, z_t)
                stage_s5_glu(nc, g, z_t)
        if until >= 10:
            w_out = g.d["od_w_out"][0]
            stage_mix_out(nc, g, 1, y_t, CTX, [(slice(0, P), k, w_out[k * P:(k + 1) * P, :]) for k in range(DK)])
    if until >= 11:
        peer(nc, g, 1, CTX)
    if until >= 12:
        stage_output(nc, g)


def rope_table(rot_dim):
    axis_dim = rot_dim // 2
    inv = np.float32(10000.0) ** (-np.arange(0, axis_dim, 2, dtype=np.float32) / np.float32(axis_dim))
    t = np.arange(LAT)
    angle = np.stack([(t // GRID_W).astype(np.float32)[:, None] * inv,
                      (t % GRID_W).astype(np.float32)[:, None] * inv], 1)
    return np.stack([np.cos(angle), np.sin(angle)]).astype(np.float32)


def constants():
    gqa = rope_table(HEAD).reshape(2, 4, P, 2, 16).transpose(2, 0, 1, 3, 4)
    masks = np.zeros((2, P, NL, P), np.float32)
    key, query = np.arange(P)[:, None], np.arange(P)[None, :]
    for e, m in enumerate(HG_LEVELS):
        same = key // (2 * m) == query // (2 * m)
        masks[0, :, e] = same & (key // m % 2 == 0) & (query // m % 2 == 1)
        masks[1, :, e] = same & (key // m % 2 == 1) & (query // m % 2 == 0)
    masks[:, :, NL - 1] = np.eye(P)
    mla = rope_table(MLA_ROPE)
    cos, sin = (np.stack([mla[w], mla[w]], 2).reshape(LAT, MLA_ROPE).T for w in range(2))
    channel = np.arange(MLA_ROPE)
    sin = sin * np.where(channel // 8 % 2 == 0, -1.0, 1.0).astype(np.float32)[:, None]
    swap = np.zeros((MLA_ROPE, MLA_ROPE), np.float32)
    swap[channel ^ 8, channel] = 1.0
    part = np.arange(P)
    tile, group = np.arange(4)[:, None], np.arange(8)[None, :]
    bmask = (group[None] == 2 * tile[None] + (part // S5_P)[:, None, None]).astype(np.float32)
    cmask = (part[:, None] // S5_C == np.arange(8)[None, :]).astype(np.float32)
    t = np.arange(T)
    tau = np.stack([t, np.where(t < CTX, CTX - 1 - t, CTX + T - 1 - t)]).astype(np.float32)
    return {"k_rope_mla": np.ascontiguousarray(np.stack([cos, sin], 1)), "k_rope_swap": swap,
            "k_s5_bmask": bmask, "k_s5_cmask": cmask, "k_s5_tau": np.tile(tau[None], (P, 1, 1)),
            "k_hg_masks": masks.reshape(2, P, NL * P), "k_ident": np.eye(P, dtype=np.float32),
            "k_head_ones": (key // TOPK == query // TOPK).astype(np.float32),
            "k_iota": np.tile(np.arange(P, dtype=np.float32), (P, 1)), "k_rope_gqa": np.ascontiguousarray(gqa)}


def kernel(**inputs):
    import concourse.bacc as bacc
    from concourse.bass_utils import run_bass_kernel_spmd

    nc = bacc.Bacc("TRN2", target_bir_lowering=False, num_devices=1)
    arrays = {name: np.ascontiguousarray(v) for name, v in inputs.items()}
    arrays.update(constants())
    d = {name: nc.dram_tensor(name, v.shape, mybir.dt.from_np(v.dtype), kind="ExternalInput").ap()
         for name, v in arrays.items()}
    out = nc.dram_tensor("out", (1, LAT, D), F32, kind="ExternalOutput").ap()
    build(nc, d, out)
    result = run_bass_kernel_spmd(nc, [arrays], core_ids=[0])
    return result.results[0]["out"]
```

```python
from contextlib import ExitStack

import numpy as np

import concourse.bass as bass
from concourse import mybir

F32 = mybir.dt.float32
F32R = mybir.dt.float32r
U32 = mybir.dt.uint32
ACT = mybir.ActivationFunctionType
ALU = mybir.AluOpType
AX = mybir.AxisListType

P = 128
D = 1024
DK = D // P
CTX, LAT = 256, 512
T = CTX + LAT
GRID_W = 64
EPS = 1e-6
BANK = 512

GQA_Q, GQA_KV, HEAD = 8, 2, 64
GQA_IN = (GQA_Q + 2 * GQA_KV) * HEAD
HG_HEADS = 4
EVEN_IN = GQA_IN + 5 * 512
MLA_H, MLA_NOPE, MLA_ROPE, MLA_V = 8, 64, 32, 64
MLA_QR, MLA_KVR = 384, 256
MLA_IN = MLA_QR + MLA_KVR + MLA_ROPE
ODD_IN = MLA_IN + 512
S5_G, S5_P, S5_C = 32, 64, 16

PEER_H, KEYS, TOPK, QDIM = 8, 128, 16, 256
SLOTS = PEER_H * TOPK
EXPERTS = KEYS * KEYS
LOWEST = -3.0e38
FIRST_SEM, SEM_BANK = 100, 77

VEC = {}
for _name, _n in (("c", 8), ("c_ctx", 8), ("norm1", 16), ("norm2", 16), ("final", 8), ("lb", 16), ("onorm", 1),
                  ("s5_d", 4), ("s5_bglu", 4), ("mla_qa", 3), ("mla_kva", 2)):
    VEC[_name] = (sum(n for _, n in VEC.values()), _n)
VEC_ROWS = sum(n for _, n in VEC.values())


class Steps:

    def __init__(self, engine, sem):
        self.engine, self.sem, self.n = engine, sem, 0

    def __call__(self, instruction):
        instruction.then_inc(self.sem, 1)
        self.n += 1

    def settle(self):
        self.engine.wait_ge(self.sem, self.n)


class Arena:

    uses = {}
    stages = 0

    def __init__(self, nc, stack):
        self.nc, self.stack, self.sems = nc, stack, []

    @staticmethod
    def fresh(name):
        Arena.uses[name] = n = Arena.uses.get(name, 0) + 1
        return name if n == 1 else f"{name}_{n}"

    def sb(self, name, shape, dt=F32):
        return self.stack.enter_context(self.nc.sbuf_tensor(Arena.fresh(name), shape, dt))

    def sem(self, *names):
        if not self.sems:
            Arena.stages += 1
            self.stack.callback(self.clear)
        base = FIRST_SEM + (Arena.stages % 2) * SEM_BANK
        for name in names:
            assert len(self.sems) < SEM_BANK
            self.sems.append(self.nc.alloc_semaphore(Arena.fresh(name), num=base + len(self.sems)))
        got = self.sems[-len(names):]
        return got[0] if len(got) == 1 else got

    def clear(self):
        base = FIRST_SEM + (Arena.stages % 2) * SEM_BANK
        self.nc.gpsimd.sem_clear(range(base, base + len(self.sems)))
        for sem in self.sems:
            self.nc.release_semaphore(sem)

    def block(self):
        return self.stack.enter_context(self.nc.Block())


def stage_load_tokens(nc, g):
    with ExitStack() as stack:
        a = Arena(nc, stack)
        tokens = a.sb("tokens", [P, T // P, D])
        rows = a.sb("rows", [VEC_ROWS, P])
        ada_rows = a.sb("ada_rows", [96, P])
        const_loaded, rows_loaded, tile_loaded = a.sem("const_loaded", "rows_loaded", "tile_loaded")
        transposed, evacuated_v, evacuated_s = a.sem("transposed", "evacuated_v", "evacuated_s")
        block = a.block()
        ps = g.ps

        @block.sync
        def _(sp):
            sp.dma_start(g.ident[:], g.d["k_ident"]).then_inc(const_loaded, 16)
            for j in range(T // P):
                src = g.d["ctx"][0, j * P:(j + 1) * P, :] if j < 2 else g.d["x"][0, (j - 2) * P:(j - 1) * P, :]
                if j:
                    sp.wait_ge(tile_loaded, 16 * j)
                sp.dma_start(tokens[:, j, :], src).then_inc(tile_loaded, 16)

        n_rows = 16 * (len(VEC) + 1)

        @block.tensor
        def _(pe):
            pe.wait_ge(const_loaded, 16)
            for j in range(T // P):
                pe.wait_ge(tile_loaded, 16 * (j + 1))
                slot = j % 3
                if j >= 3:
                    pe.wait_ge(evacuated_v, j - 2)
                    pe.wait_ge(evacuated_s, j - 2)
                for k in range(DK):
                    last = nc.tensor.transpose(ps[:, (slot * 8 + k) * P:(slot * 8 + k + 1) * P],
                                               tokens[:, j, k * P:(k + 1) * P], g.ident[:])
                last.then_inc(transposed, 1)
            pe.wait_ge(rows_loaded, n_rows)
            nc.tensor.transpose(ps[:, 6 * BANK:6 * BANK + VEC_ROWS], rows[:], g.ident[:VEC_ROWS, :VEC_ROWS])
            nc.tensor.transpose(ps[:, 7 * BANK:7 * BANK + 96], ada_rows[:], g.ident[:96, :96]).then_inc(transposed, 1)

        @block.vector
        def _(dve):
            nc.vector.memset(g.ones_d[:], 1.0 / D)
            for j in range(T // P):
                dve.wait_ge(transposed, j + 1)
                src = ps[:, (j % 3) * 1024:(j % 3) * 1024 + 512].rearrange("p (k t) -> p k t", t=P)
                nc.vector.tensor_copy(g.x_t[:, 0:4, j * P:(j + 1) * P], src).then_inc(evacuated_v, 1)
            dve.wait_ge(transposed, T // P + 1)
            nc.vector.tensor_copy(g.vec[:], ps[:, 6 * BANK:6 * BANK + VEC_ROWS])
            nc.vector.tensor_copy(g.ada_b[:], ps[:, 7 * BANK:7 * BANK + 96])

        @block.scalar
        def _(act):
            d = g.d
            loads = [("c", d["c"].rearrange("o (k p) -> (o k) p", p=P)),
                     ("c_ctx", d["c_ctx"].rearrange("(k p) -> k p", p=P)),
                     ("norm1", d["norm1_g"].rearrange("l (k p) -> (l k) p", p=P)),
                     ("norm2", d["norm2_g"].rearrange("l (k p) -> (l k) p", p=P)),
                     ("final", d["final_g"].rearrange("(k p) -> k p", p=P)),
                     ("lb", d["hg_lb_logits"].rearrange("d e (k p) -> (d e k) p", p=P)),
                     ("onorm", d["hg_onorm_g"]),
                     ("s5_d", d["s5_d"].rearrange("o (k p) -> (o k) p", p=P)),
                     ("s5_bglu", d["s5_b_glu"].rearrange("o (k p) -> (o k) p", p=P)),
                     ("mla_qa", d["mla_qa_g"].rearrange("o (k p) -> (o k) p", p=P)),
                     ("mla_kva", d["mla_kva_g"].rearrange("o (k p) -> (o k) p", p=P))]
            for name, src in loads:
                at, n = VEC[name]
                act.dma_start(rows[at:at + n, :], src).then_inc(rows_loaded, 16)
            act.dma_start(ada_rows[:], d["ada_b"].rearrange("l (k p) -> (l k) p", p=P)).then_inc(rows_loaded, 16)
            for j in range(T // P):
                act.wait_ge(transposed, j + 1)
                src = ps[:, (j % 3) * 1024 + 512:(j % 3) * 1024 + 1024].rearrange("p (k t) -> p k t", t=P)
                nc.scalar.copy(g.x_t[:, 4:8, j * P:(j + 1) * P], src).then_inc(evacuated_s, 1)


def stage_modulation(nc, g):
    COLS, RING = 512, 3
    with ExitStack() as stack:
        a = Arena(nc, stack)
        w = a.sb("ada_ring", [P, RING, DK, COLS])
        cond = a.sb("cond", [P, DK, 2])
        rows = a.sb("mod_rows", [2, RING, COLS])
        w_loaded = [a.sem(f"w_loaded{r}") for r in range(RING)]
        summed = [a.sem(f"summed{r}") for r in range(RING)]
        rows_ready = [a.sem(f"rows_ready{r}") for r in range(RING)]
        turned = [a.sem(f"turned{r}") for r in range(RING)]
        kept = [a.sem(f"kept{r}") for r in range(RING)]
        cond_ready, scaled = a.sem("cond_ready", "scaled")
        block = a.block()
        ps = g.ps
        tiles = COLS // P
        ada = [g.d["ada_w"][layer].rearrange("(k p) n -> p k n", p=P) for layer in range(2)]
        turns = 6 * D // COLS // RING

        def ring_turns(engine, emit):
            emit(0, 0, True)
            emit(0, 1, False)
            for layer in range(2):
                with engine.Fori(0 if layer else 2, turns) as i:
                    emit(layer, i, False)

        @block.sync
        def _(sp):
            def turn(layer, i, first):
                for r in range(RING):
                    if not first:
                        sp.wait_ge(summed[r], i + layer * turns)
                    sp.dma_start(w[:, r], ada[layer][:, :, bass.ds((i * RING + r) * COLS, COLS)])\
                        .then_inc(w_loaded[r], 16)

            ring_turns(sp, turn)

        @block.scalar
        def _(act):
            nc.scalar.activation(cond[:], g.vec[:, 0:16].rearrange("p (s k) -> p k s", s=2), ACT.Silu)\
                .then_inc(cond_ready, 1)

            def turn(layer, i, first):
                for r in range(RING):
                    act.wait_ge(summed[r], i + (layer * turns + 1))
                    if not first:
                        act.wait_ge(turned[r], i + layer * turns)
                    nc.scalar.copy(rows[:, r], ps[0:2, r * BANK:r * BANK + COLS]).then_inc(rows_ready[r], 1)

            ring_turns(act, turn)

        @block.tensor
        def _(pe):
            def to_channels(r, count, start):
                pe.wait_ge(rows_ready[r], count)
                if not start:
                    pe.wait_ge(kept[r], count - 1)
                for m in range(tiles):
                    last = nc.tensor.matmul(ps[:, (4 + r) * BANK + 2 * m:(4 + r) * BANK + 2 * m + 2],
                                            rows[:, r, m * P:(m + 1) * P], g.ident[0:2, 0:2], start=True, stop=True)
                last.then_inc(turned[r], 1)

            def turn(layer, i, first):
                for r in range(RING):
                    pe.wait_ge(w_loaded[r], i * 16 + (layer * turns + 1) * 16)
                    if not first:
                        pe.wait_ge(rows_ready[r], i + layer * turns)
                    for k in range(DK):
                        last = nc.tensor.matmul(ps[0:2, r * BANK:r * BANK + COLS], cond[:, k], w[:, r, k],
                                                start=(k == 0), stop=(k == DK - 1))
                    last.then_inc(summed[r], 1)
                    if r:
                        to_channels(r - 1, i + (layer * turns + 1), first)
                    elif not first:
                        to_channels(RING - 1, i + layer * turns, second(layer, i))

            def second(layer, i):
                return layer == 0 and isinstance(i, int) and i == 1

            pe.wait_ge(cond_ready, 1)
            ring_turns(pe, turn)
            to_channels(RING - 1, 2 * turns, False)

        @block.vector
        def _(dve):
            def turn(layer, i, first):
                bias = g.ada_b[:, 48 * layer:48 * (layer + 1)]
                for r in range(RING):
                    dve.wait_ge(turned[r], i + (layer * turns + 1))
                    sums = ps[:, (4 + r) * BANK:(4 + r) * BANK + 2 * tiles].rearrange("p (m s) -> p m s", s=2)
                    for s in range(2):
                        last = nc.vector.tensor_tensor(g.mod[:, layer, bass.ds((i * RING + r) * tiles, tiles), s],
                                                       sums[:, :, s],
                                                       bias[:, bass.ds((i * RING + r) * tiles, tiles)], ALU.add)
                    last.then_inc(kept[r], 1)

            ring_turns(dve, turn)
            for r in range(RING):
                dve.wait_ge(kept[r], 2 * turns)
            own = Steps(dve, scaled)
            for layer in range(2):
                for which, (norm, part) in enumerate((("norm1", 1), ("norm2", 4))):
                    at = VEC[norm][0] + 8 * layer
                    gs = g.gs[:, layer, which]
                    own(nc.vector.tensor_scalar(gs, g.mod[:, layer, 8 * part:8 * part + 8, :], 1.0, None, ALU.add))
                    own.settle()
                    own(nc.vector.tensor_tensor(gs, gs, g.vec[:, at:at + 8].unsqueeze(2).to_broadcast([P, 8, 2]),
                                                ALU.mult))


STREAMS = ((1, 0, CTX), (0, CTX, T))


def stage_norm(nc, g, layer, which, t0, hi, lo, room, w_view, blocks, latents_first=False):
    n = T - t0

    def cols(b, e):
        if latents_first:
            b, e = ((b + LAT, e + LAT) if b < CTX else (b - CTX, e - CTX))
            return slice(b, e)
        return slice(b - t0, e - t0)

    parts = [(s, e) for s, e in ((t0, CTX), (CTX, T)) if e > s]
    streams = [(s, max(b, t0), e) for s, b, e in STREAMS if e > t0]
    shift = 8 * 3 * which
    with ExitStack() as stack:
        a = Arena(nc, stack)
        sq = a.sb("sq", [P, DK, n])
        rstd = a.sb("rstd", [P, n])
        h_t = sq
        squared, summed, root_in, rooted, scaled = a.sem("squared", "summed", "root_in", "rooted", "scaled")
        shifted, hi_ready, w_loaded = a.sem("shifted", "hi_ready", "w_loaded")
        own_v = a.sem("own_v")
        block = a.block()
        ps = g.ps

        @block.sync
        def _(sp):
            for b, (c0, cols, _) in enumerate(blocks[:W_RING]):
                sp.dma_start(weight_slots(room)[:, b, :, 0:cols], w_view[:, :, c0:c0 + cols]).then_inc(w_loaded, 16)
            sp.wait_ge(w_loaded, 16 * W_RING)

        @block.scalar
        def _(act):
            for k in range(DK):
                nc.scalar.activation(sq[:, k], g.x_t[:, k, t0:T], ACT.Square).then_inc(squared, 1)
            act.wait_ge(root_in, 1)
            nc.scalar.activation(rstd[:], rstd[:], ACT.Sqrt).then_inc(rooted, 1)
            for k in range(DK):
                for i, (s, b, e) in enumerate(streams):
                    act.wait_ge(scaled, len(streams) * k + i + 1)
                    nc.scalar.activation(h_t[:, k, cols(b, e)], h_t[:, k, cols(b, e)], ACT.Identity,
                                         bias=g.mod[:, layer, shift + k, s:s + 1]).then_inc(shifted, 1)
                if k:
                    act.wait_ge(shifted, len(streams) * k)
                    nc.scalar.copy(hi[:, k - 1], h_t[:, k - 1]).then_inc(hi_ready, 1)
            act.wait_ge(shifted, len(streams) * DK)
            nc.scalar.copy(hi[:, DK - 1], h_t[:, DK - 1]).then_inc(hi_ready, 1)

        @block.gpsimd
        def _(pool):
            for k in range(DK):
                pool.wait_ge(hi_ready, k + 1)
                nc.gpsimd.tensor_tensor(lo[:, k], h_t[:, k], hi[:, k].bitcast(F32), ALU.subtract)

        @block.tensor
        def _(pe):
            for k in range(DK):
                pe.wait_ge(squared, k + 1)
                for i, (b, e) in enumerate(parts):
                    last = nc.tensor.matmul(ps[:, i * BANK:i * BANK + e - b], g.ones_d[:], sq[:, k, b - t0:e - t0],
                                            start=(k == 0), stop=(k == DK - 1))
            last.then_inc(summed, 1)

        @block.vector
        def _(dve):
            own = Steps(dve, own_v)
            dve.wait_ge(summed, 1)
            for i, (b, e) in enumerate(parts):
                last = nc.vector.tensor_scalar(rstd[:, b - t0:e - t0], ps[:, i * BANK:i * BANK + e - b], EPS, None,
                                               ALU.add)
            last.then_inc(root_in, 1)
            dve.wait_ge(rooted, 1)
            own(nc.vector.reciprocal(rstd[:], rstd[:]))
            own.settle()
            for k in range(DK):
                for s, b, e in streams:
                    nc.vector.scalar_tensor_tensor(out=h_t[:, k, cols(b, e)], in0=g.x_t[:, k, b:e],
                                                   scalar=g.gs[:, layer, which, k, s:s + 1],
                                                   in1=rstd[:, b - t0:e - t0],
                                                   op0=ALU.mult, op1=ALU.mult).then_inc(scaled, 1)


W_RING, W_COLS = 2, 256


def weight_slots(room):
    return room[:, 0:W_RING * DK * W_COLS].rearrange("p (r k c) -> p r k c", r=W_RING, k=DK)


def halves(n):
    return [(b, min(b + BANK, n)) for b in range(0, n, BANK)]


def stage_project_split(nc, g, name, h_hi, h_lo, w_view, blocks, room, kc=DK):
    RING, SLOTS_PS = W_RING, 4
    widest = max(cols for _, cols, _ in blocks)
    units = [(b, kind, place, out) for b, (_, _, us) in enumerate(blocks) for kind, place, out in us]
    with ExitStack() as stack:
        a = Arena(nc, stack)
        w_raw = weight_slots(room)
        w_hi = a.sb(f"{name}_hi", [P, RING, kc, widest], F32R)
        w_lo = a.sb(f"{name}_lo", [P, RING, kc, widest], F32R)
        w_loaded = [a.sem(f"w_loaded{r}") for r in range(RING)]
        w_used, hi_ready, lo_ready, summed, kept_v, kept_s = a.sem("w_used", "hi_ready", "lo_ready", "summed",
                                                                   "kept_v", "kept_s")
        block = a.block()
        ps = g.ps

        @block.sync
        def _(sp):
            for b, (c0, cols, _) in enumerate(blocks):
                if b >= RING:
                    sp.wait_ge(lo_ready, b - RING + 1)
                    sp.dma_start(w_raw[:, b % RING, :, 0:cols], w_view[:, :, c0:c0 + cols])\
                        .then_inc(w_loaded[b % RING], 16)

        @block.tensor
        def _(pe):
            for u, (b, kind, place, _) in enumerate(units):
                cols = blocks[b][1]
                at = (u % SLOTS_PS) * 2 * BANK
                pe.wait_ge(lo_ready, b + 1)
                if u >= SLOTS_PS:
                    pe.wait_ge(kept_s if u % 2 else kept_v, (u - SLOTS_PS) // 2 + 1)
                for k in range(kc):
                    for i, (w, h) in enumerate(((w_hi, h_hi), (w_hi, h_lo), (w_lo, h_hi))):
                        start, stop = k == 0 and i == 0, k == kc - 1 and i == 2
                        if kind != "tokens":
                            m = min(P, cols - place)
                            t0 = CTX if kind == "latents" else 0
                            for b0, b1 in halves(h.shape[2] - t0):
                                last = nc.tensor.matmul(ps[0:m, at + b0:at + b1], w[:, b % RING, k, place:place + m],
                                                        h[:, k, t0 + b0:t0 + b1], start=start, stop=stop)
                        else:
                            last = nc.tensor.matmul(ps[:, at:at + cols], h[:, k, place * P:(place + 1) * P],
                                                    w[:, b % RING, k, 0:cols], start=start, stop=stop)
                last.then_inc(summed, 1)
                if u + 1 == len(units) or units[u + 1][0] != b:
                    pe.wait_ge(summed, u + 1)
                    pe.sem_inc(w_used, 1)

        def result(u):
            b, kind, place, _ = units[u]
            at = (u % SLOTS_PS) * 2 * BANK
            cols = blocks[b][1]
            if kind != "tokens":
                return ps[0:min(P, cols - place), at:at + h_hi.shape[2] - (CTX if kind == "latents" else 0)]
            if len(units[u][3].shape) == 3:
                return ps[:, at:at + cols].rearrange("p (j c) -> p j c", j=units[u][3].shape[1])
            return ps[:, at:at + cols]

        ends = {max(u for u in range(len(units)) if units[u][0] == b): b for b in range(len(blocks))}

        def of_block(w, b):
            return w[:, b % RING, :, 0:blocks[b][1]]

        @block.vector
        def _(dve):
            def lo(b):
                dve.wait_ge(hi_ready, b + 1)
                nc.vector.tensor_tensor(of_block(w_lo, b), of_block(w_raw, b), of_block(w_hi, b).bitcast(F32),
                                        ALU.subtract).then_inc(lo_ready, 1)

            for b in range(min(RING, len(blocks))):
                lo(b)
            for u in range(len(units)):
                if u % 2 == 0:
                    dve.wait_ge(summed, u + 1)
                    nc.vector.tensor_copy(units[u][3], result(u)).then_inc(kept_v, 1)
                if u in ends and ends[u] + RING < len(blocks):
                    lo(ends[u] + RING)

        @block.scalar
        def _(act):
            def hi(b):
                if b >= RING:
                    act.wait_ge(w_loaded[b % RING], 16 * (b // RING))
                    act.wait_ge(w_used, b - RING + 1)
                nc.scalar.copy(of_block(w_hi, b), of_block(w_raw, b)).then_inc(hi_ready, 1)

            for b in range(min(RING, len(blocks))):
                hi(b)
            for u in range(len(units)):
                if u % 2:
                    act.wait_ge(summed, u + 1)
                    nc.scalar.copy(units[u][3], result(u)).then_inc(kept_s, 1)
                if u in ends and ends[u] + RING < len(blocks):
                    hi(ends[u] + RING)


def channel_units(out, tiles):
    return [("channels", m * P, out[:, m, :]) for m in range(tiles)]


def column_blocks(c0, units):
    return [(c0 + P * m, 2 * P, [(kind, place - P * m, out) for kind, place, out in units[m:m + 2]])
            for m in range(0, len(units), 2)]


def token_units(out, tiles):
    return [("tokens", j, out[:, j, :]) for j in range(tiles)]


def stage_gqa_heads(nc, g, proj, q_t, k_t):
    NT, NH, N = T // P, GQA_Q + GQA_KV, (GQA_Q + GQA_KV) * HEAD
    with ExitStack() as stack:
        a = Arena(nc, stack)
        sq = a.sb("sq", [P, NT, N])
        heads = a.sb("heads", [P, NT, N])
        rstd = a.sb("rstd", [P, NT, NH])
        gain = a.sb("gain", [P, 2, HEAD])
        rope = a.sb("rope", [P, 2, 4, 2, 16])
        scratch = a.sb("scratch", [P, 4, NH * 2 * 16])
        loaded, root_in, rooted, ready, transposed, kept, own_v = a.sem(
            "loaded", "root_in", "rooted", "ready", "transposed", "kept", "own_v")
        block = a.block()
        ps = g.ps

        @block.sync
        def _(sp):
            sp.dma_start(gain[:, 0, :], g.d["gqa_qn_g"].to_broadcast([P, HEAD])).then_inc(loaded, 16)
            sp.dma_start(gain[:, 1, :], g.d["gqa_kn_g"].to_broadcast([P, HEAD])).then_inc(loaded, 16)
            sp.dma_start(rope[:], g.d["k_rope_gqa"]).then_inc(loaded, 16)

        @block.vector
        def _(dve):
            own = Steps(dve, own_v)
            own(nc.vector.tensor_tensor(sq[:], proj[:, :, 0:N], proj[:, :, 0:N], ALU.mult))
            own.settle()
            own(nc.vector.tensor_reduce(rstd[:], sq[:].rearrange("p t (h c) -> p t h c", c=HEAD), AX.X, ALU.add))
            own.settle()
            nc.vector.tensor_scalar(rstd[:], rstd[:], 1.0 / HEAD, EPS, ALU.mult, ALU.add).then_inc(root_in, 1)
            dve.wait_ge(rooted, 1)
            own(nc.vector.reciprocal(rstd[:], rstd[:]))
            own.settle()
            own(nc.vector.tensor_scalar(rstd[:, :, 0:GQA_Q], rstd[:, :, 0:GQA_Q], HEAD ** -0.5, None, ALU.mult))
            own.settle()
            for t in range(NT):
                own(nc.vector.tensor_tensor(sq[:, t].rearrange("p (h c) -> p h c", c=HEAD),
                                            proj[:, t, 0:N].rearrange("p (h c) -> p h c", c=HEAD),
                                            rstd[:, t].unsqueeze(2).to_broadcast([P, NH, HEAD]), ALU.mult))
            dve.wait_ge(loaded, 48)
            own.settle()
            for which, h0, nh in ((0, 0, GQA_Q), (1, GQA_Q, GQA_KV)):
                cols = slice(h0 * HEAD, (h0 + nh) * HEAD)
                for out, lo, hi in ((heads, 0, 2), (sq, 2, NT)):
                    for t in range(lo, hi):
                        own(nc.vector.tensor_tensor(out[:, t, cols].rearrange("p (h c) -> p h c", c=HEAD),
                                                    sq[:, t, cols].rearrange("p (h c) -> p h c", c=HEAD),
                                                    gain[:, which, :].unsqueeze(1).to_broadcast([P, nh, HEAD]),
                                                    ALU.mult))
            own.settle()
            dve.sem_inc(ready, 2)
            for t in range(2, NT):
                for axis in range(2):
                    def half(x, i):
                        return x[:, t].rearrange("p (h a i c) -> p h a i c", a=2, i=2, c=16)[:, :, axis, i, :]

                    cos, sin = (rope[:, w, t - 2, axis, :].unsqueeze(1).to_broadcast([P, NH, 16]) for w in range(2))
                    parts = [scratch[:, 2 * axis + w, 0:NH * 16].rearrange("p (h c) -> p h c", c=16)
                             for w in range(2)]
                    parts += [scratch[:, 2 * axis + w, NH * 16:].rearrange("p (h c) -> p h c", c=16)
                              for w in range(2)]
                    own(nc.vector.tensor_tensor(parts[0], half(sq, 0), cos, ALU.mult))
                    own(nc.vector.tensor_tensor(parts[1], half(sq, 1), sin, ALU.mult))
                    own(nc.vector.tensor_tensor(parts[2], half(sq, 0), sin, ALU.mult))
                    own(nc.vector.tensor_tensor(parts[3], half(sq, 1), cos, ALU.mult))
                    own.settle()
                    own(nc.vector.tensor_tensor(half(heads, 0), parts[0], parts[1], ALU.subtract))
                    own(nc.vector.tensor_tensor(half(heads, 1), parts[2], parts[3], ALU.add))
                own.settle()
                dve.sem_inc(ready, 1)

        @block.tensor
        def _(pe):
            for t in range(NT):
                pe.wait_ge(ready, t + 1)
                if t >= 4:
                    pe.wait_ge(kept, t - 3)
                at = (t % 4) * 1024
                for j in range(4):
                    nc.tensor.transpose(ps[:, at + j * P:at + (j + 1) * P], heads[:, t, j * P:(j + 1) * P], g.ident[:])
                nc.tensor.transpose(ps[:, at + 4 * P:at + 5 * P], heads[:, t, GQA_Q * HEAD:N], g.ident[:])\
                    .then_inc(transposed, 1)

        @block.scalar
        def _(act):
            act.wait_ge(root_in, 1)
            nc.scalar.activation(rstd[:], rstd[:], ACT.Sqrt).then_inc(rooted, 1)
            for t in range(NT):
                act.wait_ge(transposed, t + 1)
                at = (t % 4) * 1024
                nc.scalar.copy(q_t[:, :, t * P:(t + 1) * P],
                               ps[:, at:at + 4 * P].rearrange("p (j t) -> p j t", t=P))
                nc.scalar.copy(k_t[:, t * P:(t + 1) * P], ps[:, at + 4 * P:at + 5 * P]).then_inc(kept, 1)


def stage_attention(nc, g, units):
    widest = max(u[1].shape[1] for u in units)
    with ExitStack() as stack:
        a = Arena(nc, stack)
        probs = a.sb("probs", [P, 2, widest])
        probs_t = a.sb("probs_t", [P, 2, widest])
        neg_max = a.sb("neg_max", [P, 2, 1])
        sums = a.sb("sums", [P, 2, 1])
        inverse = a.sb("inverse", [P, 2, 1])
        scores_ready, max_ready, exps_ready, probs_ready, transposed, probs_t_ready, mixed, out_kept, own_v = a.sem(
            "scores_ready", "max_ready", "exps_ready", "probs_ready", "transposed", "probs_t_ready", "mixed",
            "out_kept", "own_v")
        block = a.block()
        ps = g.ps
        n_units = len(units)
        assert widest <= 2 * BANK
        TURN = 4 * BANK

        def scores_at(u, lo, hi):
            return ps[:, (u % 2) * 2 * BANK + lo:(u % 2) * 2 * BANK + hi]

        def output_at(u):
            at = (6 + u // 2 % 2) * BANK
            return slice(at, at + P)

        @block.tensor
        def _(pe):
            def scores(u):
                q, k = units[u][0], units[u][1]
                n = k.shape[1]
                if u >= 2:
                    pe.wait_ge(exps_ready, u - 1)
                for lo, hi in halves(n):
                    last = nc.tensor.matmul(scores_at(u, lo, hi), q, k[:, lo:hi], start=True, stop=True)
                last.then_inc(scores_ready, 1)

            def turn(u):
                pe.wait_ge(probs_ready, u + 1)
                if u:
                    pe.wait_ge(probs_t_ready, u)
                for i in range(units[u][1].shape[1] // P):
                    last = nc.tensor.transpose(ps[:, TURN + i * P:TURN + (i + 1) * P],
                                               probs[:, u % 2, i * P:(i + 1) * P], g.ident[:])
                last.then_inc(transposed, 1)

            def mix(u):
                _, k, v, p0, _ = units[u]
                tiles = k.shape[1] // P
                pe.wait_ge(probs_t_ready, u + 1)
                if u >= 4:
                    pe.wait_ge(out_kept, (u // 2) - 1)
                for i in range(tiles):
                    last = nc.tensor.matmul(ps[p0:p0 + 64, output_at(u)], v(i), probs_t[:, u % 2, i * P:(i + 1) * P],
                                            start=(i == 0), stop=(i == tiles - 1))
                last.then_inc(mixed, 1)

            scores(0)
            for u in range(n_units):
                if u + 1 < n_units:
                    scores(u + 1)
                turn(u)
                if u:
                    mix(u - 1)
            mix(n_units - 1)

        @block.vector
        def _(dve):
            own = Steps(dve, own_v)

            def maximum(u):
                n = units[u][1].shape[1]
                dve.wait_ge(scores_ready, u + 1)
                if u >= 2:
                    dve.wait_ge(exps_ready, u - 1)
                nc.vector.tensor_reduce(neg_max[:, u % 2], scores_at(u, 0, n), AX.X, ALU.max,
                                        negate=True).then_inc(max_ready, 1)

            def normalise(u):
                n = units[u][1].shape[1]
                dve.wait_ge(exps_ready, u + 1)
                own(nc.vector.reciprocal(inverse[:, u % 2], sums[:, u % 2]))
                own.settle()
                nc.vector.tensor_scalar(probs[:, u % 2, 0:n], probs[:, u % 2, 0:n], inverse[:, u % 2], None,
                                        ALU.mult).then_inc(probs_ready, 1)

            def output(u):
                if u % 2 and u > 0:
                    dve.wait_ge(mixed, u + 1)
                    nc.vector.tensor_copy(units[u][4], ps[:, output_at(u)]).then_inc(out_kept, 1)

            maximum(0)
            for u in range(n_units):
                normalise(u)
                if u + 1 < n_units:
                    maximum(u + 1)
                output(u - 2)
            output(n_units - 2)
            output(n_units - 1)

        @block.scalar
        def _(act):
            def exps(u):
                n = units[u][1].shape[1]
                act.wait_ge(max_ready, u + 1)
                if u >= 2:
                    act.wait_ge(transposed, u - 1)
                    act.wait_ge(probs_ready, u - 1)
                nc.scalar.activation(probs[:, u % 2, 0:n], scores_at(u, 0, n), ACT.Exp,
                                     bias=neg_max[:, u % 2], accum_out=sums[:, u % 2]).then_inc(exps_ready, 1)

            def keep_turned(u):
                n = units[u][1].shape[1]
                act.wait_ge(transposed, u + 1)
                if u >= 2:
                    act.wait_ge(mixed, u - 1)
                nc.scalar.copy(probs_t[:, u % 2, 0:n], ps[:, TURN:TURN + n]).then_inc(probs_t_ready, 1)

            exps(0)
            for u in range(n_units):
                if u:
                    keep_turned(u - 1)
                if u + 1 < n_units:
                    exps(u + 1)
            keep_turned(n_units - 1)


def build(nc, d, out, until=99, keep=None):
    class G:
        pass

    g = G()
    Arena.uses.clear()
    Arena.stages = 0
    g.d, g.out = d, out
    g.keep = keep
    with ExitStack() as stack:
        a = Arena(nc, stack)
        psum = stack.enter_context(nc.psum_tensor("banks", [P, 8 * BANK], F32))
        g.ps = psum
        g.ident = a.sb("ident", [P, P])
        g.ones_d = a.sb("ones_d", [P, P])
        g.vec = a.sb("vec", [P, VEC_ROWS])
        g.ada_b = a.sb("ada_bias", [P, 96])
        g.mod = a.sb("mod", [P, 2, 48, 2])
        g.gs = a.sb("gs", [P, 2, 2, DK, 2])
        g.x_t = a.sb("x_t", [P, DK, T])
        stage_load_tokens(nc, g)
        stage_modulation(nc, g)
        if until >= 1:
            layer_even(nc, g, until)
        if until >= 8:
            layer_odd(nc, g, until)


HG_LEVELS = (64, 32, 16, 8, 4, 2, 1)
NL = len(HG_LEVELS) + 1


def stage_hgrn2_gates(nc, g, hg, forget, keep_k, cum):
    N = HG_HEADS * T
    with ExitStack() as stack:
        a = Arena(nc, stack)
        lb = a.sb("lb", [P, 5, 2, HG_HEADS])
        restart = a.sb("restart", [P, 2, T])
        gate_ready, sig_ready, f_ready, log_ready, lb_in, lb_exp, own_v, cum_done = a.sem(
            "gate_ready", "sig_ready", "f_ready", "log_ready", "lb_in", "lb_exp", "own_v", "cum_done")
        block = a.block()
        at = VEC["lb"][0]
        logits = g.vec[:, at:at + 16].rearrange("p (d e h) -> p d e h", d=2, e=2)

        @block.scalar
        def _(act):
            act.wait_ge(lb_in, 2)
            nc.scalar.activation(lb[:, 0:2], lb[:, 0:2], ACT.Exp).then_inc(lb_exp, 1)
            for d in range(2):
                nc.scalar.activation(keep_k[:, d * 4:d * 4 + 4], hg[:, 1 + d], ACT.Sigmoid).then_inc(sig_ready, 1)
            for d in range(2):
                act.wait_ge(f_ready, d + 1)
                if d:
                    act.wait_ge(cum_done, 1)
                nc.scalar.activation(forget[:], keep_k[:, d * 4:d * 4 + 4], ACT.Ln).then_inc(log_ready, 1)

        @block.vector
        def _(dve):
            own = Steps(dve, own_v)
            own(nc.vector.tensor_tensor(lb[:, 2], logits[:, :, 0], logits[:, :, 1], ALU.max))
            own.settle()
            for e in range(2):
                nc.vector.tensor_tensor(lb[:, e], logits[:, :, e], lb[:, 2], ALU.subtract).then_inc(lb_in, 1)
            for d in range(2):
                own(nc.vector.memset(restart[:, d], 1.0))
            own.settle()
            own(nc.vector.memset(restart[:, 0].rearrange("p (n t) -> p n t", t=P)[:, :, 0:1], 0.0))
            own(nc.vector.memset(restart[:, 1].rearrange("p (n t) -> p n t", t=P)[:, :, P - 1:P], 0.0))
            dve.wait_ge(lb_exp, 1)
            own(nc.vector.tensor_tensor(lb[:, 3], lb[:, 0], lb[:, 1], ALU.add))
            own.settle()
            own(nc.vector.reciprocal(lb[:, 3], lb[:, 3]))
            own.settle()
            own(nc.vector.tensor_tensor(lb[:, 4], lb[:, 0], lb[:, 3], ALU.mult))
            own.settle()
            own(nc.vector.tensor_scalar(lb[:, 3], lb[:, 4], -1.0, 1.0, ALU.mult, ALU.add))
            own.settle()
            for d in range(2):
                dve.wait_ge(sig_ready, d + 1)
                for h in range(HG_HEADS):
                    own(nc.vector.tensor_scalar(keep_k[:, d * 4 + h], keep_k[:, d * 4 + h], lb[:, 3, d, h:h + 1],
                                                lb[:, 4, d, h:h + 1], ALU.mult, ALU.add))
                own.settle()
                nc.vector.tensor_scalar(keep_k[:, d * 4:d * 4 + 4], keep_k[:, d * 4:d * 4 + 4], 1e-19, None,
                                        ALU.max).then_inc(f_ready, 1)
            for d in range(2):
                dve.wait_ge(log_ready, d + 1)
                own(nc.vector.tensor_scalar(keep_k[:, d * 4:d * 4 + 4], keep_k[:, d * 4:d * 4 + 4], -1.0, 1.0,
                                            ALU.mult, ALU.add))
                for h in range(HG_HEADS):
                    src, out = forget[:, h], cum[:, d * 4 + h]
                    if d:
                        src, out = src[:, ::-1], out[:, ::-1]
                    last = nc.vector.tensor_tensor_scan(out, restart[:, d][:, ::-1] if d else restart[:, d], src,
                                                        0.0, ALU.mult, ALU.add)
                    if h < HG_HEADS - 1:
                        own(last)
                last.then_inc(cum_done, 1)


def stage_hgrn2_scan(nc, g, hg, hg_v, keep_k, cum, y_t):
    NC = T // P
    units = [(d, h) for d in range(2) for h in range(HG_HEADS)]
    orders = [list(range(NC)), [1, 0] + list(range(NC - 1, 1, -1))]
    with ExitStack() as stack:
        a = Arena(nc, stack)
        masks = a.sb("masks", [P, NL * P])
        z_even = a.sb("z", [P, len(HG_LEVELS), T])
        expo = a.sb("expo", [P, 2, T])
        q_dec_even = a.sb("q_dec", [P, T])
        k_dec = a.sb("k_dec", [P, T])
        k_tok = a.sb("k_tok", [P, T])
        last_decs = a.sb("last_dec", [P, 2, NC])
        spent = hg[:, 1:3].rearrange("p d h t -> p (d h) t")
        z_of = (z_even[:], spent[:, 0:len(HG_LEVELS)])
        q_dec_of = (q_dec_even[:], spent[:, len(HG_LEVELS)])
        state = a.sb("state", [P, 2, P])
        pairs = a.sb("pairs", [P, 2, NL * P])
        (mask_loaded, expo_in, expo_out, z_ready, multiplied, k_turned, k_tok_ready, gram_ready, pairs_ready,
         out_ready, out_kept, update_ready, state_ready, own_v) = a.sem(
            "mask_loaded", "expo_in", "expo_out", "z_ready", "multiplied", "k_turned", "k_tok_ready", "gram_ready",
            "pairs_ready", "out_ready", "out_kept", "update_ready", "state_ready", "own_v")
        block = a.block()
        ps = g.ps
        E = len(HG_LEVELS) + 2
        GRAM, TURN, OUT, UPD = 0, 4 * BANK, 6 * BANK, 7 * BANK

        def sides(m, x, d):
            v = x.rearrange("p (b i t) -> p b i t", i=2, t=m)
            r = v[:, :, 0, m - 1:m] if d == 0 else v[:, :, 1, 0:1]
            return v[:, :, 1 - d, :], v[:, :, d, :], r.to_broadcast([P, T // (2 * m), m])

        shares = [range(E * i // NC, E * (i + 1) // NC) for i in range(NC)]

        @block.sync
        def _(sp):
            for d in range(2):
                if d:
                    sp.wait_ge(pairs_ready, HG_HEADS * NC)
                sp.dma_start(masks[:], g.d["k_hg_masks"][d]).then_inc(mask_loaded, 16)

        @block.scalar
        def _(act):
            def exponentials(u, steps):
                for e in steps:
                    act.wait_ge(expo_in, u * E + e + 1)
                    d, h = units[u]
                    source = cum[:, d * 4 + h] if e == len(HG_LEVELS) else expo[:, e % 2]
                    nc.scalar.activation(expo[:, e % 2], source, ACT.Exp).then_inc(expo_out, 1)

            exponentials(0, range(E))
            for u, (d, h) in enumerate(units):
                act.wait_ge(k_turned, u + 1)
                nc.scalar.copy(k_tok[:], ps[:, TURN:TURN + T]).then_inc(k_tok_ready, 1)
                for i, c in enumerate(orders[d]):
                    if u + 1 < len(units):
                        exponentials(u + 1, shares[i])
                    if d == 0:
                        act.wait_ge(out_ready, u * NC + i + 1)
                        nc.scalar.copy(y_t[:, 4 + h, c * P:(c + 1) * P], ps[:, OUT:OUT + P]).then_inc(out_kept, 1)

        @block.gpsimd
        def _(pool):
            for u, (d, h) in enumerate(units):
                q, k = hg[:, 0, h], keep_k[:, d * 4 + h]
                if u >= 2:
                    pool.wait_ge(out_ready, (u - 1) * NC)
                for e in range(E):
                    x = expo[:, e % 2]
                    pool.wait_ge(expo_out, u * E + e + 1)
                    if e < len(HG_LEVELS):
                        m = HG_LEVELS[e]
                        nc.gpsimd.tensor_tensor(sides(m, z_of[u % 2][:, e], d)[1], sides(m, x, d)[1],
                                                sides(m, k, d)[1], ALU.mult).then_inc(multiplied, 1)
                    elif e == len(HG_LEVELS):
                        nc.gpsimd.tensor_tensor(q_dec_of[u % 2], x, q, ALU.mult).then_inc(multiplied, 1)
                    else:
                        if u:
                            pool.wait_ge(k_turned, u)
                        nc.gpsimd.tensor_tensor(k_dec[:], x, k, ALU.mult).then_inc(multiplied, 1)

        @block.vector
        def _(dve):
            own = Steps(dve, own_v)

            def prepare(u, steps):
                d, h = units[u]
                q, c = hg[:, 0, h], cum[:, d * 4 + h]
                z, last_dec = z_of[u % 2], last_decs[:, u % 2]
                last_of = c.rearrange("p (n t) -> p n t", t=P)[:, :, 0:1] if d else \
                    c.rearrange("p (n t) -> p n t", t=P)[:, :, P - 1:P]

                def differences(e):
                    if u or e >= 2:
                        own.settle()
                        dve.wait_ge(multiplied, u * E + e - 1 if e else u * E)
                    x = expo[:, e % 2]
                    if e < len(HG_LEVELS):
                        m = HG_LEVELS[e]
                        cq, ck, r = sides(m, c, d)
                        xq, xk, _ = sides(m, x, d)
                        own(nc.vector.tensor_tensor(xq, cq, r, ALU.subtract))
                        nc.vector.tensor_tensor(xk, r, ck, ALU.subtract).then_inc(expo_in, 1)
                    elif e == len(HG_LEVELS):
                        dve.sem_inc(expo_in, 1)
                    else:
                        nc.vector.tensor_tensor(x.rearrange("p (n t) -> p n t", t=P), last_of.to_broadcast([P, NC, P]),
                                                c.rearrange("p (n t) -> p n t", t=P), ALU.subtract).then_inc(expo_in, 1)

                if u >= 2 and 0 in steps:
                    dve.wait_ge(out_ready, (u - 1) * NC)
                if 0 in steps:
                    differences(0)
                for e in steps:
                    if e + 1 < E:
                        differences(e + 1)
                    dve.wait_ge(expo_out, u * E + e + 1)
                    x = expo[:, e % 2]
                    if e < len(HG_LEVELS):
                        m = HG_LEVELS[e]
                        own(nc.vector.tensor_tensor(sides(m, z[:, e], d)[0], sides(m, x, d)[0], sides(m, q, d)[0],
                                                    ALU.mult))
                        if e == len(HG_LEVELS) - 1:
                            own.settle()
                            dve.sem_inc(z_ready, 1)
                    elif e == len(HG_LEVELS):
                        own(nc.vector.tensor_copy(last_dec.unsqueeze(2),
                                                  x.rearrange("p (n t) -> p n t", t=P)[:, :, 0:1] if d else
                                                  x.rearrange("p (n t) -> p n t", t=P)[:, :, P - 1:P]))

            prepare(0, range(E))
            for u, (d, h) in enumerate(units):
                last_dec = last_decs[:, u % 2]

                def mask_pairs(i, u=u):
                    n = u * NC + i
                    dve.wait_ge(gram_ready, n + 1)
                    if n >= 2:
                        dve.wait_ge(out_ready, n - 1)
                    nc.vector.tensor_tensor(pairs[:, n % 2], ps[:, GRAM + (n % 2) * 1024:GRAM + (n % 2) * 1024 + 1024],
                                            masks[:], ALU.mult).then_inc(pairs_ready, 1)

                dve.wait_ge(mask_loaded, 16 * (d + 1))
                mask_pairs(0)
                for i, ch in enumerate(orders[d]):
                    n = u * NC + i
                    if i + 1 < NC:
                        mask_pairs(i + 1)
                    dve.wait_ge(update_ready, n + 1)
                    if i >= 1:
                        dve.wait_ge(state_ready, n)
                    if i == 0:
                        nc.vector.tensor_copy(state[:, i % 2], ps[:, UPD:UPD + P]).then_inc(state_ready, 1)
                    else:
                        nc.vector.scalar_tensor_tensor(out=state[:, i % 2], in0=state[:, 1 - i % 2],
                                                       scalar=last_dec[:, ch:ch + 1], in1=ps[:, UPD:UPD + P],
                                                       op0=ALU.mult, op1=ALU.add).then_inc(state_ready, 1)
                    if d == 1:
                        dve.wait_ge(out_ready, n + 1)
                        out = y_t[:, 4 + h, ch * P:(ch + 1) * P]
                        nc.vector.tensor_tensor(out, out, ps[:, OUT:OUT + P], ALU.add).then_inc(out_kept, 1)
                    if u + 1 < len(units):
                        prepare(u + 1, shares[i])

        @block.tensor
        def _(pe):
            for u, (d, h) in enumerate(units):
                unit = d * 4 + h
                z, q_dec = z_of[u % 2], q_dec_of[u % 2]
                pe.wait_ge(multiplied, (u + 1) * E)
                if u:
                    pe.wait_ge(k_tok_ready, u)
                for c in range(NC):
                    last = nc.tensor.transpose(ps[:, TURN + c * P:TURN + (c + 1) * P], k_dec[:, c * P:(c + 1) * P],
                                               g.ident[:])
                last.then_inc(k_turned, 1)

                def gram(i, u=u, d=d, h=h, unit=unit, z=z):
                    n = u * NC + i
                    t = slice(orders[d][i] * P, (orders[d][i] + 1) * P)
                    at = GRAM + (n % 2) * 1024
                    if n >= 2:
                        pe.wait_ge(pairs_ready, n - 1)
                    for e in range(len(HG_LEVELS)):
                        nc.tensor.matmul(ps[:, at + e * P:at + (e + 1) * P], z[:, e, t], z[:, e, t],
                                         start=True, stop=True)
                    e = NL - 1
                    nc.tensor.matmul(ps[:, at + e * P:at + (e + 1) * P], keep_k[:, unit, t], hg[:, 0, h, t],
                                     start=True, stop=True).then_inc(gram_ready, 1)

                pe.wait_ge(z_ready, u + 1)
                gram(0)
                pe.wait_ge(k_tok_ready, u + 1)
                for i, c in enumerate(orders[d]):
                    n = u * NC + i
                    if i + 1 < NC:
                        gram(i + 1)
                    v = hg_v[:, c, h * P:(h + 1) * P]
                    if n:
                        pe.wait_ge(state_ready, n)
                    nc.tensor.matmul(ps[:, UPD:UPD + P], k_tok[:, c * P:(c + 1) * P], v, start=True, stop=True)\
                        .then_inc(update_ready, 1)
                    pe.wait_ge(pairs_ready, n + 1)
                    if n:
                        pe.wait_ge(out_kept, n)
                    if i:
                        nc.tensor.matmul(ps[:, OUT:OUT + P], state[:, 1 - i % 2], q_dec[:, c * P:(c + 1) * P],
                                         start=True, stop=False)
                    for e in range(NL):
                        last = nc.tensor.matmul(ps[:, OUT:OUT + P], v, pairs[:, n % 2, e * P:(e + 1) * P],
                                                start=(i == 0 and e == 0), stop=(e == NL - 1))
                    last.then_inc(out_ready, 1)


def stage_hgrn2_readout(nc, g, hg, y_t, w, w_rows):
    with ExitStack() as stack:
        a = Arena(nc, stack)
        sq = a.sb("sq", [P, HG_HEADS, T])
        silu = hg[:, 3]
        squared, summed, root_in, rooted, silu_ready, normed, w_loaded, own_v = a.sem(
            "squared", "summed", "root_in", "rooted", "silu_ready", "normed", "w_loaded", "own_v")
        block = a.block()
        ps = g.ps
        gain = g.vec[:, VEC["onorm"][0]:VEC["onorm"][0] + 1]

        @block.sync
        def _(sp):
            load_rows(sp, w, w_rows, w_loaded)
            sp.wait_ge(w_loaded, 16 * len(w_rows))

        @block.scalar
        def _(act):
            for h in range(HG_HEADS):
                nc.scalar.activation(sq[:, h], y_t[:, 4 + h], ACT.Square).then_inc(squared, 1)
            for h in range(HG_HEADS):
                act.wait_ge(root_in, h + 1)
                nc.scalar.activation(sq[:, h], sq[:, h], ACT.Sqrt).then_inc(rooted, 1)
            nc.scalar.activation(silu, hg[:, 3], ACT.Silu).then_inc(silu_ready, 1)

        @block.tensor
        def _(pe):
            for h in range(HG_HEADS):
                pe.wait_ge(squared, h + 1)
                for lo, hi in halves(T):
                    last = nc.tensor.matmul(ps[:, h * 1024 + lo:h * 1024 + hi], g.ones_d[:], sq[:, h, lo:hi],
                                            start=True, stop=True)
                last.then_inc(summed, 1)

        @block.vector
        def _(dve):
            own = Steps(dve, own_v)
            for h in range(HG_HEADS):
                dve.wait_ge(summed, h + 1)
                nc.vector.tensor_scalar(sq[:, h], ps[:, h * 1024:h * 1024 + T], float(D // P), EPS,
                                        ALU.mult, ALU.add).then_inc(root_in, 1)
            for h in range(HG_HEADS):
                dve.wait_ge(rooted, h + 1)
                own(nc.vector.reciprocal(sq[:, h], sq[:, h]))
                own.settle()
                nc.vector.scalar_tensor_tensor(out=y_t[:, 4 + h], in0=y_t[:, 4 + h], scalar=gain,
                                               in1=sq[:, h], op0=ALU.mult, op1=ALU.mult).then_inc(normed, 1)

        @block.gpsimd
        def _(pool):
            pool.wait_ge(silu_ready, 1)
            for h in range(HG_HEADS):
                pool.wait_ge(normed, h + 1)
                nc.gpsimd.tensor_tensor(y_t[:, 4 + h], y_t[:, 4 + h], silu[:, h], ALU.mult)


def load_rows(engine, w, w_rows, loaded):
    for parts, k, rows in w_rows:
        engine.dma_start(w[parts, k, :], rows).then_inc(loaded, 16)


def stage_mix_out(nc, g, layer, y_t, t0, w):
    n = T - t0
    with ExitStack() as stack:
        a = Arena(nc, stack)
        summed, kept = a.sem("summed", "kept")
        block = a.block()
        ps = g.ps

        @block.tensor
        def _(pe):
            for m in range(DK):
                if m >= 4:
                    pe.wait_ge(kept, m - 3)
                at = (m % 4) * 1024
                for k in range(DK):
                    for lo, hi in halves(n):
                        last = nc.tensor.matmul(ps[:, at + lo:at + hi], w[:, k, m * P:(m + 1) * P], y_t[:, k, lo:hi],
                                                start=(k == 0), stop=(k == DK - 1))
                last.then_inc(summed, 1)

        @block.vector
        def _(dve):
            for m in range(DK):
                dve.wait_ge(summed, m + 1)
                at = (m % 4) * 1024
                for s, b, e in STREAMS:
                    if e > t0:
                        b = max(b, t0)
                        last = nc.vector.scalar_tensor_tensor(
                            out=g.x_t[:, m, b:e], in0=ps[:, at + b - t0:at + e - t0],
                            scalar=g.mod[:, layer, 16 + m, s:s + 1], in1=g.x_t[:, m, b:e],
                            op0=ALU.mult, op1=ALU.add)
                last.then_inc(kept, 1)


TB = 32


def stage_scores(nc, g, layer, q_t, scores_d, x_d, n):
    NT, G2 = n // P, 2 * PEER_H
    with ExitStack() as stack:
        a = Arena(nc, stack)
        keys = a.sb("keys", [P, G2, P])
        keys_t = a.sb("keys_t", [P, G2, P])
        score = a.sb("score_out", [P, 2, G2, P])
        loaded, keys_turned, keys_ready, scored, score_ready = a.sem(
            "loaded", "keys_turned", "keys_ready", "scored", "score_ready")
        stored = [a.sem(f"stored{b}") for b in range(2)]
        x_stored = a.sem("x_stored")
        block = a.block()
        ps = g.ps

        @block.sync
        def _(sp):
            sp.dma_start(keys[:], g.d["peer_keys"][layer].rearrange("h s n k -> n (h s) k")).then_inc(loaded, 16)
            sp.dma_start(x_d, g.x_t[:]).then_inc(x_stored, 16)
            for t in range(NT):
                sp.wait_ge(score_ready, t + 1)
                sp.dma_start(scores_d[t], score[:, t % 2]).then_inc(stored[t % 2], 16)
            for b in range(2):
                sp.wait_ge(stored[b], 16 * (NT // 2))
            sp.wait_ge(x_stored, 16)

        @block.tensor
        def _(pe):
            pe.wait_ge(loaded, 16)
            for i in range(G2):
                last = nc.tensor.transpose(ps[:, i * P:(i + 1) * P], keys[:, i], g.ident[:])
            last.then_inc(keys_turned, 1)
            pe.wait_ge(keys_ready, 1)
            for t in range(NT):
                if t >= 2:
                    pe.wait_ge(score_ready, t - 1)
                at = (t % 2) * 4 * BANK
                for i in range(G2):
                    last = nc.tensor.matmul(ps[:, at + i * P:at + (i + 1) * P], q_t[:, i, t * P:(t + 1) * P],
                                            keys_t[:, i], start=True, stop=True)
                last.then_inc(scored, 1)

        @block.scalar
        def _(act):
            act.wait_ge(keys_turned, 1)
            nc.scalar.copy(keys_t[:], ps[:, 0:4 * BANK].rearrange("p (g n) -> p g n", n=P)).then_inc(keys_ready, 1)
            for t in range(NT):
                at = (t % 2) * 4 * BANK
                act.wait_ge(scored, t + 1)
                if t >= 2:
                    act.wait_ge(stored[t % 2], 16 * (t // 2))
                nc.scalar.copy(score[:, t % 2], ps[:, at:at + 4 * BANK].rearrange("p (g n) -> p g n", n=P))\
                    .then_inc(score_ready, 1)


def stage_route_and_activate(nc, g, layer, hi, lo, scores_d, acts_d, table, n):
    NT, G2 = n // P, 2 * PEER_H
    BODIES = KEYS // 2
    ROUTE_BODIES = 4 if NT > 4 else 5
    QUAD = 4
    GATE_BLOCKS = n // TB
    PARTS = 1 if NT > 4 else 2
    cols = halves(n)
    u_rows = g.d["peer_u"][layer].rearrange("(a b) d -> a b d", b=KEYS)
    with ExitStack() as stack:
        a = Arena(nc, stack)
        room = g.x_t[:].rearrange("p k t -> p (k t)")
        score = room[:, 0:2048].rearrange("p (g n) -> p g n", n=P)
        rest = room[:, 2048:4096].rearrange("p (g n) -> p g n", n=P)
        cand = room[:, 4096:6144].rearrange("p (h c) -> p h c", h=PEER_H)
        cand_rest = room[:, 2048:4096].rearrange("p (h c) -> p h c", h=PEER_H)
        hot = room[:, 4096:6144].rearrange("p (s a) -> p s a", a=TOPK)
        best = a.sb("best", [P, G2, TOPK])
        best_at = a.sb("best_at", [P, G2, TOPK], U32)
        best_key = a.sb("best_key", [P, G2, TOPK])
        top = a.sb("top", [P, PEER_H, TOPK])
        top_at = a.sb("top_at", [P, PEER_H, TOPK], U32)
        pick = a.sb("pick", [P, 2, SLOTS], U32)
        pick_f = a.sb("pick_f", [P, 2, SLOTS])
        found = a.sb("found", [P, 3, SLOTS])
        iota = a.sb("iota", [P, P])
        head_ones = a.sb("head_ones", [P, P])
        slots = a.sb("slots", [P, 4, n])
        w_hi = a.sb("slot_hi", [P, n], F32R)
        first_hot = a.sb("first_hot", [P, 2, QUAD, P], F32R)
        hot_hi = a.sb("hot_hi", [P, 2, QUAD, P], F32R)
        hot_lo = a.sb("hot_lo", [P, 2, QUAD, P], F32R)
        part = a.sb("part", [P, 2, P, TB])
        u_raw = a.sb("u_raw", [P, 2, D])
        u_hi = a.sb("u_hi", [P, 2, D], F32R)
        u_lo = a.sb("u_lo", [P, 2, D], F32R)
        ut_hi = a.sb("ut_hi", [P, 2, D], F32R)
        ut_lo = a.sb("ut_lo", [P, 2, D], F32R)
        acts = a.sb("acts", [P, 2, n])
        ident_r = a.sb("ident_r", [P, P], F32R)

        def two(name):
            return [a.sem(f"{name}{r}") for r in range(2)]

        u_loaded, u_hi_ready, u_lo_ready, turned, ut_ready, acts_stored = map(
            two, ("u_loaded", "u_hi_ready", "u_lo_ready", "turned", "ut_ready", "acts_stored"))
        LAST = len(cols) - 1
        acted, gelued = ([two(f"{name}_{c}_") for c in range(LAST + 1)] for name in ("acted", "gelued"))
        hot_ready, multiplied, kept, part_stored = map(two, ("hot_ready", "multiplied", "kept", "part_stored"))
        (loaded, ident_ready, score_loaded, score_used, found_ready, found_turned, found_used, soft_ready,
         soft_summed, own_v) = a.sem(
            "loaded", "ident_ready", "score_loaded", "score_used", "found_ready", "found_turned", "found_used",
            "soft_ready", "soft_summed", "own_v")
        block = a.block()
        ps = g.ps
        TURN_HI, TURN_LO, ACTS, GATE = 0, 2 * BANK, 4 * BANK, 6 * BANK
        TWO_ACTS = n <= BANK

        def acts_at(r, b, e):
            at = ACTS + (r * BANK if TWO_ACTS else 0)
            return ps[:, at + b:at + e]


        def nothing(*_):
            pass

        def octets(gate, r):
            return [] if gate is None else [2 * r, 2 * r + 1] if PARTS == 1 else [2 * gate[4] + r]

        def segments(engine, body, after_tile=nothing, after_soft=nothing, after_gates=nothing):
            body(0, None, True, False)
            body(1, None, False, False)
            at = 1
            for t in range(NT):
                with engine.Fori(at + (t == 0), at + ROUTE_BODIES) as i:
                    body(i, None, False, False)
                at += ROUTE_BODIES
                after_tile(t)
            body(at, None, False, False)
            after_soft()
            body(at + 1, None, False, False)
            at += 2
            for r in range(2):
                for p in range(PARTS):
                    body(at + r * PARTS + p, (r, r, 0, True, p), False, False)
            with engine.Fori(1, GATE_BLOCKS // 2) as i:
                for r in range(2):
                    for p in range(PARTS):
                        body(i * (2 * PARTS) + (at + r * PARTS + p), (i * 2 + r, r, i, False, p), False, False)
            at += GATE_BLOCKS * PARTS
            after_gates()
            with engine.Fori(at, BODIES - 1) as i:
                body(i, None, False, False)
            body(BODIES - 1, None, False, True)

        @block.sync
        def _(sp):
            sp.dma_start(iota[:], g.d["k_iota"]).then_inc(loaded, 16)
            sp.dma_start(head_ones[:], g.d["k_head_ones"]).then_inc(loaded, 16)
            sp.dma_start(score, scores_d[0]).then_inc(score_loaded, 16)

            def load(r, i):
                sp.dma_start(u_raw[:, r:r + 1], u_rows[:, bass.ds(i * 2 + r, 1), :]).then_inc(u_loaded[r], 16)

            def store(r, i):
                for c in range(LAST + 1):
                    sp.wait_ge(gelued[c][r], i + 1)
                sp.dma_start(acts_d[bass.ds(i * 2 + r, 1)].rearrange("o p n -> (o p) n"), acts[:, r])\
                    .then_inc(acts_stored[r], 16)

            def store_part(r, index):
                for b in range(2):
                    sp.wait_ge(kept[b], index * 4 + 4)
                sp.dma_start(table[:, bass.ds(index, 1)], part[:, r:r + 1]).then_inc(part_stored[r], 16)

            def body(i, gate, first, last):
                if not last:
                    sp.wait_ge(u_lo_ready[0], i + 1)
                    load(0, i + 1)
                if not first:
                    store(1, i - 1)
                if not last:
                    sp.wait_ge(u_lo_ready[1], i + 1)
                    load(1, i + 1)
                store(0, i)
                if gate and gate[4] == 0 and not (gate[3] and gate[1] == 0):
                    store_part(1 - gate[1], gate[0] - 1)
                if last:
                    store(1, i)

            def next_scores(t):
                if t + 1 < NT:
                    sp.wait_ge(score_used, t + 1)
                    sp.dma_start(score, scores_d[t + 1]).then_inc(score_loaded, 16)

            load(0, 0)
            load(1, 0)
            segments(sp, body, after_tile=next_scores, after_gates=lambda: store_part(1, GATE_BLOCKS - 1))
            for r in range(2):
                sp.wait_ge(acts_stored[r], 16 * BODIES)
                sp.wait_ge(part_stored[r], 16 * (GATE_BLOCKS // 2))

        @block.tensor
        def _(pe):
            def turn(r, i, first=False):
                pe.wait_ge(u_lo_ready[r], i + 1)
                if not first:
                    pe.wait_ge(ut_ready[1 - r], i + 1 - (1 - r))
                for at, u in ((TURN_HI, u_hi), (TURN_LO, u_lo)):
                    for k in range(DK):
                        last = nc.tensor.transpose(ps[:, at + k * P:at + (k + 1) * P].bitcast(F32R),
                                                   u[:, r, k * P:(k + 1) * P], ident_r[:])
                last.then_inc(turned[r], 1)

            def octet(index, start=False):
                for b in range(2):
                    pe.wait_ge(hot_ready[b], index + 1)
                    if not start:
                        pe.wait_ge(kept[b], index)
                    for q in range(QUAD):
                        out = ps[:, GATE + b * BANK + q * P:GATE + b * BANK + (q + 1) * P]
                        nc.tensor.matmul(out, first_hot[:, b, q], hot_hi[:, b, q], start=True, stop=False)
                        last = nc.tensor.matmul(out, first_hot[:, b, q], hot_lo[:, b, q], start=False, stop=True)
                    last.then_inc(multiplied[b], 1)

            def products(r, i, first, c, ks):
                if 0 in ks:
                    if TWO_ACTS and not first:
                        pe.wait_ge(gelued[c][r], i)
                    elif not TWO_ACTS and not (first and r == 0):
                        pe.wait_ge(gelued[c][1 - r], i + 1 - (1 - r))
                b, e = cols[c]
                for k in ks:
                    for u, h in ((ut_hi, hi), (ut_hi, lo), (ut_lo, hi)):
                        last = nc.tensor.matmul(acts_at(r, b, e), u[:, r, k * P:(k + 1) * P], h[:, k, b:e],
                                                start=(k == 0 and u is ut_hi and h is hi),
                                                stop=(k == DK - 1 and u is ut_lo))
                if DK - 1 in ks:
                    last.then_inc(acted[c][r], 1)

            def body(i, gate, first, last):
                for r in range(2):
                    if r == 0:
                        turn(1, i)
                    elif not last:
                        turn(0, i + 1)
                    for o in octets(gate, r)[:1]:
                        octet(gate[0] * 4 + o, start=gate[3] and gate[1] == 0 and o == 0)
                    pe.wait_ge(ut_ready[r], i + 1)
                    firsts, seconds = ((([(0, range(0, 4))], [(0, range(4, DK))]) if LAST == 0 else
                                        ([(0, range(DK))], [(1, range(DK))])))
                    for c, ks in firsts:
                        products(r, i, first, c, ks)
                    for o in octets(gate, r)[1:]:
                        octet(gate[0] * 4 + o)
                    for c, ks in seconds:
                        products(r, i, first, c, ks)

            def turn_found(t):
                pe.wait_ge(found_ready, t + 1)
                if t:
                    pe.wait_ge(found_used, t)
                for i in range(3):
                    last = nc.tensor.transpose(ps[:, GATE + i * P:GATE + (i + 1) * P], found[:, i], g.ident[:])
                last.then_inc(found_turned, 1)

            def sum_heads():
                pe.wait_ge(soft_ready, 1)
                for b, e in cols:
                    last = nc.tensor.matmul(ps[:, GATE + b:GATE + e], head_ones[:], slots[:, 2, b:e],
                                            start=True, stop=True)
                last.then_inc(soft_summed, 1)

            pe.wait_ge(ident_ready, 1)
            pe.wait_ge(loaded, 32)
            turn(0, 0, True)
            segments(pe, body, after_tile=turn_found, after_soft=sum_heads)

        @block.scalar
        def _(act):
            def round_u(r, i, first=False):
                act.wait_ge(u_loaded[r], (i + 1) * 16)
                if not first:
                    act.wait_ge(turned[r], i)
                nc.scalar.copy(u_hi[:, r], u_raw[:, r]).then_inc(u_hi_ready[r], 1)

            def turned_out(r, i, first=False):
                act.wait_ge(turned[r], i + 1)
                if not first:
                    act.wait_ge(acted[LAST][r], i)
                nc.scalar.copy(ut_hi[:, r], ps[:, TURN_HI:TURN_HI + D])
                nc.scalar.copy(ut_lo[:, r], ps[:, TURN_LO:TURN_LO + D]).then_inc(ut_ready[r], 1)

            def gelu(r, i, c, first=False):
                act.wait_ge(acted[c][r], i + 1)
                if c == 0 and not first:
                    act.wait_ge(acts_stored[r], i * 16)
                b, e = cols[c]
                nc.scalar.activation(acts[:, r, b:e], acts_at(r, b, e), ACT.Gelu).then_inc(gelued[c][r], 1)

            def gates_out(gate, octet):
                for b in range(2):
                    act.wait_ge(multiplied[b], gate[0] * 4 + octet + 1)
                    t = (2 * octet + b) * QUAD
                    nc.scalar.copy(part[:, gate[1], :, t:t + QUAD],
                                   ps[:, GATE + b * BANK:GATE + (b + 1) * BANK].rearrange("p (t m) -> p m t", m=P))\
                        .then_inc(kept[b], 1)

            def body(i, gate, first, last):
                for r in range(2):
                    if r == 0:
                        if not first:
                            gelu(1, i - 1, LAST, isinstance(i, int) and i == 1)
                    else:
                        gelu(0, i, LAST, first)
                    if not last:
                        round_u(r, i + 1)
                    for o in octets(gate, r)[:1]:
                        if o == 0 and not gate[3]:
                            act.wait_ge(part_stored[gate[1]], gate[2] * 16)
                        gates_out(gate, o)
                    if r == 0:
                        turned_out(1, i, first)
                    elif not last:
                        turned_out(0, i + 1)
                    for o in octets(gate, r)[1:]:
                        gates_out(gate, o)
                    if LAST:
                        gelu(r, i, 0, first)
                if last:
                    gelu(1, i, LAST)

            def keep_found(t):
                act.wait_ge(found_turned, t + 1)
                nc.scalar.copy(slots[:, 0:3, t * P:(t + 1) * P],
                               ps[:, GATE:GATE + 3 * P].rearrange("p (i t) -> p i t", t=P)).then_inc(found_used, 1)
                if t == NT - 1:
                    act.wait_ge(found_used, NT)
                    nc.scalar.activation(slots[:, 2], slots[:, 2], ACT.Exp).then_inc(soft_ready, 1)

            act.wait_ge(loaded, 32)
            nc.scalar.copy(ident_r[:], g.ident[:]).then_inc(ident_ready, 1)
            round_u(0, 0, True)
            round_u(1, 0, True)
            turned_out(0, 0, True)
            segments(act, body, after_tile=keep_found)

        @block.gpsimd
        def _(pool):
            def body(i):
                for r in range(2):
                    pool.wait_ge(u_hi_ready[r], i + 1)
                    nc.gpsimd.tensor_tensor(u_lo[:, r], u_raw[:, r], u_hi[:, r].bitcast(F32), ALU.subtract)\
                        .then_inc(u_lo_ready[r], 1)

            body(0)
            with pool.Fori(1, BODIES) as i:
                body(i)

        @block.vector
        def _(dve):
            own = Steps(dve, own_v)

            def sixteen(values, without, out, at, groups):
                for i in range(groups):
                    own(nc.vector.max(out[:, i, 0:8], values[:, i]))
                own.settle()
                for i in range(groups):
                    own(nc.vector.match_replace(without[:, i], out[:, i, 0:8], values[:, i], LOWEST))
                    own(nc.vector.max_index(at[:, i, 0:8], out[:, i, 0:8], values[:, i]))
                own.settle()
                for i in range(groups):
                    own(nc.vector.max(out[:, i, 8:16], without[:, i]))
                own.settle()
                for i in range(groups):
                    own(nc.vector.max_index(at[:, i, 8:16], out[:, i, 8:16], without[:, i]))
                own.settle()

            dve.wait_ge(loaded, 32)
            for t in range(NT):
                dve.wait_ge(score_loaded, 16 * (t + 1))
                sixteen(score, rest, best, best_at, G2)
                dve.sem_inc(score_used, 1)
                own(nc.vector.tensor_copy(best_key[:], best_at[:]))
                sides = best[:].rearrange("p (h s) k -> p h s k", s=2)
                own(nc.vector.tensor_tensor(cand.rearrange("p h (a b) -> p h a b", a=TOPK),
                                            sides[:, :, 0, :].unsqueeze(3).to_broadcast([P, PEER_H, TOPK, TOPK]),
                                            sides[:, :, 1, :].unsqueeze(2).to_broadcast([P, PEER_H, TOPK, TOPK]),
                                            ALU.add))
                own.settle()
                sixteen(cand, cand_rest, top, top_at, PEER_H)
                at = top_at[:].rearrange("p h k -> p (h k)")
                own(nc.vector.tensor_scalar(pick[:, 0], at, 4, None, ALU.logical_shift_right))
                own(nc.vector.tensor_scalar(pick[:, 1], at, 15, None, ALU.bitwise_and))
                own.settle()
                own(nc.vector.tensor_copy(pick_f[:], pick[:]))
                if t:
                    dve.wait_ge(found_turned, t)
                own(nc.vector.tensor_tensor(found[:, 2].rearrange("p (h k) -> p h k", h=PEER_H), top[:],
                                            top[:, :, 0:1].to_broadcast([P, PEER_H, TOPK]), ALU.subtract))
                own.settle()
                keys_of = best_key[:].rearrange("p (h s) k -> p h s k", s=2)
                for i in range(2):
                    own(nc.vector.tensor_tensor(hot, pick_f[:, i].unsqueeze(2).to_broadcast([P, SLOTS, TOPK]),
                                                iota[:, 0:TOPK].unsqueeze(1).to_broadcast([P, SLOTS, TOPK]),
                                                ALU.is_equal))
                    own.settle()
                    h4 = hot.rearrange("p (h k) a -> p h k a", h=PEER_H)
                    own(nc.vector.tensor_tensor(h4, h4, keys_of[:, :, i, :].unsqueeze(2)
                                                .to_broadcast([P, PEER_H, TOPK, TOPK]), ALU.mult))
                    own.settle()
                    own(nc.vector.tensor_reduce(found[:, i], hot, AX.X, ALU.add))
                    own.settle()
                dve.sem_inc(found_ready, 1)

            dve.wait_ge(soft_summed, 1)
            own(nc.vector.reciprocal(slots[:, 3], ps[:, GATE:GATE + n]))
            own.settle()
            own(nc.vector.tensor_tensor(slots[:, 2], slots[:, 2], slots[:, 3], ALU.mult))
            own.settle()
            own(nc.vector.tensor_copy(w_hi[:], slots[:, 2]))
            own.settle()
            own(nc.vector.tensor_tensor(slots[:, 3], slots[:, 2], w_hi[:].bitcast(F32), ALU.subtract))
            own.settle()
            own(nc.vector.tensor_copy(slots[:, 2], w_hi[:].bitcast(F32)))
            own.settle()

            def octet(i, first):
                for b in range(2):
                    if not first:
                        dve.wait_ge(multiplied[b], i)
                    for q in range(QUAD):
                        t = i * (2 * QUAD) + (b * QUAD + q)
                        key, w0, w1 = (slots[:, c, bass.ds(t, 1)] for c in (1, 2, 3))
                        nc.vector.tensor_scalar(first_hot[:, b, q], iota[:], slots[:, 0, bass.ds(t, 1)], None,
                                                ALU.is_equal)
                        nc.vector.tensor_scalar(hot_hi[:, b, q], iota[:], key, w0, ALU.is_equal, ALU.mult)
                        last = nc.vector.tensor_scalar(hot_lo[:, b, q], iota[:], key, w1, ALU.is_equal, ALU.mult)
                    last.then_inc(hot_ready[b], 1)

            octet(0, True)
            with dve.Fori(1, n // (2 * QUAD)) as i:
                octet(i, False)


def stage_mix_experts(nc, g, layer, acts_d, table, x_d, n, spans):
    GROUP = 4
    BODIES = KEYS // GROUP // 2
    BANKS = 4
    v_rows = g.d["peer_v"][layer].rearrange("(a b) d -> a b d", b=KEYS)
    Y_UNITS = [(m, s) for m in range(DK) for s in range(len(spans))]
    PER = len(Y_UNITS) // BANKS
    with ExitStack() as stack:
        a = Arena(nc, stack)
        v_raw = a.sb("v_raw", [P, GROUP, D])
        v_hi = a.sb("v_hi", [P, 2, GROUP, D], F32R)
        v_lo = a.sb("v_lo", [P, 2, GROUP, D], F32R)
        gates = a.sb("gates", [P, 2, n // TB, GROUP, TB])
        acts = a.sb("acts_in", [P, GROUP, n])
        w_hi = a.sb("w_hi", [P, 2, GROUP, n], F32R)
        w_lo = a.sb("w_lo", [P, 2, GROUP, n], F32R)

        def two(name):
            return [a.sem(f"{name}{q}") for q in range(2)]

        v_loaded, gates_loaded, acts_loaded, v_hi_ready, v_lo_ready, weighted, w_hi_ready, w_lo_ready = map(
            two, ("v_loaded", "gates_loaded", "acts_loaded", "v_hi_ready", "v_lo_ready", "weighted", "w_hi_ready",
                  "w_lo_ready"))
        x_loaded = a.sem("x_loaded")
        y_done = [a.sem(f"y_done{b}") for b in range(BANKS)]
        y_added = [a.sem(f"y_added{b}") for b in range(BANKS)]
        block = a.block()
        ps = g.ps

        def bodies(engine, emit):
            emit(0, True, False)
            with engine.Fori(1, BODIES - 1) as i:
                emit(i, False, False)
            emit(BODIES - 1, False, True)

        def before(q, i):
            return (0, i + 1) if q else (1, i)

        @block.sync
        def _(sp):
            def body(i, first, last):
                for q in range(2):
                    at = i * (2 * GROUP) + q * GROUP
                    b, count = before(q, i)
                    start = first and q == 0
                    if not start:
                        sp.wait_ge(v_lo_ready[b], count)
                    sp.dma_start(v_raw[:], v_rows[:, bass.ds(at, GROUP), :]).then_inc(v_loaded[q], 16)
                    if not first:
                        sp.wait_ge(weighted[q], i * GROUP)
                    sp.dma_start(gates[:, q], table[:, :, bass.ds(at, GROUP), :]).then_inc(gates_loaded[q], 16)
                    if not start:
                        sp.wait_ge(w_lo_ready[b], count * GROUP)
                    sp.dma_start(acts[:], acts_d[bass.ds(at, GROUP)].rearrange("s p t -> p s t"))\
                        .then_inc(acts_loaded[q], 16)
                    if start:
                        sp.dma_start(g.x_t[:], x_d).then_inc(x_loaded, 16)

            bodies(sp, body)

        @block.scalar
        def _(act):
            def body(i, first, last):
                for q in range(2):
                    act.wait_ge(v_loaded[q], (i + 1) * 16)
                    if not first:
                        act.wait_ge(y_done[BANKS - 1], i * (2 * PER) + (q + 1) * PER - 2 * PER)
                    nc.scalar.copy(v_hi[:, q], v_raw[:]).then_inc(v_hi_ready[q], 1)

            bodies(act, body)

        @block.gpsimd
        def _(pool):
            def body(i, first, last):
                for q in range(2):
                    pool.wait_ge(v_hi_ready[q], i + 1)
                    nc.gpsimd.tensor_tensor(v_lo[:, q], v_raw[:], v_hi[:, q].bitcast(F32), ALU.subtract)\
                        .then_inc(v_lo_ready[q], 1)

            bodies(pool, body)

        @block.vector
        def _(dve):
            def weigh(q, i, first, op):
                what, r = op // GROUP, op % GROUP
                if what == 0:
                    if r == 0:
                        dve.wait_ge(acts_loaded[q], (i + 1) * 16)
                        dve.wait_ge(gates_loaded[q], (i + 1) * 16)
                    x = acts[:, r].rearrange("p (b t) -> p b t", t=TB)
                    nc.vector.tensor_tensor(x, x, gates[:, q, :, r, :], ALU.mult).then_inc(weighted[q], 1)
                elif what == 1:
                    if r == 0 and not first:
                        dve.wait_ge(y_done[BANKS - 1], i * (2 * PER) + (q + 1) * PER - 2 * PER)
                    dve.wait_ge(weighted[q], i * GROUP + r + 1)
                    nc.vector.tensor_copy(w_hi[:, q, r], acts[:, r]).then_inc(w_hi_ready[q], 1)
                else:
                    dve.wait_ge(w_hi_ready[q], i * GROUP + r + 1)
                    nc.vector.tensor_tensor(w_lo[:, q, r], acts[:, r], w_hi[:, q, r].bitcast(F32), ALU.subtract)\
                        .then_inc(w_lo_ready[q], 1)

            def add(q, i, c):
                m, s = Y_UNITS[c]
                b, e, t, stream = spans[s]
                bank = c % BANKS
                dve.wait_ge(y_done[bank], i * (2 * PER) + (q * PER + c // BANKS + 1))
                x = g.x_t[:, m, t:t + e - b]
                nc.vector.scalar_tensor_tensor(out=x, in0=ps[:, bank * BANK:bank * BANK + e - b],
                                               scalar=g.mod[:, layer, 40 + m, stream:stream + 1], in1=x,
                                               op0=ALU.mult, op1=ALU.add).then_inc(y_added[bank], 1)

            def body(i, first, last):
                for q in range(2):
                    for c in range(len(Y_UNITS)):
                        add(q, i, c)
                        if 1 <= c < 7 and not (last and q):
                            for op in (2 * c - 2, 2 * c - 1):
                                if q:
                                    weigh(0, i + 1, False, op)
                                else:
                                    weigh(1, i, first, op)

            for op in range(3 * GROUP):
                weigh(0, 0, True, op)
            dve.wait_ge(x_loaded, 16)
            bodies(dve, body)

        @block.tensor
        def _(pe):
            def body(i, first, last):
                for q in range(2):
                    pe.wait_ge(v_lo_ready[q], i + 1)
                    pe.wait_ge(w_lo_ready[q], (i + 1) * GROUP)
                    for c, (m, s) in enumerate(Y_UNITS):
                        b, e, _, _ = spans[s]
                        bank = c % BANKS
                        if not (first and q == 0 and c < BANKS):
                            pe.wait_ge(y_added[bank], i * (2 * PER) + (q * PER + c // BANKS))
                        for r in range(GROUP):
                            for v, w in ((v_hi, w_hi), (v_hi, w_lo), (v_lo, w_hi)):
                                last_mm = nc.tensor.matmul(ps[:, bank * BANK:bank * BANK + e - b],
                                                           v[:, q, r, m * P:(m + 1) * P], w[:, q, r, b:e],
                                                           start=(r == 0 and v is v_hi and w is w_hi),
                                                           stop=(r == GROUP - 1 and v is v_lo))
                        last_mm.then_inc(y_done[bank], 1)

            bodies(pe, body)


def stage_rms_channels(nc, g, x, kc, gain, factor=1.0):
    n = x.shape[2]
    with ExitStack() as stack:
        a = Arena(nc, stack)
        sq = a.sb("sq", [P, kc, n])
        rstd = a.sb("rstd", [P, n])
        squared, summed, root_in, rooted, own_v = a.sem("squared", "summed", "root_in", "rooted", "own_v")
        block = a.block()
        ps = g.ps

        @block.scalar
        def _(act):
            for k in range(kc):
                nc.scalar.activation(sq[:, k], x[:, k], ACT.Square).then_inc(squared, 1)
            act.wait_ge(root_in, 1)
            nc.scalar.activation(rstd[:], rstd[:], ACT.Sqrt).then_inc(rooted, 1)

        @block.tensor
        def _(pe):
            for k in range(kc):
                pe.wait_ge(squared, k + 1)
                for lo, hi in halves(n):
                    last = nc.tensor.matmul(ps[:, lo:hi], g.ones_d[:], sq[:, k, lo:hi],
                                            start=(k == 0), stop=(k == kc - 1))
            last.then_inc(summed, 1)

        @block.vector
        def _(dve):
            own = Steps(dve, own_v)
            dve.wait_ge(summed, 1)
            nc.vector.tensor_scalar(rstd[:], ps[:, 0:n], D / (kc * P), EPS, ALU.mult, ALU.add).then_inc(root_in, 1)
            dve.wait_ge(rooted, 1)
            own(nc.vector.reciprocal(rstd[:], rstd[:]))
            own.settle()
            if factor != 1.0:
                own(nc.vector.tensor_scalar(rstd[:], rstd[:], factor, None, ALU.mult))
                own.settle()
            for k in range(kc):
                own(nc.vector.scalar_tensor_tensor(out=x[:, k], in0=x[:, k], scalar=gain[:, k:k + 1], in1=rstd[:],
                                                   op0=ALU.mult, op1=ALU.mult))


def stage_mla_heads(nc, g, q_a, kv_a, k_rope, q_t, k_t, v_tok):
    QH, KH = MLA_NOPE + MLA_ROPE, MLA_NOPE + MLA_V
    NQ, NK = MLA_QR // P, MLA_KVR // P
    with ExitStack() as stack:
        a = Arena(nc, stack)
        w_q = a.sb("w_qup", [P, NQ, MLA_H * QH])
        w_kv = a.sb("w_kvup", [P, NK, MLA_H * KH])
        q_rope = a.sb("q_rope", [MLA_ROPE, MLA_H, LAT])
        rope = a.sb("rope", [MLA_ROPE, 2, LAT])
        swap = a.sb("swap", [MLA_ROPE, MLA_ROPE])
        direct_cos = a.sb("direct_cos", [MLA_ROPE, 2, LAT])
        swapped_sin = a.sb("swapped_sin", [MLA_ROPE, 2, LAT])
        k_turned = a.sb("k_turned", [MLA_ROPE, T])
        loaded, product, kept, swapped, swap_free, k_ready, own_v = a.sem(
            "loaded", "product", "kept", "swapped", "swap_free", "k_ready", "own_v")
        block = a.block()
        ps = g.ps
        SWAP = 6 * BANK
        units = []
        for h in range(MLA_H):
            units.append(([(w_q[:, k, h * QH:h * QH + 64], q_a[:, k, :]) for k in range(NQ)], 64, LAT,
                          q_t[0:64, h, :]))
            units.append(([(w_q[:, k, h * QH + 64:(h + 1) * QH], q_a[:, k, :]) for k in range(NQ)], MLA_ROPE, LAT,
                          q_rope[:, h, :]))
            units.append(([(w_kv[:, k, h * KH:h * KH + 64], kv_a[:, k, :]) for k in range(NK)], 64, T,
                          k_t[0:64, h, :]))
        for t in range(T // P):
            values = [w_kv[:, k].rearrange("p (h c) -> p h c", c=KH)[:, :, MLA_NOPE:] for k in range(NK)]
            units.append(([(kv_a[:, k, t * P:(t + 1) * P], values[k]) for k in range(NK)], P, 512, v_tok[:, t, :]))

        @block.sync
        def _(sp):
            sp.dma_start(w_q[:], g.d["mla_w_qup"][0].rearrange("(k p) n -> p k n", p=P)).then_inc(loaded, 16)
            sp.dma_start(w_kv[:], g.d["mla_w_kvup"][0].rearrange("(k p) n -> p k n", p=P)).then_inc(loaded, 16)
            sp.dma_start(rope[:], g.d["k_rope_mla"]).then_inc(loaded, 16)
            sp.dma_start(swap[:], g.d["k_rope_swap"]).then_inc(loaded, 16)

        @block.tensor
        def _(pe):
            pe.wait_ge(loaded, 64)
            for u, (pairs, m, n, _) in enumerate(units):
                at = (u % 3) * 1024
                if u >= 3:
                    pe.wait_ge(kept, u - 2)
                for i, (left, right) in enumerate(pairs):
                    if len(right.shape) == 3:
                        last = nc.tensor.matmul(ps[0:m, at:at + n], left, right, start=(i == 0),
                                                stop=(i == len(pairs) - 1))
                    else:
                        for lo, hi in halves(n):
                            last = nc.tensor.matmul(ps[0:m, at + lo:at + hi], left, right[:, lo:hi], start=(i == 0),
                                                    stop=(i == len(pairs) - 1))
                last.then_inc(product, 1)
            pe.wait_ge(kept, len(units))
            for h in range(MLA_H + 1):
                if h >= 2:
                    pe.wait_ge(swap_free, h - 1)
                x = q_rope[:, h, :] if h < MLA_H else k_rope[:, CTX:T]
                nc.tensor.matmul(ps[0:MLA_ROPE, SWAP + (h % 2) * BANK:SWAP + (h % 2 + 1) * BANK], swap[:], x,
                                 start=True, stop=True).then_inc(swapped, 1)

        @block.scalar
        def _(act):
            for u, (pairs, m, n, out) in enumerate(units):
                act.wait_ge(product, u + 1)
                nc.scalar.copy(out, ps[0:m, (u % 3) * 1024:(u % 3) * 1024 + n]).then_inc(kept, 1)
            act.wait_ge(k_ready, 1)
            for h in range(MLA_H):
                nc.scalar.copy(k_t[64:96, h, :], k_turned[:])

        @block.vector
        def _(dve):
            own = Steps(dve, own_v)
            dve.wait_ge(kept, len(units))
            dve.wait_ge(loaded, 64)
            for h in range(MLA_H + 1):
                x = q_rope[:, h, :] if h < MLA_H else k_rope[:, CTX:T]
                out = q_t[64:96, h, :] if h < MLA_H else k_turned[:, CTX:T]
                own(nc.vector.tensor_tensor(direct_cos[:, h % 2], x, rope[:, 0], ALU.mult))
                dve.wait_ge(swapped, h + 1)
                nc.vector.tensor_tensor(swapped_sin[:, h % 2], rope[:, 1],
                                        ps[0:MLA_ROPE, SWAP + (h % 2) * BANK:SWAP + (h % 2 + 1) * BANK],
                                        ALU.mult).then_inc(swap_free, 1)
                dve.wait_ge(swap_free, h + 1)
                own.settle()
                own(nc.vector.tensor_tensor(out, direct_cos[:, h % 2], swapped_sin[:, h % 2], ALU.add))
            own(nc.vector.tensor_copy(k_turned[:, 0:CTX], k_rope[:, 0:CTX]))
            own.settle()
            dve.sem_inc(k_ready, 1)


S5_TILES = S5_G // 2
TWO_PI = 6.283185
ROUND = 1.5 * 2.0 ** 23


def stage_s5_parameters(nc, g, rate, turns, b_t, c_t):
    N = 2 * S5_TILES
    with ExitStack() as stack:
        a = Arena(nc, stack)
        rows = a.sb("s5_rows", [3 * N, P])
        dt_rows = a.sb("dt_rows", [3 * N, 2])
        par = a.sb("par", [P, 3, N])
        f = a.sb("s5_f", [P, 12, N])
        b_nat = a.sb("b_nat", [P, 2, N, S5_C])
        b_eff = a.sb("b_eff", [P, 2, N, S5_C])
        tmp = a.sb("tmp", [P, N, S5_C])
        c_nat = a.sb("c_nat", [P, 2, 8, S5_P])
        b_mask = a.sb("b_mask", [P, 4, 8])
        c_mask = a.sb("c_mask", [P, 8])
        padded = a.sb("padded", [P, 2, 4, P])
        loaded, spread, turned, par_ready, trig_in, trig_out, own_v, pad_ready, pad_turned, pad_kept = a.sem(
            "loaded", "spread", "turned", "par_ready", "trig_in", "trig_out", "own_v", "pad_ready", "pad_turned",
            "pad_kept")
        block = a.block()
        ps = g.ps
        jobs = [(m, part, d, j) for m in "bc" for part in range(2) for d in range(2) for j in range(4)]

        @block.sync
        def _(sp):
            d = g.d
            sp.dma_start(rows[0:N, :], d["s5_a_re"][0].rearrange("d (i g) p -> (d i) (g p)", g=2)).then_inc(loaded, 16)
            sp.dma_start(rows[N:2 * N, :], d["s5_a_im"][0].rearrange("d (i g) p -> (d i) (g p)", g=2))\
                .then_inc(loaded, 16)
            sp.dma_start(dt_rows[2 * N:3 * N, :], d["s5_log_dt"][0].rearrange("d (i g) -> (d i) g", g=2))\
                .then_inc(loaded, 16)
            sp.dma_start(b_mask[:], d["k_s5_bmask"]).then_inc(loaded, 16)
            sp.dma_start(c_mask[:], d["k_s5_cmask"]).then_inc(loaded, 16)
            for part, name in enumerate(("s5_b_re", "s5_b_im")):
                for dr in range(2):
                    src = d[name][0, dr].rearrange("(i g) p c -> (g p) i c", g=2)
                    sp.dma_start(b_nat[:, part, dr * S5_TILES:(dr + 1) * S5_TILES, :], src).then_inc(loaded, 16)
            for part, name in enumerate(("s5_c_re", "s5_c_im")):
                for dr in range(2):
                    src = d[name][0, dr].rearrange("(j g) c p -> (g c) j p", g=8)
                    sp.dma_start(c_nat[:, part, dr * 4:(dr + 1) * 4, :], src).then_inc(loaded, 16)

        n_loads = 16 * 13

        @block.tensor
        def _(pe):
            pe.wait_ge(spread, 1)
            nc.tensor.transpose(ps[:, 0:3 * N], rows[:], g.ident[:3 * N, :3 * N]).then_inc(turned, 1)
            for n in range(len(jobs)):
                pe.wait_ge(pad_ready, n + 1)
                if n >= 2:
                    pe.wait_ge(pad_kept, n - 1)
                at = (2 + n % 2) * BANK
                for i in range(4):
                    last = nc.tensor.transpose(ps[:, at + i * P:at + (i + 1) * P], padded[:, n % 2, i], g.ident[:])
                last.then_inc(pad_turned, 1)

        @block.scalar
        def _(act):
            act.wait_ge(par_ready, 1)
            nc.scalar.activation(f[:, 0], par[:, 2], ACT.Exp).then_inc(trig_out, 1)
            act.wait_ge(trig_in, 1)
            nc.scalar.activation(rate[:], f[:, 1], ACT.Exp).then_inc(trig_out, 1)
            nc.scalar.activation(f[:, 4], turns[:], ACT.Sin, scale=TWO_PI).then_inc(trig_out, 1)
            nc.scalar.activation(f[:, 5], turns[:], ACT.Sin, scale=TWO_PI / 2).then_inc(trig_out, 1)
            for n, (m, part, d, j) in enumerate(jobs):
                act.wait_ge(pad_turned, n + 1)
                src = ps[:, (2 + n % 2) * BANK:(3 + n % 2) * BANK].rearrange("p (i n) -> p i n", i=4)
                tiles = slice(d * S5_TILES + 4 * j, d * S5_TILES + 4 * j + 4)
                if m == "b":
                    nc.scalar.copy(b_t[:, part, tiles, :], src).then_inc(pad_kept, 1)
                elif part == 0:
                    nc.scalar.copy(c_t[:, 0, tiles, :], src)
                    nc.scalar.mul(c_t[:, 1, tiles, :], src, -1.0).then_inc(pad_kept, 1)
                else:
                    nc.scalar.mul(c_t[:, 2, tiles, :], src, -1.0).then_inc(pad_kept, 1)

        @block.vector
        def _(dve):
            own = Steps(dve, own_v)
            dve.wait_ge(loaded, n_loads)
            nc.vector.tensor_copy(rows[2 * N:3 * N, :].rearrange("r (g p) -> r g p", g=2),
                                  dt_rows[2 * N:3 * N, :].unsqueeze(2).to_broadcast([N, 2, S5_P])).then_inc(spread, 1)
            dve.wait_ge(turned, 1)
            nc.vector.tensor_copy(par[:], ps[:, 0:3 * N].rearrange("p (i n) -> p i n", i=3)).then_inc(par_ready, 1)
            dve.wait_ge(par_ready, 1)
            dve.wait_ge(trig_out, 1)
            lam_re, lam_im = par[:, 0], par[:, 1]
            tt, ts = nc.vector.tensor_tensor, nc.vector.tensor_scalar
            own(tt(f[:, 1], lam_re, f[:, 0], ALU.mult))
            own(tt(f[:, 2], lam_im, f[:, 0], ALU.mult))
            own.settle()
            own(ts(f[:, 2], f[:, 2], float(1 / (2 * np.pi)), None, ALU.mult))
            own.settle()
            own(ts(f[:, 3], f[:, 2], ROUND, ROUND, ALU.add, ALU.subtract))
            own.settle()
            own(tt(turns[:], f[:, 2], f[:, 3], ALU.subtract))
            own.settle()
            dve.sem_inc(trig_in, 1)
            dve.wait_ge(trig_out, 4)
            own(tt(f[:, 6], f[:, 5], f[:, 5], ALU.mult))
            own.settle()
            own(ts(f[:, 6], f[:, 6], -2.0, 1.0, ALU.mult, ALU.add))
            own(tt(f[:, 7], rate[:], f[:, 4], ALU.mult))
            own.settle()
            own(tt(f[:, 6], rate[:], f[:, 6], ALU.mult))
            own(tt(f[:, 8], lam_re, lam_re, ALU.mult))
            own(tt(f[:, 9], lam_im, lam_im, ALU.mult))
            own.settle()
            own(ts(f[:, 6], f[:, 6], 1.0, None, ALU.subtract))
            own(tt(f[:, 8], f[:, 8], f[:, 9], ALU.add))
            own.settle()
            own(nc.vector.reciprocal(f[:, 8], f[:, 8]))
            own(tt(f[:, 9], f[:, 6], lam_re, ALU.mult))
            own(tt(f[:, 10], f[:, 7], lam_im, ALU.mult))
            own(tt(f[:, 11], f[:, 7], lam_re, ALU.mult))
            own(tt(f[:, 5], f[:, 6], lam_im, ALU.mult))
            own.settle()
            own(tt(f[:, 9], f[:, 9], f[:, 10], ALU.add))
            own(tt(f[:, 11], f[:, 11], f[:, 5], ALU.subtract))
            own.settle()
            own(tt(f[:, 9], f[:, 9], f[:, 8], ALU.mult))
            own(tt(f[:, 11], f[:, 11], f[:, 8], ALU.mult))
            own.settle()
            re = f[:, 9].unsqueeze(2).to_broadcast([P, N, S5_C])
            im = f[:, 11].unsqueeze(2).to_broadcast([P, N, S5_C])
            for part, (x, y, op) in enumerate(((re, im, ALU.subtract), (im, re, ALU.add))):
                own(tt(b_eff[:, part], b_nat[:, 0], x, ALU.mult))
                own(tt(tmp[:], b_nat[:, 1], y, ALU.mult))
                own.settle()
                own(tt(b_eff[:, part], b_eff[:, part], tmp[:], op))
                own.settle()
            for n, (m, part, d, j) in enumerate(jobs):
                if n >= 2:
                    dve.wait_ge(pad_turned, n - 1)
                if m == "b":
                    tiles = slice(d * S5_TILES + 4 * j, d * S5_TILES + 4 * j + 4)
                    last = tt(padded[:, n % 2].rearrange("p i (g c) -> p i g c", g=8),
                              b_eff[:, part, tiles].unsqueeze(2).to_broadcast([P, 4, 8, S5_C]),
                              b_mask[:].unsqueeze(3).to_broadcast([P, 4, 8, S5_C]), ALU.mult)
                else:
                    last = tt(padded[:, n % 2].rearrange("p i (g s) -> p (i g) s", g=2),
                              c_nat[:, part, d * 4 + j].unsqueeze(1).to_broadcast([P, 8, S5_P]),
                              c_mask[:].unsqueeze(2).to_broadcast([P, 8, S5_P]), ALU.mult)
                last.then_inc(pad_ready, 1)


def stage_s5_scan(nc, g, u_t, rate, turns, b_t, c_t, z_t):
    units = [(j, i, d) for j in range(4) for i in range(4) for d in range(2)]
    with ExitStack() as stack:
        a = Arena(nc, stack)
        tau = a.sb("tau", [P, 2, T])
        phase = a.sb("phase", [P, 2, T])
        whole = a.sb("whole", [P, T])
        sin = a.sb("sin", [P, 2, T])
        cos = a.sb("cos", [P, 2, T])
        x2 = a.sb("x2", [P, 2, T])
        v = a.sb("v", [P, 2, T])
        s = a.sb("s", [P, 2, 2, T])
        prods = a.sb("prods", [P, 2, 4, LAT])
        to_whole = a.sb("to_whole", [P, 1])
        (loaded, rounding_ready, phase_made, phase_rounded, phase_ready, half_ready, sq_ready, trig_ready, bu_ready, bu_used, scanned, prods_ready, y_ready,
         y_read, own_v, phase_used, d_added) = a.sem(
            "loaded", "rounding_ready", "phase_made", "phase_rounded", "phase_ready", "half_ready", "sq_ready", "trig_ready", "bu_ready", "bu_used", "scanned",
            "prods_ready", "y_ready", "y_read", "own_v", "phase_used", "d_added")
        block = a.block()
        ps = g.ps
        BU, YB = 0, 6 * BANK

        @block.sync
        def _(sp):
            sp.dma_start(tau[:], g.d["k_s5_tau"]).then_inc(loaded, 16)

        @block.tensor
        def _(pe):
            def inputs(n):
                j, i, d = units[n]
                unit = d * S5_TILES + 4 * j + i
                if n:
                    pe.wait_ge(bu_used, n)
                for part in range(2):
                    for lo, hi in halves(T):
                        last = nc.tensor.matmul(ps[:, BU + part * 1024 + lo:BU + part * 1024 + hi],
                                                b_t[:, part, unit], u_t[:, j, lo:hi], start=True, stop=True)
                last.then_inc(bu_ready, 1)

            def outputs(n):
                j, i, d = units[n]
                unit = d * S5_TILES + 4 * j + i
                pe.wait_ge(prods_ready, n + 1)
                if i == 0 and d == 0 and j >= 2:
                    pe.wait_ge(y_read, j - 1)
                out = ps[:, YB + (j % 2) * BANK:YB + (j % 2 + 1) * BANK]
                for c, which in enumerate((0, 1, 2, 2)):
                    last = nc.tensor.matmul(out, c_t[:, which, unit], prods[:, n % 2, c],
                                            start=(i == 0 and d == 0 and c == 0), stop=(i == 3 and d == 1 and c == 3))
                last.then_inc(y_ready, 1)

            inputs(0)
            for n in range(len(units)):
                if n + 1 < len(units):
                    inputs(n + 1)
                if n:
                    outputs(n - 1)
            outputs(len(units) - 1)

        @block.scalar
        def _(act):
            def phases(n):
                j, i, d = units[n]
                unit = d * S5_TILES + 4 * j + i
                if n:
                    act.wait_ge(phase_ready, n)
                if n >= 2:
                    act.wait_ge(half_ready, n - 1)
                nc.scalar.activation(phase[:, n % 2], tau[:, d], ACT.Copy, scale=turns[:, unit:unit + 1])\
                    .then_inc(phase_made, 1)
                act.wait_ge(phase_made, n + 1)
                nc.scalar.activation(whole[:], phase[:, n % 2], ACT.Identity, bias=to_whole[:])\
                    .then_inc(phase_rounded, 1)

            act.wait_ge(loaded, 16)
            act.wait_ge(rounding_ready, 1)
            phases(0)
            for n in range(len(units)):
                b = n % 2
                if n + 1 < len(units):
                    phases(n + 1)
                act.wait_ge(phase_ready, n + 1)
                if n >= 2:
                    act.wait_ge(prods_ready, n - 1)
                nc.scalar.activation(sin[:, b], phase[:, b], ACT.Sin, scale=-TWO_PI)
                nc.scalar.activation(cos[:, b], phase[:, b], ACT.Sin, scale=TWO_PI / 2).then_inc(half_ready, 1)
                act.wait_ge(half_ready, n + 1)
                nc.scalar.activation(cos[:, b], cos[:, b], ACT.Square).then_inc(sq_ready, 1)
                act.wait_ge(sq_ready, n + 1)
                nc.scalar.activation(cos[:, b], cos[:, b], ACT.Identity, bias=1.0, scale=-2.0)\
                    .then_inc(trig_ready, 1)
            for j in range(4):
                act.wait_ge(d_added, j + 1)
                nc.scalar.activation(z_t[:, j], z_t[:, j], ACT.Gelu)

        @block.vector
        def _(dve):
            own = Steps(dve, own_v)
            tt = nc.vector.tensor_tensor

            def phases(n):
                dve.wait_ge(phase_rounded, n + 1)
                nc.vector.scalar_tensor_tensor(out=phase[:, n % 2], in0=whole[:], scalar=ROUND, in1=phase[:, n % 2],
                                               op0=ALU.subtract, op1=ALU.subtract).then_inc(phase_ready, 1)

            def readout(j):
                dve.wait_ge(y_ready, 8 * (j + 1))
                at = VEC["s5_d"][0] + j
                nc.vector.scalar_tensor_tensor(out=z_t[:, j], in0=u_t[:, j, CTX:T], scalar=g.vec[:, at:at + 1],
                                               in1=ps[:, YB + (j % 2) * BANK:YB + (j % 2 + 1) * BANK],
                                               op0=ALU.mult, op1=ALU.add).then_inc(y_read, 1)
                dve.wait_ge(y_read, j + 1)
                dve.sem_inc(d_added, 1)

            nc.vector.memset(to_whole[:], ROUND).then_inc(rounding_ready, 1)
            phases(0)
            for n, (j, i, d) in enumerate(units):
                unit = d * S5_TILES + 4 * j + i
                b = n % 2
                if n + 1 < len(units):
                    phases(n + 1)
                re, im = ps[:, BU:BU + T], ps[:, BU + 1024:BU + 1024 + T]
                dve.wait_ge(trig_ready, n + 1)
                dve.wait_ge(bu_ready, n + 1)
                own(tt(v[:, 0], cos[:, b], re, ALU.mult))
                own(tt(x2[:, 0], sin[:, b], im, ALU.mult))
                own(tt(v[:, 1], cos[:, b], im, ALU.mult))
                own(tt(x2[:, 1], sin[:, b], re, ALU.mult))
                own.settle()
                dve.sem_inc(bu_used, 1)
                own(tt(v[:, 0], v[:, 0], x2[:, 0], ALU.add))
                own(tt(v[:, 1], v[:, 1], x2[:, 1], ALU.subtract))
                own.settle()
                if n >= 2:
                    dve.wait_ge(prods_ready, n - 1)
                r = rate[:, unit:unit + 1]
                for part in range(2):
                    x, out = v[:, part], s[:, b, part]
                    if d == 0:
                        own(nc.vector.tensor_tensor_scan(out, r.to_broadcast([P, T]), x, 0.0, ALU.mult, ALU.add))
                    else:
                        own(nc.vector.tensor_tensor_scan(out[:, 0:CTX][:, ::-1], r.to_broadcast([P, CTX]),
                                                         x[:, 0:CTX][:, ::-1], 0.0, ALU.mult, ALU.add))
                if d == 1:
                    own.settle()
                    for part in range(2):
                        x, out = v[:, part], s[:, b, part]
                        own(nc.vector.tensor_tensor_scan(out[:, CTX:T][:, ::-1], r.to_broadcast([P, LAT]),
                                                         x[:, CTX:T][:, ::-1], out[:, 0:1], ALU.mult, ALU.add))
                own.settle()
                dve.sem_inc(scanned, 1)
                if i == 0 and d == 1 and j:
                    readout(j - 1)
            readout(3)

        @block.gpsimd
        def _(pool):
            for n in range(len(units)):
                b = n % 2
                pool.wait_ge(scanned, n + 1)
                pool.wait_ge(trig_ready, n + 1)
                if n >= 2:
                    pool.wait_ge(y_ready, n - 1)
                for c, (part, table) in enumerate(((0, cos), (1, sin), (0, sin), (1, cos))):
                    last = nc.gpsimd.tensor_tensor(prods[:, b, c], s[:, b, part, CTX:T], table[:, b, CTX:T], ALU.mult)
                last.then_inc(prods_ready, 1)


def stage_s5_glu(nc, g, z_t, w_out, w_rows):
    with ExitStack() as stack:
        a = Arena(nc, stack)
        w = a.sb("w_glu", [P, 4, 512])
        gate = a.sb("gate", [P, 4, LAT])
        loaded, w_loaded, summed, gated = a.sem("loaded", "w_loaded", "summed", "gated")
        block = a.block()
        ps = g.ps

        @block.sync
        def _(sp):
            sp.dma_start(w[:], g.d["s5_w_glu"][0].rearrange("(k p) n -> p k n", p=P)).then_inc(loaded, 16)
            load_rows(sp, w_out, w_rows, w_loaded)
            sp.wait_ge(w_loaded, 16 * len(w_rows))

        @block.tensor
        def _(pe):
            pe.wait_ge(loaded, 16)
            for m in range(4):
                for k in range(4):
                    last = nc.tensor.matmul(ps[:, m * BANK:(m + 1) * BANK], w[:, k, m * P:(m + 1) * P], z_t[:, k],
                                            start=(k == 0), stop=(k == 3))
                last.then_inc(summed, 1)

        @block.scalar
        def _(act):
            for m in range(4):
                act.wait_ge(summed, m + 1)
                at = VEC["s5_bglu"][0] + m
                nc.scalar.activation(gate[:, m], ps[:, m * BANK:(m + 1) * BANK], ACT.Sigmoid,
                                     bias=g.vec[:, at:at + 1]).then_inc(gated, 1)

        @block.vector
        def _(dve):
            dve.wait_ge(summed, 4)
            for m in range(4):
                dve.wait_ge(gated, m + 1)
                nc.vector.tensor_tensor(z_t[:, m], z_t[:, m], gate[:, m], ALU.mult)


def stage_output(nc, g):
    x = g.x_t[:, :, CTX:T]
    at = VEC["final"][0]
    stage_rms_channels(nc, g, x, DK, g.vec[:, at:at + 8])
    with ExitStack() as stack:
        a = Arena(nc, stack)
        rows = a.sb("out_rows", [P, LAT // P, D])
        turned, kept, stored = a.sem("turned", "kept", "stored")
        block = a.block()
        ps = g.ps

        @block.tensor
        def _(pe):
            for t in range(LAT // P):
                for k in range(DK):
                    last = nc.tensor.transpose(ps[:, t * 1024 + k * P:t * 1024 + (k + 1) * P],
                                               x[:, k, t * P:(t + 1) * P], g.ident[:])
                last.then_inc(turned, 1)

        @block.vector
        def _(dve):
            for t in range(LAT // P):
                dve.wait_ge(turned, t + 1)
                nc.vector.tensor_copy(rows[:, t], ps[:, t * 1024:(t + 1) * 1024]).then_inc(kept, 1)

        @block.sync
        def _(sp):
            for t in range(LAT // P):
                sp.wait_ge(kept, t + 1)
                sp.dma_start(g.out[0, t * P:(t + 1) * P, :], rows[:, t]).then_inc(stored, 16)
            sp.wait_ge(stored, 16 * (LAT // P))


def peer(nc, g, layer, t0, until=99):
    n = T - t0
    spans = [(0, LAT, CTX, 0)] + ([(LAT, T, 0, 1)] if t0 == 0 else [])
    with ExitStack() as stack:
        a = Arena(nc, stack)
        scores_d = nc.dram_tensor(f"scores{layer}", (n // P, P, 2 * PEER_H, KEYS), F32).ap()
        acts_d = nc.dram_tensor(f"activations{layer}", (KEYS, P, n), F32).ap()
        table = nc.dram_tensor(f"gate_table{layer}", (P, n // TB, KEYS, TB), F32).ap()
        x_d = nc.dram_tensor(f"x_kept{layer}", (P, DK, T), F32).ap()
        with ExitStack() as inner:
            b = Arena(nc, inner)
            hi = b.sb("h_hi", [P, DK, n], F32R)
            lo = b.sb("h_lo", [P, DK, n], F32R)
            with ExitStack() as scope:
                c = Arena(nc, scope)
                q_t = c.sb("peer_q", [P, 2 * PEER_H, n])
                wq = g.d["peer_wq"][layer].rearrange("(k p) n -> p k n", p=P)
                blocks = column_blocks(0, channel_units(q_t, 2 * PEER_H))
                with ExitStack() as early:
                    room = Arena(nc, early).sb("peer_wq_in", [P, W_RING * DK * W_COLS])
                    stage_norm(nc, g, layer, 1, t0, hi, lo, room, wq, blocks, latents_first=True)
                    stage_project_split(nc, g, "peer_wq", hi, lo, wq, blocks, room)
                stage_scores(nc, g, layer, q_t, scores_d, x_d, n)
            if until >= 7:
                stage_route_and_activate(nc, g, layer, hi, lo, scores_d, acts_d, table, n)
        if until >= 7:
            stage_mix_experts(nc, g, layer, acts_d, table, x_d, n, spans)


def layer_even(nc, g, until):
    w_in = g.d["ev_w_in"][0].rearrange("(k p) n -> p k n", p=P)
    with ExitStack() as stack:
        a = Arena(nc, stack)
        y_t = a.sb("y_t", [P, DK, T])
        with ExitStack() as inner:
            b = Arena(nc, inner)
            hg = b.sb("hg", [P, 4, HG_HEADS, T])
            hg_v = b.sb("hg_v", [P, T // P, 512])
            with ExitStack() as scope:
                c = Arena(nc, scope)
                proj = c.sb("gqa_proj", [P, T // P, (GQA_Q + GQA_KV) * HEAD])
                values = y_t[:, DK - 1].rearrange("p (t c) -> p t c", c=P)
                with ExitStack() as early:
                    e = Arena(nc, early)
                    hi, lo = (e.sb(name, [P, DK, T], F32R) for name in ("h_hi", "h_lo"))
                    at = GQA_IN
                    pairs = proj[:, :, 0:512].rearrange("p t (j kv c) -> p t kv j c", j=4, kv=2)
                    blocks = [(256 * kv, 256, [("tokens", t, pairs[:, t, kv]) for t in range(T // P)])
                              for kv in range(2)]
                    blocks += [(512, P, token_units(proj[:, :, 512:640], T // P)),
                               (640, P, token_units(values, T // P))]
                    blocks += column_blocks(at, channel_units(hg[:, 0:3].rearrange("p a h t -> p (a h) t"), 12))
                    blocks += [(at + 1536 + c, 256, token_units(hg_v[:, :, c:c + 256], T // P)) for c in (0, 256)]
                    blocks += column_blocks(at + 2048, channel_units(hg[:, 3], 4))
                    room = y_t[:].rearrange("p k t -> p (k t)")
                    stage_norm(nc, g, 0, 0, 0, hi, lo, room, w_in, blocks)
                    stage_project_split(nc, g, "ev_in", hi, lo, w_in, blocks, room)
                if until >= 2:
                    q_t = c.sb("q_t", [P, 4, T])
                    k_t = c.sb("k_t", [P, T])
                    stage_gqa_heads(nc, g, proj, q_t, k_t)
                if until >= 3:
                    units = []
                    for t in range(T // P):
                        keys = CTX if t < CTX // P else T
                        for j in range(4):
                            for kv in range(2):
                                rows = slice(64 * kv, 64 * kv + 64)

                                def v(i, kv=kv):
                                    return values[:, i, kv * HEAD:(kv + 1) * HEAD]

                                units.append((q_t[rows, j, t * P:(t + 1) * P], k_t[rows, 0:keys], v, 64 * kv,
                                              y_t[:, j, t * P:(t + 1) * P]))
                    stage_attention(nc, g, units)
            if until >= 4:
                keep_k = b.sb("keep_k", [P, 2 * HG_HEADS, T])
                cum = b.sb("cum", [P, 2 * HG_HEADS, T])
                with ExitStack() as scope:
                    forget = Arena(nc, scope).sb("forget", [P, HG_HEADS, T])
                    stage_hgrn2_gates(nc, g, hg, forget, keep_k, cum)
                stage_hgrn2_scan(nc, g, hg, hg_v, keep_k, cum, y_t)
                w_out = g.d["ev_w_out"][0]
                rows = [(slice(64 * kv, 64 * kv + 64), j, w_out[256 * kv + 64 * j:256 * kv + 64 * j + 64, :])
                        for kv in range(2) for j in range(4)]
                rows += [(slice(0, P), k, w_out[k * P:(k + 1) * P, :]) for k in range(4, DK)]
                w = b.sb("w_out", [P, DK, D])
                stage_hgrn2_readout(nc, g, hg, y_t, w, rows)
                if until >= 5:
                    stage_mix_out(nc, g, 0, y_t, 0, w)
    if until >= 6:
        peer(nc, g, 0, 0, until)


def layer_odd(nc, g, until):
    w_in = g.d["od_w_in"][0].rearrange("(k p) n -> p k n", p=P)
    with ExitStack() as stack:
        a = Arena(nc, stack)
        y_t = a.sb("y_t", [P, DK, LAT])
        with ExitStack() as inner:
            b = Arena(nc, inner)
            u_t = b.sb("u_t", [P, 4, T])
            with ExitStack() as scope:
                c = Arena(nc, scope)
                q_a = c.sb("q_a", [P, MLA_QR // P, LAT])
                kv_a = c.sb("kv_a", [P, MLA_KVR // P, T])
                k_rope = c.sb("k_rope", [MLA_ROPE, T])
                with ExitStack() as early:
                    e = Arena(nc, early)
                    hi, lo = (e.sb(name, [P, DK, T], F32R) for name in ("h_hi", "h_lo"))
                    blocks = [(0, 256, [("latents", m * P, q_a[:, m, :]) for m in range(2)]),
                              (256, P, [("latents", 0, q_a[:, 2, :])]),
                              (MLA_QR, MLA_KVR, channel_units(kv_a, MLA_KVR // P)),
                              (MLA_QR + MLA_KVR, MLA_ROPE, [("channels", 0, k_rope[:])])]
                    blocks += column_blocks(MLA_IN, channel_units(u_t, 4))
                    room = e.sb("od_in_in", [P, W_RING * DK * W_COLS])
                    stage_norm(nc, g, 1, 0, 0, hi, lo, room, w_in, blocks)
                    stage_project_split(nc, g, "od_in", hi, lo, w_in, blocks, room)
                at, _ = VEC["mla_qa"]
                stage_rms_channels(nc, g, q_a, MLA_QR // P, g.vec[:, at:at + 3], (MLA_NOPE + MLA_ROPE) ** -0.5)
                at, _ = VEC["mla_kva"]
                stage_rms_channels(nc, g, kv_a, MLA_KVR // P, g.vec[:, at:at + 2])
                q_t = c.sb("mla_q", [P, MLA_H, LAT])
                k_t = c.sb("mla_k", [P, MLA_H, T])
                v_tok = c.sb("mla_v", [P, T // P, MLA_H * MLA_V])
                stage_mla_heads(nc, g, q_a, kv_a, k_rope, q_t, k_t, v_tok)
                units = []
                for t in range(LAT // P):
                    for h in range(MLA_H):
                        def v(i, h=h):
                            return v_tok[:, i, h * MLA_V:(h + 1) * MLA_V]

                        units.append((q_t[0:96, h, t * P:(t + 1) * P], k_t[0:96, h, :], v, 64 * (h % 2),
                                      y_t[:, h // 2, t * P:(t + 1) * P]))
                stage_attention(nc, g, units)
            if until >= 9:
                N = 2 * S5_TILES
                rate = b.sb("rate", [P, N])
                turns = b.sb("turns", [P, N])
                b_t = b.sb("b_t", [P, 2, N, P])
                c_t = b.sb("c_t", [P, 3, N, P])
                z_t = y_t[:, 4:DK]
                stage_s5_parameters(nc, g, rate, turns, b_t, c_t)
                stage_s5_scan(nc, g, u_t, rate, turns, b_t, c_t, z_t)
                w = b.sb("w_out_odd", [P, DK, D])
                w_out = g.d["od_w_out"][0]
                rows = [(slice(0, P), k, w_out[k * P:(k + 1) * P, :]) for k in range(DK)]
                stage_s5_glu(nc, g, z_t, w, rows)
                if until >= 10:
                    stage_mix_out(nc, g, 1, y_t, CTX, w)
    if until >= 11:
        peer(nc, g, 1, CTX)
    if until >= 12:
        stage_output(nc, g)


def rope_table(rot_dim):
    axis_dim = rot_dim // 2
    inv = np.float32(10000.0) ** (-np.arange(0, axis_dim, 2, dtype=np.float32) / np.float32(axis_dim))
    t = np.arange(LAT)
    angle = np.stack([(t // GRID_W).astype(np.float32)[:, None] * inv,
                      (t % GRID_W).astype(np.float32)[:, None] * inv], 1)
    return np.stack([np.cos(angle), np.sin(angle)]).astype(np.float32)


def constants():
    gqa = rope_table(HEAD).reshape(2, 4, P, 2, 16).transpose(2, 0, 1, 3, 4)
    masks = np.zeros((2, P, NL, P), np.float32)
    key, query = np.arange(P)[:, None], np.arange(P)[None, :]
    for e, m in enumerate(HG_LEVELS):
        same = key // (2 * m) == query // (2 * m)
        masks[0, :, e] = same & (key // m % 2 == 0) & (query // m % 2 == 1)
        masks[1, :, e] = same & (key // m % 2 == 1) & (query // m % 2 == 0)
    masks[:, :, NL - 1] = np.eye(P)
    mla = rope_table(MLA_ROPE)
    cos, sin = (np.stack([mla[w], mla[w]], 2).reshape(LAT, MLA_ROPE).T for w in range(2))
    channel = np.arange(MLA_ROPE)
    sin = sin * np.where(channel // 8 % 2 == 0, -1.0, 1.0).astype(np.float32)[:, None]
    swap = np.zeros((MLA_ROPE, MLA_ROPE), np.float32)
    swap[channel ^ 8, channel] = 1.0
    part = np.arange(P)
    tile, group = np.arange(4)[:, None], np.arange(8)[None, :]
    bmask = (group[None] == 2 * tile[None] + (part // S5_P)[:, None, None]).astype(np.float32)
    cmask = (part[:, None] // S5_C == np.arange(8)[None, :]).astype(np.float32)
    t = np.arange(T)
    tau = np.stack([t, np.where(t < CTX, CTX - 1 - t, CTX + T - 1 - t)]).astype(np.float32)
    return {"k_rope_mla": np.ascontiguousarray(np.stack([cos, sin], 1)), "k_rope_swap": swap,
            "k_s5_bmask": bmask, "k_s5_cmask": cmask, "k_s5_tau": np.tile(tau[None], (P, 1, 1)),
            "k_hg_masks": masks.reshape(2, P, NL * P), "k_ident": np.eye(P, dtype=np.float32),
            "k_head_ones": (key // TOPK == query // TOPK).astype(np.float32),
            "k_iota": np.tile(np.arange(P, dtype=np.float32), (P, 1)), "k_rope_gqa": np.ascontiguousarray(gqa)}


def kernel(**inputs):
    import concourse.bacc as bacc
    from concourse.bass_utils import run_bass_kernel_spmd

    nc = bacc.Bacc("TRN2", target_bir_lowering=False, num_devices=1)
    arrays = {name: np.ascontiguousarray(v) for name, v in inputs.items()}
    arrays.update(constants())
    d = {name: nc.dram_tensor(name, v.shape, mybir.dt.from_np(v.dtype), kind="ExternalInput").ap()
         for name, v in arrays.items()}
    out = nc.dram_tensor("out", (1, LAT, D), F32, kind="ExternalOutput").ap()
    build(nc, d, out)
    result = run_bass_kernel_spmd(nc, [arrays], core_ids=[0])
    return result.results[0]["out"]
```
